# Optimizing a Trainium2 kernel written in Bass

```python
import math
import jax
import jax.numpy as jnp
from jax import lax
import numpy as np

D_MODEL = 1024
BATCH = 1
SEQ = 1024
DEPTH = 1
DEC_BATCH = 8
DEC_SEQ = 4
PAST_LEN = 4096
PAGE_SIZE = 128

EPS = 1e-6
N_MEM = 256
SSD_HEADS = 8
SSD_HEAD_DIM = 64
SSD_WIDTH = SSD_HEADS * SSD_HEAD_DIM
SSD_GROUPS = 2
SSD_STATE = 128
SSD_CONV = 4
SSD_CHUNK = 128
SSD_CONV_DIM = SSD_WIDTH + 2 * SSD_GROUPS * SSD_STATE
ATT_HEADS = 8
ATT_KV_HEADS = 2
ATT_GROUP = ATT_HEADS // ATT_KV_HEADS
ATT_HEAD_DIM = 64
ATT_WIDTH = ATT_HEADS * ATT_HEAD_DIM
ATT_KV_WIDTH = ATT_KV_HEADS * ATT_HEAD_DIM
WINDOW = 128
ATT_SCALE = ATT_HEAD_DIM ** -0.5
MIX_WIDTH = SSD_WIDTH + ATT_WIDTH
X_HEADS = 4
X_HEAD_DIM = D_MODEL // X_HEADS
X_SCALE = X_HEAD_DIM ** -0.5
D_FF = -(-8 * D_MODEL // (3 * 256)) * 256
IN_SPLITS = (SSD_WIDTH, SSD_CONV_DIM, SSD_HEADS, ATT_WIDTH, ATT_KV_WIDTH, ATT_KV_WIDTH)
IN_DIM = sum(IN_SPLITS)
SPLIT_AT = tuple(int(s) for s in np.cumsum(IN_SPLITS)[:-1])

kernel_name = 'hymba_ssd_swa_sink_memxattn_step'

def rmsnorm(x, g):
    xf = x.astype(jnp.float32)
    y = xf * lax.rsqrt(jnp.mean(xf * xf, axis=-1, keepdims=True) + EPS)
    return (y * g.astype(jnp.float32)).astype(x.dtype)

def gated_group_rmsnorm(y, z, g):
    b, l, _ = y.shape
    u = (y * jax.nn.silu(z.astype(jnp.float32))).reshape(b, l, SSD_GROUPS, SSD_WIDTH // SSD_GROUPS)
    u = u * lax.rsqrt(jnp.mean(u * u, axis=-1, keepdims=True) + EPS)
    return u.reshape(b, l, SSD_WIDTH) * g.astype(jnp.float32)

def causal_conv(u, prev, w, bias):
    l = u.shape[1]
    up = jnp.concatenate([prev.astype(u.dtype), u], axis=1)
    out = bias
    for j in range(SSD_CONV):
        out = out + up[:, j:j + l] * w[j]
    return jax.nn.silu(out), up[:, l:]

def segsum(a):
    t = a.shape[-1]
    cs = jnp.cumsum(a, axis=-1)
    diff = cs[..., :, None] - cs[..., None, :]
    lower = jnp.tril(jnp.ones((t, t), dtype=bool))
    return jnp.where(lower, diff, -jnp.inf)

def ssd_scan(x, dt, a, bm, cm, h0):
    bsz, l = x.shape[0], x.shape[1]
    t = SSD_CHUNK if l % SSD_CHUNK == 0 else l
    nc = l // t
    r = SSD_HEADS // SSD_GROUPS
    xdt = (x * dt[..., None]).reshape(bsz, nc, t, SSD_GROUPS, r, SSD_HEAD_DIM)
    adt = (dt * a).reshape(bsz, nc, t, SSD_GROUPS, r).transpose(0, 3, 4, 1, 2)
    bc = bm.reshape(bsz, nc, t, SSD_GROUPS, SSD_STATE)
    cc = cm.reshape(bsz, nc, t, SSD_GROUPS, SSD_STATE)
    a_cum = jnp.cumsum(adt, axis=-1)
    decay_in = jnp.exp(segsum(adt))
    cb = jnp.einsum('bctgn,bcsgn->bgcts', cc, bc)
    y_diag = jnp.einsum('bgcts,bgrcts,bcsgrp->bctgrp', cb, decay_in, xdt)
    decay_to_end = jnp.exp(a_cum[..., -1:] - a_cum)
    chunk_states = jnp.einsum('bctgn,bgrct,bctgrp->bcgrpn', bc, decay_to_end, xdt)
    h0g = h0.reshape(bsz, 1, SSD_GROUPS, r, SSD_HEAD_DIM, SSD_STATE)
    states = jnp.concatenate([h0g, chunk_states], axis=1)
    chunk_tot = jnp.pad(a_cum[..., -1], ((0, 0), (0, 0), (0, 0), (1, 0)))
    decay_chunk = jnp.exp(segsum(chunk_tot))
    states = jnp.einsum('bgrzc,bcgrpn->bzgrpn', decay_chunk, states)
    y_off = jnp.einsum('bctgn,bcgrpn,bgrct->bctgrp', cc, states[:, :-1], jnp.exp(a_cum))
    y = (y_diag + y_off).reshape(bsz, l, SSD_HEADS, SSD_HEAD_DIM)
    return y, states[:, -1].reshape(bsz, SSD_HEADS, SSD_HEAD_DIM, SSD_STATE)

def ssd_mixer(z, xbc_raw, dt_raw, conv_prev, h0, conv_w, conv_b, dt_bias, a_log, d_skip, g_norm):
    dtype = z.dtype
    xbc, conv_new = causal_conv(xbc_raw, conv_prev, conv_w, conv_b)
    b, l, _ = xbc.shape
    xbc = xbc.astype(jnp.float32)
    gn = SSD_GROUPS * SSD_STATE
    xs = xbc[..., :SSD_WIDTH].reshape(b, l, SSD_HEADS, SSD_HEAD_DIM)
    bm = xbc[..., SSD_WIDTH:SSD_WIDTH + gn].reshape(b, l, SSD_GROUPS, SSD_STATE)
    cm = xbc[..., SSD_WIDTH + gn:].reshape(b, l, SSD_GROUPS, SSD_STATE)
    dt = jax.nn.softplus(dt_raw.astype(jnp.float32) + dt_bias.astype(jnp.float32))
    a = -jnp.exp(a_log.astype(jnp.float32))
    y, h_new = ssd_scan(xs, dt, a, bm, cm, h0.astype(jnp.float32))
    y = y + xs * d_skip.astype(jnp.float32)[:, None]
    y = gated_group_rmsnorm(y.reshape(b, l, SSD_WIDTH), z, g_norm)
    return y.astype(dtype), conv_new, h_new.astype(h0.dtype)

def sink_softmax(s, mask, sinks):
    sink = sinks.astype(jnp.float32).reshape(ATT_KV_HEADS, ATT_GROUP, 1, 1)
    s = jnp.where(mask, s, -jnp.inf)
    m = jnp.maximum(jnp.max(s, axis=-1, keepdims=True), sink)
    e = jnp.exp(s - m)
    return e / (jnp.sum(e, axis=-1, keepdims=True) + jnp.exp(sink - m))

def swa_prompt(q, k, v, sinks):
    bsz, l = q.shape[0], q.shape[1]
    nb = l // WINDOW
    qb = q.reshape(bsz, nb, WINDOW, ATT_KV_HEADS, ATT_GROUP, ATT_HEAD_DIM)
    kb = k.reshape(bsz, nb, WINDOW, ATT_KV_HEADS, ATT_HEAD_DIM)
    vb = v.reshape(bsz, nb, WINDOW, ATT_KV_HEADS, ATT_HEAD_DIM)
    pad = ((0, 0), (1, 0), (0, 0), (0, 0), (0, 0))
    kk = jnp.concatenate([jnp.pad(kb, pad)[:, :-1], kb], axis=2)
    vv = jnp.concatenate([jnp.pad(vb, pad)[:, :-1], vb], axis=2)
    s = jnp.einsum('bnqhrd,bnkhd->bnhrqk', qb, kk, preferred_element_type=jnp.float32) * ATT_SCALE
    qi = jnp.arange(WINDOW)[:, None] + WINDOW
    kj = jnp.arange(2 * WINDOW)[None, :]
    band = (kj <= qi) & (qi - kj < WINDOW)
    has_prev = (jnp.arange(nb) > 0)[:, None, None]
    mask = band[None] & (has_prev | (kj >= WINDOW)[None])
    pr = sink_softmax(s, mask[:, None, None], sinks)
    o = jnp.einsum('bnhrqk,bnkhd->bnqhrd', pr.astype(vv.dtype), vv)
    return o.reshape(bsz, l, ATT_WIDTH)

def swa_sample(q, k, v, buf_k, buf_v, sinks):
    bsz, l = q.shape[0], q.shape[1]
    wb = buf_k.shape[1]
    kk = jnp.concatenate([buf_k.astype(k.dtype), k], axis=1)
    vv = jnp.concatenate([buf_v.astype(v.dtype), v], axis=1)
    s = jnp.einsum('bqhrd,bkhd->bhrqk', q, kk, preferred_element_type=jnp.float32) * ATT_SCALE
    qpos = PAST_LEN + jnp.arange(l)[:, None]
    kpos = PAST_LEN - wb + jnp.arange(wb + l)[None, :]
    mask = (kpos <= qpos) & (qpos - kpos < WINDOW)
    pr = sink_softmax(s, mask, sinks)
    o = jnp.einsum('bhrqk,bkhd->bqhrd', pr.astype(vv.dtype), vv)
    return o.reshape(bsz, l, ATT_WIDTH), kk[:, -wb:], vv[:, -wb:]

def memory_kv(mem, g, w_k, w_v):
    b, m, _ = mem.shape
    mn = rmsnorm(mem, g)
    return ((mn @ w_k).reshape(b, m, X_HEADS, X_HEAD_DIM),
            (mn @ w_v).reshape(b, m, X_HEADS, X_HEAD_DIM))

def cross_attend(h, mem_k, mem_v, w_q, w_o):
    bsz, l, _ = h.shape
    q = (h @ w_q).reshape(bsz, l, X_HEADS, X_HEAD_DIM)
    s = jnp.einsum('blhd,bmhd->bhlm', q, mem_k.astype(q.dtype), preferred_element_type=jnp.float32) * X_SCALE
    pr = jax.nn.softmax(s, axis=-1)
    o = jnp.einsum('bhlm,bmhd->blhd', pr.astype(q.dtype), mem_v.astype(q.dtype))
    return o.reshape(bsz, l, D_MODEL) @ w_o

def decoder_layer(x, conv_prev, h0, win_k, win_v, mem_k, mem_v, p):
    bsz, l, _ = x.shape
    h = rmsnorm(x, p['g_mix_pre'])
    proj = h @ p['w_in']
    z, xbc_raw, dt_raw, q, k, v = jnp.split(proj, SPLIT_AT, axis=-1)
    y_ssd, conv_new, h_new = ssd_mixer(z, xbc_raw, dt_raw, conv_prev, h0, p['conv_w'], p['conv_b'],
                                       p['dt_bias'], p['a_log'], p['d_skip'], p['g_ssd_norm'])
    q = q.reshape(bsz, l, ATT_KV_HEADS, ATT_GROUP, ATT_HEAD_DIM)
    k = k.reshape(bsz, l, ATT_KV_HEADS, ATT_HEAD_DIM)
    v = v.reshape(bsz, l, ATT_KV_HEADS, ATT_HEAD_DIM)
    if win_k is None:
        y_att = swa_prompt(q, k, v, p['sinks'])
        new_k, new_v = k[:, -WINDOW:], v[:, -WINDOW:]
    else:
        y_att, new_k, new_v = swa_sample(q, k, v, win_k, win_v, p['sinks'])
    mix = jnp.concatenate([y_ssd, y_att.astype(x.dtype)], axis=-1) @ p['w_out']
    x = x + rmsnorm(mix, p['g_mix_post'])
    c = cross_attend(rmsnorm(x, p['g_x_pre']), mem_k, mem_v, p['w_xq'], p['w_xo'])
    x = x + rmsnorm(c, p['g_x_post'])
    hf = rmsnorm(x, p['g_ffn_pre'])
    f = (jax.nn.silu(hf @ p['w_gate']) * (hf @ p['w_up'])) @ p['w_down']
    x = x + rmsnorm(f, p['g_ffn_post'])
    return x, conv_new, h_new, new_k, new_v

def setup_inputs(seed: int = 0) -> dict:
    key = jax.random.key(seed)
    ks = iter(jax.random.split(key, 40))
    f32 = jnp.float32

    def nrm(shape, scale):
        return jax.random.normal(next(ks), shape, f32) * scale

    def gain(width):
        return 1.0 + nrm((DEPTH, width), 0.02)

    win_buf = min(WINDOW, PAST_LEN)
    x_prompt = nrm((BATCH, SEQ, D_MODEL), 1.0)
    x_sample = nrm((DEC_BATCH, DEC_SEQ, D_MODEL), 1.0)
    state_ssm = nrm((DEPTH, DEC_BATCH, SSD_HEADS, SSD_HEAD_DIM, SSD_STATE), 0.5)
    state_conv = nrm((DEPTH, DEC_BATCH, SSD_CONV - 1, SSD_CONV_DIM), 1.0)
    cache_win_k = nrm((DEPTH, DEC_BATCH, win_buf, ATT_KV_HEADS, ATT_HEAD_DIM), 1.0)
    cache_win_v = nrm((DEPTH, DEC_BATCH, win_buf, ATT_KV_HEADS, ATT_HEAD_DIM), 1.0)
    cache_mem_k = nrm((DEPTH, DEC_BATCH, N_MEM, X_HEADS, X_HEAD_DIM), 1.0)
    cache_mem_v = nrm((DEPTH, DEC_BATCH, N_MEM, X_HEADS, X_HEAD_DIM), 1.0)
    mem_prompt = nrm((BATCH, N_MEM, D_MODEL), 1.0)
    u = jax.random.uniform(next(ks), (DEPTH, SSD_HEADS), f32)
    dt0 = jnp.exp(u * (math.log(0.1) - math.log(0.001)) + math.log(0.001))
    dt_bias = dt0 + jnp.log(-jnp.expm1(-dt0))
    a_log = jnp.log(jax.random.uniform(next(ks), (DEPTH, SSD_HEADS), f32, 1.0, 16.0))
    return {
        'x_prompt': x_prompt, 'x_sample': x_sample,
        'state_ssm': state_ssm, 'state_conv': state_conv,
        'cache_win_k': cache_win_k, 'cache_win_v': cache_win_v,
        'cache_mem_k': cache_mem_k, 'cache_mem_v': cache_mem_v,
        'mem_prompt': mem_prompt,
        'g_mix_pre': gain(D_MODEL),
        'w_in': nrm((DEPTH, D_MODEL, IN_DIM), D_MODEL ** -0.5),
        'conv_w': nrm((DEPTH, SSD_CONV, SSD_CONV_DIM), SSD_CONV ** -0.5),
        'conv_b': nrm((DEPTH, SSD_CONV_DIM), 0.02),
        'dt_bias': dt_bias,
        'a_log': a_log,
        'd_skip': 1.0 + nrm((DEPTH, SSD_HEADS), 0.1),
        'g_ssd_norm': gain(SSD_WIDTH),
        'sinks': nrm((DEPTH, ATT_HEADS), 0.5),
        'w_out': nrm((DEPTH, MIX_WIDTH, D_MODEL), MIX_WIDTH ** -0.5),
        'g_mix_post': gain(D_MODEL),
        'g_x_pre': gain(D_MODEL),
        'w_xq': nrm((DEPTH, D_MODEL, D_MODEL), D_MODEL ** -0.5),
        'g_mem': gain(D_MODEL),
        'w_xk': nrm((DEPTH, D_MODEL, D_MODEL), D_MODEL ** -0.5),
        'w_xv': nrm((DEPTH, D_MODEL, D_MODEL), D_MODEL ** -0.5),
        'w_xo': nrm((DEPTH, D_MODEL, D_MODEL), D_MODEL ** -0.5),
        'g_x_post': gain(D_MODEL),
        'g_ffn_pre': gain(D_MODEL),
        'w_gate': nrm((DEPTH, D_MODEL, D_FF), D_MODEL ** -0.5),
        'w_up': nrm((DEPTH, D_MODEL, D_FF), D_MODEL ** -0.5),
        'w_down': nrm((DEPTH, D_FF, D_MODEL), D_FF ** -0.5),
        'g_ffn_post': gain(D_MODEL),
    }

def reference(x_prompt, x_sample, state_ssm, state_conv, cache_win_k, cache_win_v, cache_mem_k, cache_mem_v,
              mem_prompt, g_mix_pre, w_in, conv_w, conv_b, dt_bias, a_log, d_skip, g_ssd_norm, sinks, w_out,
              g_mix_post, g_x_pre, w_xq, g_mem, w_xk, w_xv, w_xo, g_x_post, g_ffn_pre, w_gate, w_up, w_down,
              g_ffn_post):
    yp, ys = x_prompt, x_sample
    bp = x_prompt.shape[0]
    p_ssm, p_conv, p_wk, p_wv, p_mk, p_mv = [], [], [], [], [], []
    s_ssm, s_conv, s_wk, s_wv = [], [], [], []
    for i in range(DEPTH):
        p = {'g_mix_pre': g_mix_pre[i], 'w_in': w_in[i], 'conv_w': conv_w[i], 'conv_b': conv_b[i],
             'dt_bias': dt_bias[i], 'a_log': a_log[i], 'd_skip': d_skip[i], 'g_ssd_norm': g_ssd_norm[i],
             'sinks': sinks[i], 'w_out': w_out[i], 'g_mix_post': g_mix_post[i], 'g_x_pre': g_x_pre[i],
             'w_xq': w_xq[i], 'w_xo': w_xo[i], 'g_x_post': g_x_post[i], 'g_ffn_pre': g_ffn_pre[i],
             'w_gate': w_gate[i], 'w_up': w_up[i], 'w_down': w_down[i], 'g_ffn_post': g_ffn_post[i]}
        mk, mv = memory_kv(mem_prompt, g_mem[i], w_xk[i], w_xv[i])
        conv0 = jnp.zeros((bp, SSD_CONV - 1, SSD_CONV_DIM), yp.dtype)
        h00 = jnp.zeros((bp, SSD_HEADS, SSD_HEAD_DIM, SSD_STATE), yp.dtype)
        yp, pc, ph, pk, pv = decoder_layer(yp, conv0, h00, None, None, mk, mv, p)
        p_ssm.append(ph); p_conv.append(pc); p_wk.append(pk); p_wv.append(pv); p_mk.append(mk); p_mv.append(mv)
        ys, sc, sh, sk, sv = decoder_layer(ys, state_conv[i], state_ssm[i], cache_win_k[i], cache_win_v[i],
                                           cache_mem_k[i], cache_mem_v[i], p)
        s_ssm.append(sh); s_conv.append(sc); s_wk.append(sk); s_wv.append(sv)
    return (yp, ys,
            jnp.stack(p_ssm), jnp.stack(p_conv), jnp.stack(p_wk), jnp.stack(p_wv), jnp.stack(p_mk), jnp.stack(p_mv),
            jnp.stack(s_ssm), jnp.stack(s_conv), jnp.stack(s_wk), jnp.stack(s_wv))


_drawn_inputs = setup_inputs


def setup_inputs(seed=0):
    import zlib

    import numpy as np

    out = dict(_drawn_inputs(seed))
    spreads = {}
    factors = {'g_ssd_norm': 3.671,
     'sinks': 8.0,
     'g_mix_post': 3.567,
     'g_x_pre': 4.62,
     'g_mem': 2.807,
     'g_x_post': 12.613,
     'g_ffn_pre': 12.924,
     'g_ffn_post': 23.278}
    for name, (base, spread) in spreads.items():
        noise = np.random.default_rng([zlib.crc32(name.encode()), seed]).standard_normal(out[name].shape)
        drawn = base * np.exp(spread * noise) if base else spread * noise
        out[name] = jnp.asarray(drawn.astype(out[name].dtype))
    for name, factor in factors.items():
        out[name] = (out[name] * factor).astype(out[name].dtype)
    return out
```

```python
from contextlib import ExitStack

import concourse.bass as bass
from concourse import mybir

F32 = mybir.dt.float32
F32R = mybir.dt.float32r
ALU = mybir.AluOpType
ACT = mybir.ActivationFunctionType
ds = bass.ds

P = 128
D = 1024
KT = D // P
SEQ = 1024
NCH = SEQ // P
NB, TS = 8, 4
NS = NB * TS
NTOK = SEQ + NS
SSD_W = 512
XBC = 1024
HEADS = 8
HD = 64
NST = 128
C_Z, C_XBC, C_DT, C_Q, C_K, C_V = 0, 512, 1536, 1544, 2056, 2184
DFF = 2816
FT = DFF // P
NMEM = 256
EPS = 1e-6
NEG = -1.0e30
GW = (384, 384, 288)
G0 = (0, 384, 768)
CREDIT = 32

T_XBC, T_Z, T_Q, T_K, T_V = 0, 8, 12, 16, 17
NPT = 18
NPA = NPT + 1


def ready(n):
    return n + 1 + CREDIT


def group_rows(t):
    return P if t < NCH else NS


def bc(ap, shape):
    return ap.broadcast_to(shape)


def build_mixers(nc, spent, io, mixT, ident):
    ctx = ExitStack()
    with ctx:
        def sb(name, shape, dt=F32):
            return ctx.enter_context(nc.sbuf_tensor(name, shape, dt))

        def sem(name):
            spent.append(nc.alloc_semaphore(name=name))
            return spent[-1]

        raw = sb("a_raw", [P, 3, KT, P])
        w_hi = sb("a_whi", [P, 2, KT, P], F32R)
        w_lo = sb("a_wlo", [P, 2, KT, P], F32R)
        h_hi = sb("a_hhi", [P, KT, 384], F32R)
        h_lo = sb("a_hlo", [P, KT, 384], F32R)
        xt = sb("a_x", [P, D])
        hn = sb("a_hn", [P, D])
        gpre = sb("a_gpre", [P, D])
        ss = sb("a_ss", [P, 9])
        ms = sb("a_ms", [P, 9])
        rs = sb("a_rs", [P, 9])
        proj = sb("a_proj", [P, 2, NPT, 3 + 384])
        dtr = sb("a_dtr", [HEADS, 384])
        triu = sb("c_triu", [P, P])
        slow = sb("c_slow", [P, P])
        ones = sb("c_ones", [P, P])
        band = sb("c_band", [P, 2 * P])
        mask = sb("c_mask", [P, 2 * P])
        eps = sb("c_eps", [P, 2])
        mhalf = sb("c_mhalf", [P, 9])
        convw = sb("c_convw", [P, 4, 8])
        convb = sb("c_convb", [P, 8])
        graw = sb("c_graw", [44, P])
        dtb = sb("c_dtb", [P, HEADS])
        nega = sb("c_nega", [P, HEADS])
        dsk = sb("c_dsk", [P, HEADS])
        gssd = sb("c_gssd", [P, 4])
        nsink = sb("c_nsink", [P, 8])
        dx = sb("d_x", [P, 3 * HEADS])
        dna = sb("d_na", [P, 3 * HEADS])
        de = sb("d_e", [P, 3 * HEADS])
        du = sb("d_u", [P, 3 * HEADS])
        dl = sb("d_l", [P, 3 * HEADS])
        dv = sb("d_v", [P, 3 * HEADS])
        dw = sb("d_w", [P, 3 * HEADS])
        dt = sb("d_dt", [P, 3, HEADS])
        adt = sb("d_adt", [P, 3, HEADS])
        decay = sb("d_decay", [P, 3, 3 * HEADS])
        acc = sb("k_acc", [P, 8, P])
        tc_ = sb("k_tc", [P, 8, P])
        xc = sb("k_xc", [P, 8, P])
        tz = sb("k_tz", [P, 4, P])
        zs = sb("k_zs", [P, 4, P])
        xs = sb("k_xs", [P, SSD_W])
        xdt = sb("k_xdt", [P, SSD_W])
        xdd = sb("k_xdd", [P, SSD_W])
        yd = xs
        bt = sb("k_bt", [P, 2, P])
        rr = sb("k_rr", [P, HEADS, P])
        mm = sb("k_mm", [P, HEADS, P])
        cbm = sb("k_cbm", [P, 2, P])
        yt = sb("k_yt", [P, SSD_W])
        un = sb("k_un", [P, SSD_W])
        ssu = sb("k_ssu", [P, 2])
        rsu = sb("k_rsu", [P, 2])
        st = sb("k_state", [P, SSD_W])
        qs = sb("k_qs", [P, 4, P])
        kv = sb("k_kv", [P, 3, P])
        kw = kv[:, 0:2, :].rearrange("p m n -> p (m n)")
        vs = kv[:, 2, :]
        vw = sb("k_vw", [P, 2, P])
        sc = acc[:].rearrange("p (h m) n -> p h (m n)", m=2)
        pt = tc_
        mx = sb("k_mx", [P, 8])
        nb_ = sb("k_nb", [P, 8])
        sd = sb("k_sd", [P, 8])
        es = sb("k_es", [P, 8])
        rsum = sb("k_rsum", [P, 8])
        den = sb("k_den", [P, 8])
        ri = sb("k_ri", [P, 8])
        att = sb("k_att", [P, 4, 2, HD])

        bank = [ctx.enter_context(nc.psum_tensor(f"bank{n}", [P, 512], F32)) for n in range(8)]

        raw_full = [sem(f"raw_full{n}") for n in range(3)]
        x_full = [sem(f"x_full{n}") for n in range(2)]
        consts_in, consts_done, stored = sem("consts_in"), sem("consts_done"), sem("stored")
        names = """consts_T cols_done hi_done lo_done panel_done evac_done sumsq_done mean_done rstd_done hn_done hT_done hhi_done
        hlo_done halo_done dtT_done dt_steps dt_steps2 dt_exp dt_ln adt_done cum_done decay_done
        conv0_done conv_done tanhc_done xc_done tanhz_done zs_done qs_done k_shift kv_done scores_open
        t1_done xdt_done xs_done bt_done vshift_done vw_done yd_done xdd_done rr_done cb_done seg_done cbm_done exp_done mm_done
        ydiag_done yoff_done chst_done zT_done t_yoff t_ydiag t_y u_done usq_done um_done ur_done un_done
        sdec_done state_done sc_done msk_done nb_done sd_done es_done p_done den_done ri_done mask_done
        pT_done pTa_done pTv_done pv_done att_done unT_done mixs_done attT_done mixa_done""".split()
        S = {n: sem(n) for n in names}

        in_block = ExitStack()
        block = in_block.enter_context(nc.Block())

        owners = {
            "act": "cols_done hi_done evac_done sumsq_done hhi_done dt_exp dt_ln decay_done conv0_done tanhc_done tanhz_done "
                   "qs_done kv_done xs_done bt_done vw_done exp_done usq_done es_done p_done pTa_done mixs_done mixa_done",
            "dve": "k_shift vshift_done mask_done scores_open lo_done hn_done hlo_done dt_steps dt_steps2 adt_done conv_done xc_done zs_done xdt_done cbm_done mm_done t_yoff "
                   "t_ydiag t_y u_done un_done state_done msk_done nb_done sd_done den_done ri_done pTv_done att_done",
            "pool": "mean_done rstd_done halo_done yd_done xdd_done rr_done um_done ur_done sdec_done",
            "pe": "consts_T panel_done hT_done dtT_done cum_done t1_done cb_done seg_done ydiag_done yoff_done chst_done zT_done "
                  "sc_done pT_done pv_done unT_done attT_done",
        }

        def credit(eng, who):
            for n in owners[who].split():
                eng.sem_inc(S[n], CREDIT)

        x_rows = io["x"]
        row = lambda name: io[name].rearrange("(o n) -> o n", o=1)
        loads = [
            (graw[0:32, :], io["conv_w"].rearrange("t (k p) -> (t k) p", p=P)),
            (graw[32:40, :], io["conv_b"].rearrange("(k p) -> k p", p=P)),
            (graw[40:44, :], io["g_ssd_norm"].rearrange("(k p) -> k p", p=P)),
            (dtb[:], row("dt_bias").broadcast_to([P, HEADS])),
            (nega[:], row("a_log").broadcast_to([P, HEADS])),
            (dsk[:], row("d_skip").broadcast_to([P, HEADS])),
            (nsink[:], row("sinks").broadcast_to([P, HEADS])),
            (gpre[:], row("g_mix_pre").broadcast_to([P, D])),
        ]

        @block.sync
        def _(sp):
            for dst, src in loads:
                sp.dma_start(dst, src).then_inc(consts_in, 16)

            def load_x(t):
                sp.wait_ge(S["hn_done"], ready(t - 1))
                r = group_rows(t)
                sp.dma_start(xt[0:r, :], x_rows(t)).then_inc(x_full[t % 2], 16)

            def load_panel(n):
                k = n % NPA
                sp.wait_ge(S["lo_done"], ready(n - 3))
                if T_Q <= k < T_K:
                    j = k - T_Q
                    cols = [(C_Q + HD * j, HD), (C_Q + HD * (j + 4), HD)]
                else:
                    c = {0: C_XBC + P * k, 1: C_Z + P * (k - T_Z)}[k >= T_Z] if k < T_Q else \
                        C_K if k == T_K else C_V if k == T_V else C_DT
                    cols = [(c, HD), (c + HD, HD)]
                for m, (c, w) in enumerate(cols):
                    sp.dma_start(raw[:, n % 3, :, m * HD:m * HD + w],
                                 io["w_in"][:, c:c + w].rearrange("(k p) n -> p k n", p=P)).then_inc(raw_full[n % 3], 16)

            for g in range(3):
                for t in range(3 * g, 3 * g + 3):
                    load_x(t)
                for n in range(NPA * g, NPA * g + NPA):
                    load_panel(n)

        @block.gpsimd
        def _(pool):
            credit(pool, "pool")
            k = 0
            for m, v in ((triu, 1.0), (slow, 1.0), (ones, 1.0), (band, 0.0), (mask, NEG), (mhalf, -0.5), (eps, EPS), (ident, 0.0),
                         (st, 0.0), (kv, 0.0), (vw, 0.0)):
                pool.memset(m[:], v).then_inc(consts_done, 1)
                k += 1
            for gb in range(2):
                pool.memset(proj[:, gb, 0:8, 0:3], 0.0).then_inc(consts_done, 1)
                k += 1
            pool.wait_ge(consts_done, k)
            pool.affine_select(out=triu[:], in_=triu[:], compare_op=ALU.is_ge, fill=0.0, base=0,
                               pattern=[[1, P]], channel_multiplier=-1).then_inc(consts_done, 1)
            pool.affine_select(out=slow[:], in_=slow[:], compare_op=ALU.is_gt, fill=0.0, base=0,
                               pattern=[[-1, P]], channel_multiplier=1).then_inc(consts_done, 1)
            pool.affine_select(out=ident[:], in_=ident[:], compare_op=ALU.not_equal, fill=1.0, base=0,
                               pattern=[[-1, P]], channel_multiplier=1).then_inc(consts_done, 1)
            pool.affine_select(out=band[:, 0:P], in_=band[:, 0:P], compare_op=ALU.is_gt, fill=NEG, base=0,
                               pattern=[[1, P]], channel_multiplier=-1).then_inc(consts_done, 1)
            pool.affine_select(out=band[:, P:], in_=band[:, P:], compare_op=ALU.is_ge, fill=NEG, base=0,
                               pattern=[[-1, P]], channel_multiplier=1).then_inc(consts_done, 1)
            k += 5
            pool.wait_ge(consts_done, k)
            pool.tensor_copy(mask[:, P:], band[:, P:]).then_inc(consts_done, 1)
            k += 1

            def norm(t):
                r = group_rows(t)
                pool.wait_ge(S["sumsq_done"], ready(t))
                pool.tensor_scalar(ms[0:r, t:t + 1], ss[0:r, t:t + 1], 1.0 / D, EPS, ALU.mult, ALU.add)\
                    .then_inc(S["mean_done"], 1)
                pool.wait_ge(S["mean_done"], ready(t))
                pool.tensor_tensor(rs[0:r, t:t + 1], ms[0:r, t:t + 1], mhalf[0:r, 0:1], ALU.pow)\
                    .then_inc(S["rstd_done"], 1)

            def chunk(g, i):
                c = 3 * g + i
                b, off = g % 2, 3 + 128 * i
                pool.wait_ge(S["seg_done"], ready(c - 1))
                pool.wait_ge(S["adt_done"], ready(g))
                for q in range(2):
                    pool.tensor_tensor(rr[:, 4 * q:4 * q + 4, :], bc(triu[:].rearrange("p (o n) -> p o n", o=1), [P, 4, P]),
                                       bc(adt[:, ds(i, 1), 4 * q:4 * q + 4].rearrange("p o (h u) -> p (o h) u", u=1), [P, 4, P]),
                                       ALU.mult).then_inc(S["rr_done"], 1)
                pool.wait_ge(S["xdt_done"], ready(c))
                pool.wait_ge(S["decay_done"], ready(g))
                pool.wait_ge(S["chst_done"], ready(c - 1))
                pool.tensor_tensor(xdd[:].rearrange("p (h d) -> p h d", h=HEADS), xdt[:].rearrange("p (h d) -> p h d", h=HEADS),
                                   bc(decay[:, 1, ds(8 * i, 8)].rearrange("p (h u) -> p h u", u=1), [P, HEADS, HD]),
                                   ALU.mult).then_inc(S["xdd_done"], 1)
                pool.wait_ge(S["xs_done"], ready(c))
                pool.wait_ge(S["t_y"], ready(c - 1))
                pool.tensor_tensor(yd[:].rearrange("p (h d) -> p h d", h=HEADS), xs[:].rearrange("p (h d) -> p h d", h=HEADS),
                                   bc(dsk[:].rearrange("p (h u) -> p h u", u=1), [P, HEADS, HD]), ALU.mult)\
                    .then_inc(S["yd_done"], 1)
                pool.wait_ge(S["yoff_done"], ready(c))
                pool.wait_ge(S["state_done"], ready(c - 1))
                pool.tensor_tensor(st[:].rearrange("p (h d) -> p h d", h=HEADS), st[:].rearrange("p (h d) -> p h d", h=HEADS),
                                   bc(decay[:, 2, ds(8 * i, 8)].rearrange("p (h u) -> p h u", u=1), [P, HEADS, HD]),
                                   ALU.mult).then_inc(S["sdec_done"], 1)
                pool.wait_ge(S["usq_done"], ready(2 * c + 1))
                pool.tensor_tensor(rsu[:], ssu[:], eps[:, 0:2], ALU.add).then_inc(S["um_done"], 1)
                pool.wait_ge(S["um_done"], ready(c))
                pool.tensor_tensor(rsu[:], rsu[:], mhalf[:, 0:2], ALU.pow).then_inc(S["ur_done"], 1)

            for t in range(3):
                norm(t)
            for g in range(3):
                if g < 2:
                    for t in range(3 * g + 3, 3 * g + 6):
                        norm(t)
                if g < 2:
                    pool.wait_ge(S["evac_done"], ready(NPA * g + T_XBC + 7))
                    pool.wait_ge(consts_done, k)
                    pool.tensor_copy(proj[:, (g + 1) % 2, 0:8, 0:3], proj[:, g % 2, 0:8, 384:387]).then_inc(S["halo_done"], 1)
                pool.wait_ge(S["evac_done"], ready(NPA * g + NPA - 1))
                with pool.Fori(0, 3 if g < 2 else 2) as i:
                    chunk(g, i)

        @block.scalar
        def _(act):
            credit(act, "act")
            act.wait_ge(consts_in, 16 * len(loads))
            act.wait_ge(consts_done, 19)
            act.wait_ge(S["consts_T"], ready(0))
            act.activation(convw[:].rearrange("p t k -> p (t k)"), bank[7][:, 0:32], ACT.Copy, scale=0.5).then_inc(S["cols_done"], 1)
            act.activation(convb[:], bank[7][:, 32:40], ACT.Copy, scale=0.5).then_inc(S["cols_done"], 1)
            act.activation(gssd[:], bank[7][:, 40:44], ACT.Copy).then_inc(S["cols_done"], 1)
            act.activation(dna[:, 0:8], nega[:], ACT.Exp).then_inc(S["cols_done"], 1)
            act.activation(dna[:, 8:16], nsink[:], ACT.Copy, scale=-1.0).then_inc(S["cols_done"], 1)
            act.wait_ge(S["cols_done"], ready(4))
            act.activation(nega[:], dna[:, 0:8], ACT.Copy, scale=-1.0).then_inc(S["cols_done"], 1)
            act.activation(nsink[:].rearrange("p (j v) -> p j v", v=2), dna[:, 8:16].rearrange("p (v j) -> p j v", v=2), ACT.Copy).then_inc(S["cols_done"], 1)
            act.wait_ge(S["cols_done"], ready(6))

            def split_hi(n, s3, s2, w3):
                act.wait_ge(raw_full[s3], w3)
                act.wait_ge(S["panel_done"], ready(n - 2))
                act.activation(w_hi[:, s2], raw[:, s3], ACT.Copy).then_inc(S["hi_done"], 1)

            def evac(n, g, k, s2):
                w = GW[g]
                act.wait_ge(S["panel_done"], ready(n))
                act.activation(proj[:, g % 2, ds(k, 1), 3:3 + w], bank[s2][:, 0:w].rearrange("p (o n) -> p o n", o=1),
                               ACT.Copy).then_inc(S["evac_done"], 1)

            def norm(t):
                r = group_rows(t)
                act.wait_ge(x_full[t % 2], 16 * (t // 2 + 1))
                act.wait_ge(S["hT_done"], ready(2 * t - 1))
                act.activation(hn[0:r, :], xt[0:r, :], ACT.Square, accum_out=ss[0:r, t:t + 1])\
                    .then_inc(S["sumsq_done"], 1)

            def norm_evac(t):
                r, g = group_rows(t), t // 3
                c0 = 128 * (t % 3)
                for h in range(2):
                    act.wait_ge(S["hT_done"], ready(2 * t + h))
                    act.wait_ge(S["panel_done"], ready(NPA * g - 1))
                    act.activation(h_hi[:, 4 * h:4 * h + 4, c0:c0 + r],
                                   bank[2 + h][:, 0:4 * r].rearrange("p (k n) -> p k n", k=4), ACT.Copy)\
                        .then_inc(S["hhi_done"], 1)

            def dt_part(g, d, rows, cols):
                act.wait_ge(S["dt_steps"], ready(6 * d + 1))
                act.activation(de[0:rows, 0:cols], dna[0:rows, 0:cols], ACT.Exp).then_inc(S["dt_exp"], 1)
                act.wait_ge(S["dt_steps"], ready(6 * d + 2))
                act.activation(dl[0:rows, 0:cols], du[0:rows, 0:cols], ACT.Ln).then_inc(S["dt_ln"], 1)
                act.wait_ge(S["cum_done"], ready(d))
                act.activation(decay[0:rows, :, 0:cols], bank[4][0:rows, 32:32 + 3 * cols].rearrange("p (a n) -> p a n", a=3),
                               ACT.Exp).then_inc(S["decay_done"], 1)

            def conv0(g, i):
                c, b, off = 3 * g + i, g % 2, 128 * i
                for j in range(8):
                    if j == 0:
                        act.wait_ge(S["xc_done"], ready(c - 1))
                        act.wait_ge(S["pT_done"], ready(4 * c - 1))
                    act.activation(acc[:, j:j + 1, :], proj[:, b, j:j + 1, ds(off, P)], ACT.Identity,
                                   bias=convb[:, j:j + 1], scale=convw[:, 0, j:j + 1]).then_inc(S["conv0_done"], 1)
                act.wait_ge(S["zs_done"], ready(c - 1))
                act.activation(tz[:], proj[:, b, T_Z:T_Z + 4, ds(off + 3, P)], ACT.Tanh, scale=0.5).then_inc(S["tanhz_done"], 1)
                act.wait_ge(S["sc_done"], ready(2 * c - 1))
                act.activation(qs[:], proj[:, b, T_Q:T_Q + 4, ds(off + 3, P)], ACT.Copy, scale=0.125).then_inc(S["qs_done"], 1)
                act.wait_ge(S["k_shift"], ready(c))
                act.wait_ge(S["t1_done"], ready(c - 1))
                act.activation(kv[:, 1:3, :], proj[:, b, T_K:T_K + 2, ds(off + 3, P)], ACT.Copy).then_inc(S["kv_done"], 1)

            def conv_tanh(g, i):
                c = 3 * g + i
                act.wait_ge(S["conv_done"], ready(24 * c + 23))
                act.wait_ge(S["pv_done"], ready(2 * c - 1))
                act.activation(tc_[:], acc[:], ACT.Tanh).then_inc(S["tanhc_done"], 1)

            def elt1(g, i):
                c = 3 * g + i
                act.wait_ge(S["t1_done"], ready(c))
                act.wait_ge(S["t_y"], ready(c - 1))
                act.activation(xs[:], bank[2][:], ACT.Copy).then_inc(S["xs_done"], 1)
                act.wait_ge(S["chst_done"], ready(c - 1))
                act.activation(bt[:], bank[3][:, 0:256].rearrange("p (a n) -> p a n", a=2), ACT.Copy).then_inc(S["bt_done"], 1)
                act.wait_ge(S["vshift_done"], ready(c))
                act.activation(vw[:, 1, :], bank[3][:, 256:384], ACT.Copy).then_inc(S["vw_done"], 1)
                for q in range(2):
                    act.wait_ge(S["seg_done"], ready(c))
                    act.wait_ge(S["ydiag_done"], ready(c - 1))
                    act.activation(mm[:, 4 * q:4 * q + 4, :], bank[5 + q][:].rearrange("p (h n) -> p h n", h=4), ACT.Exp)\
                        .then_inc(S["exp_done"], 1)

            def softmax(g, i, r):
                c = 3 * g + i
                act.wait_ge(S["nb_done"], ready(2 * c + r))
                for h in range(4):
                    q = 4 * r + h
                    act.activation(sc[:, h, :], sc[:, h, :], ACT.Exp, bias=nb_[:, q:q + 1], accum_out=rsum[:, q:q + 1])\
                        .then_inc(S["p_done"], 1)
                act.wait_ge(S["sd_done"], ready(2 * c + r))
                act.activation(es[:, 4 * r:4 * r + 4], sd[:, 4 * r:4 * r + 4], ACT.Exp).then_inc(S["es_done"], 1)

            def elt2(g, i):
                c = 3 * g + i
                act.wait_ge(S["u_done"], ready(c))
                for q in range(2):
                    act.wait_ge(S["unT_done"], ready(c - 1))
                    act.activation(un[:, 256 * q:256 * q + 256], yt[:, 256 * q:256 * q + 256], ACT.Square,
                                   scale=1.0 / 16, accum_out=ssu[:, q:q + 1]).then_inc(S["usq_done"], 1)
                softmax(g, i, 0)

            def evac_pt(g, i, r):
                c = 3 * g + i
                act.wait_ge(S["pT_done"], ready(4 * c + 2 * r))
                act.wait_ge(S["pv_done"], ready(2 * c + r - 1))
                act.activation(pt[:, 0:4, :], bank[2][:].rearrange("p (h n) -> p h n", h=4), ACT.Copy).then_inc(S["pTa_done"], 1)

            def mix_ssd(g, i):
                c = 3 * g + i
                act.wait_ge(S["unT_done"], ready(c))
                for j in range(4):
                    act.activation(mixT(g)[:, j:j + 1, ds(128 * i, P)], bank[3][:, 128 * j:128 * j + 128].rearrange("p (o n) -> p o n", o=1),
                                   ACT.Copy, scale=gssd[:, j:j + 1]).then_inc(S["mixs_done"], 1)

            def mix_att(g, i):
                c = 3 * g + i
                act.wait_ge(S["attT_done"], ready(c))
                act.activation(mixT(g)[:, 4:8, ds(128 * i, P)], bank[3][:].rearrange("p (o n) -> p o n", o=4), ACT.Copy)\
                    .then_inc(S["mixa_done"], 1)

            def hi_wait(n):
                return 32 * (n // 3 + 1)

            for t in range(3):
                norm(t)
                norm_evac(t)
            split_hi(0, 0, 0, 32)
            for ph in range(4):
                gp, gb = ph, ph - 1
                n0 = NPA * gp
                if gb >= 0:
                    act.wait_ge(S["evac_done"], ready(NPA * gb + NPT))
                    act.wait_ge(S["halo_done"], ready(gb - 1))
                    act.wait_ge(S["t_yoff"], ready(3 * gb - 1))
                    act.wait_ge(S["sdec_done"], ready(3 * gb - 1))
                    dt_part(gb, gb, P, 24 if gb < 2 else 16)
                with act.Fori(0, 3 if gb < 2 else 2) as i:
                    for k in range(6):
                        if gp < 3:
                            n = n0 + 6 * i + k
                            m = n0 + k + 1
                            split_hi(n + 1, m % 3, m % 2, 32 * (m // 3 + 1) + 64 * i)
                            evac(n, gp, 6 * i + k, (n0 + k) % 2)
                        if gb >= 0:
                            if k == 0:
                                conv0(gb, i)
                            elif k == 1:
                                conv_tanh(gb, i)
                            elif k == 2:
                                elt1(gb, i)
                            elif k == 3:
                                elt2(gb, i)
                            elif k == 4:
                                evac_pt(gb, i, 0)
                                softmax(gb, i, 1)
                            elif k == 5:
                                mix_ssd(gb, i)
                                evac_pt(gb, i, 1)
                    if gb >= 0:
                        mix_att(gb, i)
                if gp < 3:
                    n = n0 + NPT
                    act.wait_ge(S["panel_done"], ready(n))
                    act.wait_ge(S["dtT_done"], ready(gp - 1))
                    act.activation(dtr[:, 0:GW[gp]], bank[n % 2][0:HEADS, 0:GW[gp]], ACT.Copy).then_inc(S["evac_done"], 1)
                    if gp < 2:
                        for t in range(3 * gp + 3, 3 * gp + 6):
                            norm(t)
                            norm_evac(t)
                        split_hi(n + 1, (n + 1) % 3, (n + 1) % 2, hi_wait(n + 1))

        @block.vector
        def _(dve):
            credit(dve, "dve")
            dve.wait_ge(consts_in, 16 * len(loads))
            dve.wait_ge(consts_done, 19)
            dve.wait_ge(S["cols_done"], ready(6))

            def split_lo(n, s3, s2):
                dve.wait_ge(S["hi_done"], ready(n))
                dve.tensor_tensor(w_lo[:, s2], raw[:, s3], w_hi[:, s2].bitcast(F32), ALU.subtract).then_inc(S["lo_done"], 1)

            def norm(t):
                r = group_rows(t)
                dve.wait_ge(S["rstd_done"], ready(t))
                dve.scalar_tensor_tensor(hn[0:r, :], xt[0:r, :], rs[0:r, t:t + 1], gpre[0:r, :], ALU.mult, ALU.mult)\
                    .then_inc(S["hn_done"], 1)

            def norm_evac(t):
                r = group_rows(t)
                c0 = 128 * (t % 3)
                for h in range(2):
                    dve.wait_ge(S["hhi_done"], ready(2 * t + h))
                    dve.tensor_tensor(h_lo[:, 4 * h:4 * h + 4, c0:c0 + r],
                                      bank[2 + h][:, 0:4 * r].rearrange("p (k n) -> p k n", k=4),
                                      h_hi[:, 4 * h:4 * h + 4, c0:c0 + r].bitcast(F32), ALU.subtract).then_inc(S["hlo_done"], 1)

            def dt_part(d, rows, chunks):
                cols = 8 * chunks
                v = lambda a: a[0:rows, 0:cols]
                v3 = lambda a: a[0:rows, 0:cols].rearrange("p (a n) -> p a n", n=8)
                dve.wait_ge(S["dtT_done"], ready(d))
                dve.tensor_tensor(v3(dx), v3(bank[4]), bc(dtb[0:rows, :].rearrange("p (o n) -> p o n", o=1), [rows, chunks, 8]),
                                  ALU.add).then_inc(S["dt_steps"], 1)
                dve.wait_ge(S["dt_steps"], ready(6 * d))
                dve.scalar_tensor_tensor(v(dna), v(dx), -1.0, v(dx), ALU.mult, ALU.min).then_inc(S["dt_steps"], 1)
                dve.wait_ge(S["dt_exp"], ready(d))
                dve.tensor_scalar(v(du), v(de), 1.0, None, ALU.add).then_inc(S["dt_steps"], 1)
                dve.wait_ge(S["dt_steps"], ready(6 * d + 2))
                dve.tensor_scalar(v(dv), v(du), -1.0, 1e-30, ALU.add, ALU.max).then_inc(S["dt_steps"], 1)
                dve.wait_ge(S["dt_steps"], ready(6 * d + 3))
                dve.reciprocal(v(dw), v(dv)).then_inc(S["dt_steps"], 1)
                dve.wait_ge(S["dt_steps"], ready(6 * d + 4))
                dve.tensor_tensor(v(dw), v(dw), v(de), ALU.mult).then_inc(S["dt_steps"], 1)
                dve.wait_ge(S["dt_steps"], ready(6 * d + 5))
                dve.wait_ge(S["dt_ln"], ready(d))
                dve.tensor_tensor(v(dl), v(dl), v(dw), ALU.mult).then_inc(S["dt_steps2"], 1)
                dve.scalar_tensor_tensor(v(dv), v(dv), 1e-30, v(de), ALU.is_equal, ALU.mult).then_inc(S["dt_steps2"], 1)
                dve.wait_ge(S["dt_steps2"], ready(4 * d + 1))
                dve.tensor_tensor(v(dl), v(dl), v(dv), ALU.add).then_inc(S["dt_steps2"], 1)
                dve.wait_ge(S["dt_steps2"], ready(4 * d + 2))
                dve.scalar_tensor_tensor(dt[0:rows, 0:chunks, :], v3(dx), 0.0, v3(dl), ALU.max, ALU.add)\
                    .then_inc(S["dt_steps2"], 1)
                dve.wait_ge(S["dt_steps2"], ready(4 * d + 3))
                dve.tensor_tensor(adt[0:rows, 0:chunks, :], dt[0:rows, 0:chunks, :],
                                  bc(nega[0:rows, :].rearrange("p (o n) -> p o n", o=1), [rows, chunks, 8]), ALU.mult)\
                    .then_inc(S["adt_done"], 1)

            def conv(g, i):
                c, b = 3 * g + i, g % 2
                dve.wait_ge(S["sc_done"], ready(2 * c - 1))
                dve.tensor_copy(kv[:, 0, :], kv[:, 1, :]).then_inc(S["k_shift"], 1)
                dve.wait_ge(S["pv_done"], ready(2 * c - 1))
                dve.tensor_copy(vw[:, 0, :], vw[:, 1, :]).then_inc(S["vshift_done"], 1)
                for tap in range(1, 4):
                    for j in range(8):
                        n = 24 * c + 8 * (tap - 1) + j
                        if tap == 1:
                            dve.wait_ge(S["conv0_done"], ready(8 * c + j))
                        else:
                            dve.wait_ge(S["conv_done"], ready(n - 8))
                        dve.scalar_tensor_tensor(acc[:, j:j + 1, :], proj[:, b, j:j + 1, ds(128 * i + tap, P)],
                                                 convw[:, tap, j:j + 1], acc[:, j:j + 1, :], ALU.mult, ALU.add)\
                            .then_inc(S["conv_done"], 1)
                dve.wait_ge(S["tanhz_done"], ready(c))
                dve.wait_ge(S["zT_done"], ready(c - 1))
                dve.scalar_tensor_tensor(zs[:], tz[:], 1.0, proj[:, b, T_Z:T_Z + 4, ds(128 * i + 3, P)], ALU.add, ALU.mult)\
                    .then_inc(S["zs_done"], 1)

            def silu_xc(g, i):
                c = 3 * g + i
                dve.wait_ge(S["tanhc_done"], ready(c))
                dve.wait_ge(S["yoff_done"], ready(c - 1))
                dve.scalar_tensor_tensor(xc[:], tc_[:], 1.0, acc[:], ALU.add, ALU.mult).then_inc(S["xc_done"], 1)

            h3 = lambda a: a.rearrange("p (h d) -> p h d", d=HD)

            def per_head(a):
                return bc(a.rearrange("p (h u) -> p h u", u=1), [P, HEADS, HD])

            def elt1(g, i):
                c = 3 * g + i
                dve.wait_ge(S["xs_done"], ready(c))
                dve.wait_ge(S["ydiag_done"], ready(c - 1))
                dve.wait_ge(S["xdd_done"], ready(c - 1))
                dve.tensor_tensor(h3(xdt[:]), h3(xs[:]), bc(dt[:, ds(i, 1), :].rearrange("p o (h u) -> p (o h) u", u=1),
                                                                 [P, HEADS, HD]), ALU.mult).then_inc(S["xdt_done"], 1)
                dve.wait_ge(S["cb_done"], ready(c))
                dve.wait_ge(S["mm_done"], ready(2 * c - 1))
                dve.tensor_tensor(cbm[:], bank[4][:, 0:256].rearrange("p (a n) -> p a n", a=2),
                                  bc(triu[:].rearrange("p (o n) -> p o n", o=1), [P, 2, P]), ALU.mult).then_inc(S["cbm_done"], 1)
                for q in range(2):
                    dve.wait_ge(S["exp_done"], ready(2 * c + q))
                    dve.wait_ge(S["cbm_done"], ready(c))
                    dve.tensor_tensor(mm[:, 4 * q:4 * q + 4, :], mm[:, 4 * q:4 * q + 4, :], bc(cbm[:, q:q + 1, :], [P, 4, P]),
                                      ALU.mult).then_inc(S["mm_done"], 1)

            def scores(g, i, r):
                c = 3 * g + i
                dve.wait_ge(S["sc_done"], ready(2 * c + r))
                dve.wait_ge(S["mask_done"], ready(c - 1))
                dve.wait_ge(S["pT_done"], ready(4 * c + 2 * r - 1))
                dve.sem_inc(S["scores_open"], 1)
                for h in range(4):
                    q = 4 * r + h
                    dve.tensor_tensor_reduce(sc[:, h, :], bank[5 + h % 2][:, 256 * (h // 2):256 * (h // 2) + 256], mask[:],
                                             1.0, -3.0e38, ALU.add, ALU.max, mx[:, q:q + 1]).then_inc(S["msk_done"], 1)
                dve.wait_ge(S["msk_done"], ready(8 * c + 4 * r + 3))
                dve.scalar_tensor_tensor(nb_[:, 4 * r:4 * r + 4], mx[:, 4 * r:4 * r + 4], -1.0, nsink[:, 4 * r:4 * r + 4],
                                         ALU.mult, ALU.min).then_inc(S["nb_done"], 1)
                dve.wait_ge(S["nb_done"], ready(2 * c + r))
                dve.tensor_tensor(sd[:, 4 * r:4 * r + 4], nb_[:, 4 * r:4 * r + 4], nsink[:, 4 * r:4 * r + 4], ALU.subtract)\
                    .then_inc(S["sd_done"], 1)
                if r == 1:
                    dve.tensor_copy(mask[:, 0:P], band[:, 0:P]).then_inc(S["mask_done"], 1)

            def denominators(g, i, r):
                c = 3 * g + i
                dve.wait_ge(S["es_done"], ready(2 * c + r))
                dve.wait_ge(S["p_done"], ready(8 * c + 4 * r + 3))
                dve.tensor_tensor(den[:, 4 * r:4 * r + 4], es[:, 4 * r:4 * r + 4], rsum[:, 4 * r:4 * r + 4], ALU.add)\
                    .then_inc(S["den_done"], 1)
                dve.wait_ge(S["den_done"], ready(2 * c + r))
                dve.wait_ge(S["att_done"], ready(2 * c + r - 2))
                dve.reciprocal(ri[:, 4 * r:4 * r + 4], den[:, 4 * r:4 * r + 4]).then_inc(S["ri_done"], 1)

            def elt2(g, i):
                c = 3 * g + i
                dve.wait_ge(S["yoff_done"], ready(c))
                dve.wait_ge(S["un_done"], ready(2 * c - 1))
                dve.tensor_tensor(h3(yt[:]), h3(bank[4][:]), per_head(decay[:, 0, ds(8 * i, 8)]), ALU.mult).then_inc(S["t_yoff"], 1)
                dve.wait_ge(S["ydiag_done"], ready(c))
                dve.wait_ge(S["t_yoff"], ready(c))
                dve.tensor_tensor(yt[:], bank[7][:], yt[:], ALU.add).then_inc(S["t_ydiag"], 1)
                dve.wait_ge(S["yd_done"], ready(c))
                dve.wait_ge(S["t_ydiag"], ready(c))
                dve.tensor_tensor(yt[:], yt[:], yd[:], ALU.add).then_inc(S["t_y"], 1)
                dve.wait_ge(S["chst_done"], ready(c))
                dve.wait_ge(S["sdec_done"], ready(c))
                dve.tensor_tensor(st[:], bank[2][:], st[:], ALU.add).then_inc(S["state_done"], 1)
                dve.wait_ge(S["zT_done"], ready(c))
                dve.wait_ge(S["t_y"], ready(c))
                dve.scalar_tensor_tensor(yt[:], bank[3][:], 0.5, yt[:], ALU.mult, ALU.mult).then_inc(S["u_done"], 1)
                scores(g, i, 0)

            def normed_u(g, i):
                c = 3 * g + i
                dve.wait_ge(S["ur_done"], ready(c))
                for q in range(2):
                    dve.tensor_scalar(un[:, 256 * q:256 * q + 256], yt[:, 256 * q:256 * q + 256], rsu[:, q:q + 1], None, ALU.mult)\
                        .then_inc(S["un_done"], 1)

            def evac_pt(g, i, r):
                c = 3 * g + i
                dve.wait_ge(S["pT_done"], ready(4 * c + 2 * r + 1))
                dve.wait_ge(S["pv_done"], ready(2 * c + r - 1))
                dve.tensor_copy(pt[:, 4:8, :], bank[4][:].rearrange("p (h n) -> p h n", h=4)).then_inc(S["pTv_done"], 1)

            def attended(g, i, r):
                c = 3 * g + i
                dve.wait_ge(S["pv_done"], ready(2 * c + r))
                dve.wait_ge(S["ri_done"], ready(2 * c + r))
                dve.wait_ge(S["attT_done"], ready(c - 1))
                dve.tensor_tensor(att[:, 2 * r:2 * r + 2].rearrange("p j v d -> p (j v) d"),
                                  bank[7][:, 256 * r:256 * r + 256].rearrange("p (h d) -> p h d", d=HD),
                                  bc(ri[:, 4 * r:4 * r + 4].rearrange("p (h u) -> p h u", u=1), [P, 4, HD]), ALU.mult)\
                    .then_inc(S["att_done"], 1)

            for t in range(3):
                norm(t)
                norm_evac(t)
            split_lo(0, 0, 0)
            for ph in range(4):
                gp, gb = ph, ph - 1
                n0 = NPA * gp
                if gb >= 0:
                    dve.wait_ge(S["rr_done"], ready(2 * (3 * gb - 1) + 1))
                    dt_part(gb, P, 3 if gb < 2 else 2)
                with dve.Fori(0, 3 if gb < 2 else 2) as i:
                    for k in range(6):
                        if gp < 3:
                            m = n0 + k + 1
                            split_lo(n0 + 6 * i + k + 1, m % 3, m % 2)
                        if gb >= 0:
                            if k == 0:
                                conv(gb, i)
                            elif k == 1:
                                silu_xc(gb, i)
                            elif k == 2:
                                elt1(gb, i)
                            elif k == 3:
                                elt2(gb, i)
                            elif k == 4:
                                denominators(gb, i, 0)
                                normed_u(gb, i)
                                evac_pt(gb, i, 0)
                                scores(gb, i, 1)
                            elif k == 5:
                                attended(gb, i, 0)
                                evac_pt(gb, i, 1)
                                denominators(gb, i, 1)
                    if gb >= 0:
                        attended(gb, i, 1)
                if gp < 2:
                    for t in range(3 * gp + 3, 3 * gp + 6):
                        norm(t)
                        norm_evac(t)
                    m = n0 + NPA
                    split_lo(m, m % 3, m % 2)

        @block.tensor
        def _(pe):
            credit(pe, "pe")
            pe.wait_ge(consts_done, 19)
            pe.wait_ge(consts_in, 16 * len(loads))
            pe.transpose(bank[7][:, 0:44], graw[:], ident[0:44, 0:44]).then_inc(S["consts_T"], 1)

            def panel(n, s2, w):
                pe.wait_ge(S["lo_done"], ready(n))
                pe.wait_ge(S["evac_done"], ready(n - 2))
                for k in range(KT):
                    for m, (a, b) in enumerate(((w_hi, h_hi), (w_hi, h_lo), (w_lo, h_hi))):
                        mm_ = pe.matmul(bank[s2][:, 0:w], a[:, s2, k, :], b[:, k, 0:w],
                                        start=(k == 0 and m == 0), stop=(k == KT - 1 and m == 2))
                mm_.then_inc(S["panel_done"], 1)

            def norm(t):
                r = group_rows(t)
                cl = 3 * (t // 3) - 4
                pe.wait_ge(S["hn_done"], ready(t))
                for h in range(2):
                    pe.wait_ge(S["hlo_done"], ready(2 * t + h - 2))
                    pe.wait_ge(*((S["pTa_done"], ready(2 * cl + 1)) if h == 0 else (S["mixa_done"], ready(cl))))
                    for k in range(4):
                        mm_ = pe.transpose(bank[2 + h][:, r * k:r * k + r], hn[0:r, P * (4 * h + k):P * (4 * h + k + 1)],
                                           ident[0:r, 0:r])
                    mm_.then_inc(S["hT_done"], 1)

            def dt_part(g):
                n = 3 if g < 2 else 2
                pe.wait_ge(S["evac_done"], ready(NPA * g + NPT))
                pe.wait_ge(S["pTv_done"], ready(2 * (3 * g - 1) + 1))
                for u in range(n):
                    mm_ = pe.transpose(bank[4][:, 8 * u:8 * u + 8], dtr[:, P * u:P * u + P], ident[0:8, 0:8])
                mm_.then_inc(S["dtT_done"], 1)
                pe.wait_ge(S["adt_done"], ready(g))
                for m, lhs in enumerate((triu, slow, ones)):
                    mm_ = pe.matmul(bank[4][:, 32 + 8 * n * m:32 + 8 * n * (m + 1)], lhs[:],
                                    adt[:, 0:n, :].rearrange("p a n -> p (a n)"), start=True, stop=True)
                mm_.then_inc(S["cum_done"], 1)

            def part1(g, i):
                c = 3 * g + i
                pe.wait_ge(S["xc_done"], ready(c))
                pe.wait_ge(S["pTa_done"], ready(2 * c - 1))
                for j in range(4):
                    pe.transpose(bank[2][:, P * j:P * j + P], xc[:, j, :], ident[:])
                pe.wait_ge(S["mixa_done"], ready(c - 1))
                for j in range(2):
                    pe.transpose(bank[3][:, P * j:P * j + P], xc[:, 4 + j, :], ident[:])
                pe.wait_ge(S["kv_done"], ready(c))
                pe.transpose(bank[3][:, 256:384], vs, ident[:]).then_inc(S["t1_done"], 1)
                pe.wait_ge(S["pTv_done"], ready(2 * c - 1))
                pe.wait_ge(S["decay_done"], ready(g))
                for q in range(2):
                    mm_ = pe.matmul(bank[4][:, P * q:P * q + P], xc[:, 4 + q, :], xc[:, 6 + q, :], start=True, stop=True)
                mm_.then_inc(S["cb_done"], 1)
                pe.wait_ge(S["msk_done"], ready(8 * c - 1))
                pe.wait_ge(S["rr_done"], ready(2 * c + 1))
                for q in range(2):
                    mm_ = pe.matmul(bank[5 + q][:], slow[:], rr[:, 4 * q:4 * q + 4, :].rearrange("p h n -> p (h n)"),
                                    start=True, stop=True)
                mm_.then_inc(S["seg_done"], 1)

            def scores(c, r):
                for h in range(4):
                    j, v = 2 * r + h // 2, h % 2
                    mm_ = pe.matmul(bank[5 + h % 2][:, 256 * (h // 2):256 * (h // 2) + 256], qs[HD * v:HD * v + HD, j, :],
                                    kw[HD * v:HD * v + HD, :], start=True, stop=True)
                mm_.then_inc(S["sc_done"], 1)

            def part2(g, i):
                c = 3 * g + i
                pe.wait_ge(S["cbm_done"], ready(c))
                pe.wait_ge(S["state_done"], ready(c - 1))
                for q in range(2):
                    mm_ = pe.matmul(bank[4][:, 256 * q:256 * q + 256], xc[:, 6 + q, :], st[:, 256 * q:256 * q + 256],
                                    start=True, stop=True)
                mm_.then_inc(S["yoff_done"], 1)
                pe.wait_ge(S["zs_done"], ready(c))
                pe.wait_ge(S["bt_done"], ready(c))
                pe.wait_ge(S["vw_done"], ready(c))
                for j in range(4):
                    mm_ = pe.transpose(bank[3][:, P * j:P * j + P], zs[:, j, :], ident[:])
                mm_.then_inc(S["zT_done"], 1)
                pe.wait_ge(S["exp_done"], ready(2 * c + 1))
                pe.wait_ge(S["qs_done"], ready(c))
                scores(c, 0)
                pe.wait_ge(S["mm_done"], ready(2 * c + 1))
                pe.wait_ge(S["att_done"], ready(2 * c - 1))
                for h in range(HEADS):
                    mm_ = pe.matmul(bank[7][:, HD * h:HD * h + HD], mm[:, h, :], xdt[:, HD * h:HD * h + HD],
                                    start=True, stop=True)
                mm_.then_inc(S["ydiag_done"], 1)
                pe.wait_ge(S["xdd_done"], ready(c))
                pe.wait_ge(S["xs_done"], ready(c))
                for q in range(2):
                    mm_ = pe.matmul(bank[2][:, 256 * q:256 * q + 256], bt[:, q, :], xdd[:, 256 * q:256 * q + 256],
                                    start=True, stop=True)
                mm_.then_inc(S["chst_done"], 1)

            def p_transposed(c, r):
                pe.wait_ge(S["p_done"], ready(8 * c + 4 * r + 3))
                pe.wait_ge(*((S["pTa_done"], ready(2 * c)) if r else (S["state_done"], ready(c))))
                for q in range(4):
                    mm_ = pe.transpose(bank[2][:, P * q:P * q + P], sc[:, q // 2, P * (q % 2):P * (q % 2) + P], ident[:])
                mm_.then_inc(S["pT_done"], 1)
                pe.wait_ge(*((S["pTv_done"], ready(2 * c)) if r else (S["t_yoff"], ready(c))))
                for q in range(4):
                    mm_ = pe.transpose(bank[4][:, P * q:P * q + P], sc[:, 2 + q // 2, P * (q % 2):P * (q % 2) + P], ident[:])
                mm_.then_inc(S["pT_done"], 1)

            def part3(g, i):
                c = 3 * g + i
                pe.wait_ge(S["msk_done"], ready(8 * c + 3))
                scores(c, 1)
                p_transposed(c, 0)

            def values(c, r):
                pe.wait_ge(S["pTa_done"], ready(2 * c + r))
                pe.wait_ge(S["pTv_done"], ready(2 * c + r))
                pe.wait_ge(*((S["att_done"], ready(2 * c)) if r else (S["t_ydiag"], ready(c))))
                for h in range(4):
                    for m in range(2):
                        mm_ = pe.matmul(bank[7][:, 256 * r + HD * h:256 * r + HD * h + HD], pt[:, 2 * h + m, :],
                                        vw[:, m, HD * (h % 2):HD * (h % 2) + HD], start=(m == 0), stop=(m == 1))
                mm_.then_inc(S["pv_done"], 1)

            def part4(g, i):
                c = 3 * g + i
                values(c, 0)
                pe.wait_ge(S["un_done"], ready(2 * c + 1))
                pe.wait_ge(S["u_done"], ready(c))
                for j in range(4):
                    mm_ = pe.transpose(bank[3][:, P * j:P * j + P], un[:, P * j:P * j + P], ident[:])
                mm_.then_inc(S["unT_done"], 1)
                p_transposed(c, 1)

            def part6(g, i):
                c = 3 * g + i
                pe.wait_ge(S["att_done"], ready(2 * c + 1))
                pe.wait_ge(S["mixs_done"], ready(4 * c + 3))
                for j in range(4):
                    mm_ = pe.transpose(bank[3][:, P * j:P * j + P], att[:, j].rearrange("p v d -> p (v d)"), ident[:])
                mm_.then_inc(S["attT_done"], 1)

            for t in range(3):
                norm(t)
            for ph in range(4):
                gp, gb = ph, ph - 1
                n0 = NPA * gp
                if gb >= 0:
                    dt_part(gb)
                if gp < 3:
                    pe.wait_ge(S["hlo_done"], ready(6 * gp + 5))
                with pe.Fori(0, 3 if gb < 2 else 2) as i:
                    for k in range(6):
                        if gp < 3:
                            panel(n0 + 6 * i + k, (n0 + k) % 2, GW[gp])
                        if gb >= 0:
                            if k == 1:
                                part1(gb, i)
                            elif k == 2:
                                part2(gb, i)
                            elif k == 3:
                                part3(gb, i)
                            elif k == 4:
                                part4(gb, i)
                            elif k == 5:
                                values(3 * gb + i, 1)
                    if gb >= 0:
                        part6(gb, i)
                if gp < 3:
                    panel(n0 + NPT, (n0 + NPT) % 2, GW[gp])
                if gp < 2:
                    for t in range(3 * gp + 3, 3 * gp + 6):
                        norm(t)

        in_block.close()
        mix_samples(nc, spent, io, mixT, ident, dict(
            proj=proj, bank=bank, rr=rr, mm=mm, cbm=cbm, xs=xs, xdt=xdt, xdd=xdd, yt=yt, un=un, bt=bt, vw=vw, kv=kv, raw=raw,
            acc=acc, tc=tc_, hn=hn, x=xt, zs=zs, tz=tz, st=st, gpre=gpre, gssd=gssd, dtb=dtb, nega=nega, dsk=dsk, nsink=nsink,
            eps=eps, mhalf=mhalf, convw=convw, convb=convb, triu=triu, slow=slow, dtr=dtr))

def mix_samples(nc, spent, io, mixT, ident, B):
    R = NS
    proj, bank, w = B["proj"], B["bank"], B
    off = 3 + 256
    spare = proj[:, 1].rearrange("p k n -> p (k n)")
    used = [0]

    def take(rows, *shape):
        n = 1
        for v in shape:
            n *= v
        a = spare[0:rows, used[0]:used[0] + n]
        used[0] += n
        assert used[0] <= NPT * 387
        names = "abcd"[:len(shape)]
        if len(shape) > 1:
            a = a.rearrange("p (" + " ".join(names) + ") -> p " + " ".join(names), **dict(zip(names, shape)))
        return a

    xr = take(P, 8, NB, 7)
    acc, tmp, th, xc = (take(P, 8, R) for _ in range(4))
    tz, zs = take(P, 4, R), take(P, 4, R)
    blk = take(R, NB, TS)
    trius, slows = take(R, R), take(R, R)
    mrow = take(P, NB, R)
    selt, selj = take(4, P), take(4, P)
    selc = take(P, 4)
    m4 = take(4, 160)
    msk = take(P, 2, 160)
    zero = take(P, R)
    dx, dna, de, du, dl, dv, dw, dt, adt = (take(R, HEADS) for _ in range(9))
    decay = take(R, 3, HEADS)
    adtx = take(R, 4, P)
    decs = take(P, 4, NB)
    ssu, rsu = take(R, 2), take(R, 2)
    qd = take(P, NB, 2, 4, TS)
    sinkr, tmp24, mx, nb_, sd, es, rsum, den, ri = take(P, 2), take(P, 2, 4), take(P, 4), take(P, 4), take(P, 4), take(P, 4), \
        take(P, 4), take(P, 4), take(P, 4)
    pn = take(R, 2, 2, P)
    ctm = take(P, 2, 2, R)
    btm = take(R, 2, 2, P)
    rr = w["rr"][0:R].rearrange("p h n -> p (h n)")[:, 0:256].rearrange("p (h n) -> p h n", n=R)
    mm = w["mm"][0:R].rearrange("p h n -> p (h n)")[:, 0:256].rearrange("p (h n) -> p h n", n=R)
    cbm = w["cbm"][0:R, :, 0:R]
    xs, xdt, xdd, yt, un = (w[n][0:R, :] for n in ("xs", "xdt", "xdd", "yt", "un"))
    bt = w["bt"][0:R]
    kvt = take(R, 2, P)
    ck, cv, ckT = (w["raw"][:, n] for n in range(3))
    sn = w["acc"][:].rearrange("p (s j) n -> p s j n", s=2)
    so = w["tc"][:].rearrange("p (s j) n -> p s j n", s=2)
    stT = w["hn"][:].rearrange("p (s n) -> p s n", s=2)
    halo = w["x"]
    sc = w["zs"][:].rearrange("p a n -> p (a n)")[:, 0:320].rearrange("p (v n) -> p v n", v=2)
    pt = w["tz"][:, 0:2, :]
    att = w["bt"][:].rearrange("p a n -> p (a n)")[:, 0:P]

    order = dict(
        pe="halo dtT sels cum tot tr cb seg zT ydiag zero unT ckTa ckTb sc0 pT0 pnT0 pv0 aT0 sc1 pT1 pnT1 pv1 aT1 "
           "rawa rawb pca pcb psT pkT".split(),
        act="halo1 halo2 tanh tz qd0 qd1 mask exp ln decay decs xs bt kv expseg sq0 sq1 mixs ckTa e00 e01 es0 pt0 pn0 mixa0 "
            "e10 e11 es1 pt1 pn1 mixa1 rawa rawb pca pcb".split(),
        dve="m0 a0 m1 a1 m2 a2 m3 a3 xc zs selc snk0 snk1 dx dna du dv dw dw2 dl dve dl2 dt adt adtx xdt cbm mm0 mm1 "
            "yoff ydiag ysk u un0 un1 ckTb s00 s01 nb0 sd0 den0 ri0 att0 s10 s11 nb1 sd1 den1 ri1 att1 psT pkT".split(),
        pool="z1 z2 z3 z4 z5 z6 z8 a1 a2 a3 a4 a5 a6 a7 a8 c1 c2 k0 k1 k2 k3 rr xdd yd um ur".split(),
    )
    sems = {e: nc.alloc_semaphore(name=f"sample_{e}_steps") for e in order}
    spent += sems.values()
    at = {e: {n: k + 1 for k, n in enumerate(names)} for e, names in order.items()}
    count = dict.fromkeys(order, 0)

    def step(e, name):
        count[e] += 1
        assert order[e][count[e] - 1] == name, (e, name, order[e][count[e] - 1])
        return sems[e], 1

    def after(e, name):
        return sems[e], at[e][name]

    def sem(name):
        spent.append(nc.alloc_semaphore(name=name))
        return spent[-1]

    loaded, stored, state_full, state_stored = sem("s_loaded"), sem("s_stored"), [sem("s_sf0"), sem("s_sf1")], [sem("s_ss0"), sem("s_ss1")]
    ctm_done, btm_done, stT_pe, stT_done, yoff_done, ch_done, sdec_done, snew_done = (
        sem(n) for n in "s_ctm s_btm s_stTpe s_stT s_yoff s_ch s_sdec s_snew".split())

    in_block = ExitStack()
    block = in_block.enter_context(nc.Block())

    @block.sync
    def _(sp):
        for s in range(2):
            sp.sem_inc(state_stored[s], 16)
        sp.dma_start(halo[0:24, :], io["state_conv"][0].rearrange("b j c -> (b j) c")).then_inc(loaded, 16)
        sp.dma_start(ck, io["cache_win_k"][0].rearrange("b k v d -> k b (v d)")).then_inc(loaded, 16)
        sp.dma_start(cv, io["cache_win_v"][0].rearrange("b k v d -> k b (v d)")).then_inc(loaded, 16)
        for name, cache in (("s_win_k", "cache_win_k"), ("s_win_v", "cache_win_v")):
            sp.dma_start(io[name][0, :, 0:P - TS], io[cache][0, :, TS:P]).then_inc(stored, 16)

        def load_state(b):
            sp.wait_ge(sdec_done, ready(b - 2))
            sp.wait_ge(stT_pe, ready(b - 2))
            sp.dma_start(sn[:, b % 2], io["state_ssm"][0, b].rearrange("(j u) p n -> (u p) j n", u=2)).then_inc(state_full[b % 2], 16)

        load_state(0)
        for b in range(NB):
            if b + 1 < NB:
                load_state(b + 1)
            sp.wait_ge(snew_done, ready(b))
            sp.dma_start(io["s_ssm"][0, b].rearrange("(j u) p n -> (u p) j n", u=2), so[:, b % 2]).then_inc(state_stored[b % 2], 16)
        for name, m in (("s_win_k", 1), ("s_win_v", 0)):
            for b in range(NB):
                sp.dma_start(io[name][0, b, P - TS:P].rearrange("t v d -> t (v d)"), kvt[TS * b:TS * b + TS, m, :])\
                    .then_inc(stored, 16)
        sp.wait_ge(*after("act", "pcb"))
        for b in range(NB):
            sp.dma_start(io["s_conv"][0, b], halo[TS * b + 1:TS * b + TS, :]).then_inc(stored, 16)
        sp.dma_start(io["p_conv"][0, 0], w["gpre"][0:3, :]).then_inc(stored, 16)
        sp.wait_ge(*after("dve", "pkT"))
        sp.dma_start(io["p_ssm"][0, 0].rearrange("(j u) p n -> (u p) j n", u=2), w["xdt"][:].rearrange("p (j n) -> p j n", j=4))\
            .then_inc(stored, 16)
        sp.dma_start(io["p_win_k"][0, 0].rearrange("t v d -> t (v d)"), w["xs"][:, 0:P]).then_inc(stored, 16)
        sp.dma_start(io["p_win_v"][0, 0].rearrange("t v d -> t (v d)"), w["vw"][:, 1, :]).then_inc(stored, 16)
        sp.wait_ge(stored, 16 * (2 + 3 * NB + 4))
        for s in range(2):
            sp.wait_ge(state_stored[s], 16 * (NB // 2 + 1))

    def credit(eng, *which):
        for s in which:
            eng.sem_inc(s, CREDIT)

    @block.gpsimd
    def _(pool):
        for n, (a, v) in enumerate(((blk, 1.0), (mrow, 1.0), (selt, 1.0), (selj, 1.0), (m4, 0.0), (zero, 0.0))):
            pool.memset(a, v).then_inc(*step("pool", f"z{n + 1}"))
        pool.memset(rsu, 0.0).then_inc(*step("pool", "z8"))
        pool.wait_ge(*after("pool", "z8"))

        def select(n, a, op, fill, base, pattern, cm):
            pool.affine_select(out=a, in_=a, compare_op=op, fill=fill, base=base, pattern=pattern, channel_multiplier=cm)\
                .then_inc(*step("pool", f"a{n}"))

        sel4 = lambda a: a.rearrange("p (a b) -> p a b", b=4)
        select(1, blk, ALU.is_ge, 0.0, 0, [[-4, NB], [0, TS]], 1)
        pool.wait_ge(*after("pool", "a1"))
        select(2, blk, ALU.is_ge, 0.0, 3, [[4, NB], [0, TS]], -1)
        select(3, mrow, ALU.is_ge, 0.0, 0, [[-4, NB], [1, R]], 0)
        pool.wait_ge(*after("pool", "a3"))
        select(4, mrow, ALU.is_ge, 0.0, 3, [[4, NB], [-1, R]], 0)
        select(5, sel4(selt), ALU.is_equal, 0.0, 0, [[0, R], [1, 4]], -1)
        select(6, selj.rearrange("p (a b c) -> p a b c", b=4, c=4), ALU.is_equal, 0.0, 0, [[0, 8], [1, 4], [0, 4]], -1)
        select(7, m4[:, 0:P], ALU.is_ge, NEG, -1, [[1, P]], -1)
        select(8, sel4(m4[:, P:160]), ALU.is_ge, NEG, 0, [[0, NB], [-1, TS]], 1)
        pool.wait_ge(*after("pool", "a8"))
        b2 = blk.rearrange("p a b -> p (a b)")
        pool.tensor_tensor(trius, w["triu"][0:R, 0:R], b2, ALU.mult).then_inc(*step("pool", "c1"))
        pool.tensor_tensor(slows, w["slow"][0:R, 0:R], b2, ALU.mult).then_inc(*step("pool", "c2"))
        pool.wait_ge(*after("act", "mask"))
        for hf in range(2):
            a = sel4(msk[:, hf, P:160])
            pool.affine_select(out=a, in_=a, compare_op=ALU.is_ge, fill=NEG, base=P * hf, pattern=[[-R, NB], [0, TS]],
                               channel_multiplier=1).then_inc(*step("pool", f"k{2 * hf}"))
            pool.wait_ge(*after("pool", f"k{2 * hf}"))
            pool.affine_select(out=a, in_=a, compare_op=ALU.is_ge, fill=NEG, base=R - 1 - P * hf, pattern=[[R, NB], [0, TS]],
                               channel_multiplier=-1).then_inc(*step("pool", f"k{2 * hf + 1}"))
        pool.wait_ge(*after("dve", "adt"))
        pool.tensor_tensor(rr, bc(trius.rearrange("p (o n) -> p o n", o=1), [R, HEADS, R]),
                           bc(adt.rearrange("p (h u) -> p h u", u=1), [R, HEADS, R]), ALU.mult).then_inc(*step("pool", "rr"))
        pool.wait_ge(*after("dve", "xdt"))
        pool.wait_ge(*after("act", "decay"))
        h3 = lambda a: a.rearrange("p (h d) -> p h d", d=HD)
        ph = lambda a: bc(a.rearrange("p (h u) -> p h u", u=1), [R, HEADS, HD])
        pool.tensor_tensor(h3(xdd), h3(xdt), ph(decay[:, 1, :]), ALU.mult).then_inc(*step("pool", "xdd"))
        pool.tensor_tensor(h3(xs), h3(xs), ph(w["dsk"][0:R, :]), ALU.mult).then_inc(*step("pool", "yd"))
        pool.wait_ge(*after("act", "sq1"))
        pool.tensor_tensor(rsu, ssu, w["eps"][0:R, 0:2], ALU.add).then_inc(*step("pool", "um"))
        pool.wait_ge(*after("pool", "um"))
        pool.tensor_tensor(rsu, rsu, w["mhalf"][0:R, 0:2], ALU.pow).then_inc(*step("pool", "ur"))

    @block.scalar
    def _(act):
        credit(act, stT_done)
        act.wait_ge(*after("pe", "halo"))
        for k in range(8):
            ins = act.activation(xr[:, k, :, 0:3], bank[7][:, 24 * k:24 * k + 24].rearrange("p (b j) -> p b j", j=3), ACT.Copy)
        ins.then_inc(*step("act", "halo1"))
        for k in range(8):
            ins = act.activation(xr[:, k, :, 3:7], proj[:, 0, k, off:off + R].rearrange("p (b t) -> p b t", t=TS), ACT.Copy)
        ins.then_inc(*step("act", "halo2"))
        act.wait_ge(*after("dve", "a3"))
        act.activation(th, acc, ACT.Tanh).then_inc(*step("act", "tanh"))
        act.activation(tz, proj[:, 0, T_Z:T_Z + 4, off:off + R], ACT.Tanh, scale=0.5).then_inc(*step("act", "tz"))
        for m in range(2):
            act.activation(qd[:, :, m].rearrange("p b j t -> p j b t"),
                           proj[:, 0, T_Q:T_Q + 4, off:off + R].rearrange("p j (b t) -> p j b t", t=TS), ACT.Copy, scale=0.125)\
                .then_inc(*step("act", f"qd{m}"))
        act.wait_ge(*after("pe", "sels"))
        act.activation(msk, bc(bank[5][:, 0:160].rearrange("p (o n) -> p o n", o=1), [P, 2, 160]), ACT.Copy).then_inc(*step("act", "mask"))
        act.wait_ge(*after("dve", "dna"))
        act.activation(de, dna, ACT.Exp).then_inc(*step("act", "exp"))
        act.wait_ge(*after("dve", "du"))
        act.activation(dl, du, ACT.Ln).then_inc(*step("act", "ln"))
        act.wait_ge(*after("pe", "tot"))
        act.activation(decay, bank[4][0:R, 32:56].rearrange("p (a n) -> p a n", a=3), ACT.Exp).then_inc(*step("act", "decay"))
        act.activation(decs, bank[4][:, 64:96].rearrange("p (j b) -> p j b", j=4), ACT.Exp).then_inc(*step("act", "decs"))
        act.wait_ge(*after("pe", "tr"))
        act.activation(xs, bank[2][0:R, :], ACT.Copy).then_inc(*step("act", "xs"))
        act.activation(bt, bank[3][0:R, 0:256].rearrange("p (a n) -> p a n", a=2), ACT.Copy).then_inc(*step("act", "bt"))
        act.activation(kvt, bank[3][0:R, 256:512].rearrange("p (a n) -> p a n", a=2), ACT.Copy).then_inc(*step("act", "kv"))
        act.wait_ge(*after("pe", "seg"))
        act.activation(mm, bank[5][0:R, 256:512].rearrange("p (h n) -> p h n", n=R), ACT.Exp).then_inc(*step("act", "expseg"))
        with act.Fori(0, NB // 2) as i:
            for s in range(2):
                act.wait_ge(stT_pe, ready(2 * i + s))
                act.wait_ge(yoff_done, ready(2 * i + s - 2))
                act.activation(stT[:, s], bank[2][:], ACT.Copy).then_inc(stT_done, 1)
        act.wait_ge(*after("dve", "u"))
        for q in range(2):
            act.activation(un[:, 256 * q:256 * q + 256], yt[:, 256 * q:256 * q + 256], ACT.Square, scale=1.0 / 16,
                           accum_out=ssu[:, q:q + 1]).then_inc(*step("act", f"sq{q}"))
        act.wait_ge(*after("pe", "unT"))
        for j in range(4):
            ins = act.activation(mixT(2)[:, j, 256:256 + R], bank[3][:, R * j:R * j + R], ACT.Copy, scale=w["gssd"][:, j:j + 1])
        ins.then_inc(*step("act", "mixs"))
        act.wait_ge(*after("pe", "ckTa"))
        act.activation(ckT[:, 0:4, :], bank[2][:].rearrange("p (b n) -> p b n", b=4), ACT.Copy).then_inc(*step("act", "ckTa"))
        for hf in range(2):
            act.wait_ge(*after("dve", f"sd{hf}"))
            for v in range(2):
                c = 2 * hf + v
                act.activation(sc[:, v, :], sc[:, v, :], ACT.Exp, bias=nb_[:, c:c + 1], accum_out=rsum[:, c:c + 1])\
                    .then_inc(*step("act", f"e{hf}{v}"))
            act.activation(es[:, 2 * hf:2 * hf + 2], sd[:, 2 * hf:2 * hf + 2], ACT.Exp).then_inc(*step("act", f"es{hf}"))
            act.wait_ge(*after("pe", f"pnT{hf}"))
            act.activation(pt, bank[2][:, 0:256].rearrange("p (v n) -> p v n", v=2), ACT.Copy).then_inc(*step("act", f"pt{hf}"))
            act.activation(pn[:, hf], bank[3][0:R, 0:256].rearrange("p (v n) -> p v n", v=2), ACT.Copy).then_inc(*step("act", f"pn{hf}"))
            act.wait_ge(*after("pe", f"aT{hf}"))
            act.activation(mixT(2)[:, 4:8, 256 + 16 * hf:272 + 16 * hf].rearrange("p j (b t) -> p j b t", t=TS),
                           bank[4][:, 0:P].rearrange("p (b u j t) -> p u j b t", b=4, u=2, j=4)[:, 0], ACT.Copy)\
                .then_inc(*step("act", f"mixa{hf}"))
        for n, (bk, dst) in enumerate(((2, halo[0:R, 0:512]), (3, halo[0:R, 512:1024]), (4, w["gpre"][0:3, 0:512]), (7, w["gpre"][0:3, 512:1024]))):
            name = ("rawa", "rawb", "pca", "pcb")[n]
            act.wait_ge(*after("pe", name))
            act.activation(dst, bank[bk][0:R if n < 2 else 3, :], ACT.Copy).then_inc(*step("act", name))

    @block.vector
    def _(dve):
        credit(dve, ctm_done, btm_done, sdec_done, snew_done)

        def link(name, ins):
            ins.then_inc(*step("dve", name))
            dve.wait_ge(*after("dve", name))

        v4 = lambda a: a.rearrange("p k (b t) -> p k b t", t=TS)
        dve.wait_ge(*after("act", "halo2"))
        for t in range(4):
            wt = bc(w["convw"][:, t, :].rearrange("p (k u v) -> p k u v", u=1, v=1), [P, 8, NB, TS])
            link(f"m{t}", dve.tensor_tensor(v4(tmp if t else acc), xr[:, :, :, t:t + TS], wt, ALU.mult))
            other = tmp if t else bc(w["convb"][:].rearrange("p (k u) -> p k u", u=1), [P, 8, R])
            link(f"a{t}", dve.tensor_tensor(acc, acc, other, ALU.add))
        dve.wait_ge(*after("act", "tz"))
        dve.scalar_tensor_tensor(xc, th, 1.0, acc, ALU.add, ALU.mult).then_inc(*step("dve", "xc"))
        dve.scalar_tensor_tensor(zs, tz, 1.0, proj[:, 0, T_Z:T_Z + 4, off:off + R], ALU.add, ALU.mult).then_inc(*step("dve", "zs"))
        dve.wait_ge(*after("pe", "sels"))
        link("selc", dve.tensor_copy(selc, bank[6][:, 0:4]))
        link("snk0", dve.tensor_tensor(tmp24, w["nsink"][:].rearrange("p (j v) -> p v j", v=2),
                                       bc(selc.rearrange("p (o j) -> p o j", o=1), [P, 2, 4]), ALU.mult))
        link("snk1", dve.tensor_reduce(sinkr, tmp24, mybir.AxisListType.X, ALU.add))
        link("dx", dve.tensor_tensor(dx, bank[4][0:R, 0:8], w["dtb"][0:R, :], ALU.add))
        link("dna", dve.scalar_tensor_tensor(dna, dx, -1.0, dx, ALU.mult, ALU.min))
        dve.wait_ge(*after("act", "exp"))
        link("du", dve.tensor_scalar(du, de, 1.0, None, ALU.add))
        link("dv", dve.tensor_scalar(dv, du, -1.0, 1e-30, ALU.add, ALU.max))
        link("dw", dve.reciprocal(dw, dv))
        link("dw2", dve.tensor_tensor(dw, dw, de, ALU.mult))
        dve.wait_ge(*after("act", "ln"))
        link("dl", dve.tensor_tensor(dl, dl, dw, ALU.mult))
        link("dve", dve.scalar_tensor_tensor(dv, dv, 1e-30, de, ALU.is_equal, ALU.mult))
        link("dl2", dve.tensor_tensor(dl, dl, dv, ALU.add))
        link("dt", dve.scalar_tensor_tensor(dt, dx, 0.0, dl, ALU.max, ALU.add))
        link("adt", dve.tensor_tensor(adt, dt, w["nega"][0:R, :], ALU.mult))
        h3 = lambda a: a.rearrange("p (h d) -> p h d", d=HD)
        ph = lambda a: bc(a.rearrange("p (h u) -> p h u", u=1), [R, HEADS, HD])
        dve.tensor_copy(adtx.rearrange("p j (u d) -> p (j u) d", u=2), ph(adt)).then_inc(*step("dve", "adtx"))
        dve.wait_ge(*after("act", "xs"))
        dve.tensor_tensor(h3(xdt), h3(xs), ph(dt), ALU.mult).then_inc(*step("dve", "xdt"))
        dve.wait_ge(*after("pe", "cb"))
        link("cbm", dve.tensor_tensor(cbm, bank[6][0:R, 64:128].rearrange("p (q n) -> p q n", q=2),
                                      bc(trius.rearrange("p (o n) -> p o n", o=1), [R, 2, R]), ALU.mult))
        dve.wait_ge(*after("act", "expseg"))
        for q in range(2):
            dve.tensor_tensor(mm[:, 4 * q:4 * q + 4, :], mm[:, 4 * q:4 * q + 4, :], bc(cbm[:, q:q + 1, :], [R, 4, R]), ALU.mult)\
                .then_inc(*step("dve", f"mm{q}"))
        dve.wait_ge(*after("act", "decs"))
        with dve.Fori(0, NB // 2) as i:
            for s in range(2):
                n = 2 * i + s
                dve.wait_ge(yoff_done, ready(n - 2))
                dve.tensor_tensor(ctm[:, s], xc[:, 6:8, :], bc(mrow[:, ds(n, 1), :], [P, 2, R]), ALU.mult).then_inc(ctm_done, 1)
                dve.wait_ge(ch_done, ready(n - 2))
                dve.tensor_tensor(btm[:, s], bt, bc(blk[:, ds(n, 1), 0:1], [R, 2, P]), ALU.mult).then_inc(btm_done, 1)
                dve.wait_ge(state_full[s], 16 * i + 16)
                dve.wait_ge(state_stored[s], 16 * i + 16)
                dve.tensor_tensor(so[:, s], sn[:, s], bc(decs[:, :, ds(n, 1)], [P, 4, P]), ALU.mult).then_inc(sdec_done, 1)
                dve.wait_ge(ch_done, ready(n))
                dve.wait_ge(sdec_done, ready(n))
                dve.tensor_tensor(so[:, s], so[:, s], bank[5][:].rearrange("p (j n) -> p j n", j=4), ALU.add).then_inc(snew_done, 1)
        dve.wait_ge(yoff_done, ready(NB - 1))
        link("yoff", dve.tensor_tensor(h3(yt), h3(bank[6][0:R, :]), ph(decay[:, 0, :]), ALU.mult))
        dve.wait_ge(*after("pe", "ydiag"))
        link("ydiag", dve.tensor_tensor(yt, yt, bank[7][0:R, :], ALU.add))
        dve.wait_ge(*after("pool", "yd"))
        link("ysk", dve.tensor_tensor(yt, yt, xs, ALU.add))
        dve.wait_ge(*after("pe", "zT"))
        link("u", dve.scalar_tensor_tensor(yt, bank[3][0:R, :], 0.5, yt, ALU.mult, ALU.mult))
        dve.wait_ge(*after("pool", "ur"))
        for q in range(2):
            dve.tensor_scalar(un[:, 256 * q:256 * q + 256], yt[:, 256 * q:256 * q + 256], rsu[:, q:q + 1], None, ALU.mult)\
                .then_inc(*step("dve", f"un{q}"))
        dve.wait_ge(*after("pe", "ckTb"))
        dve.tensor_copy(ckT[:, 4:8, :], bank[7][:].rearrange("p (b n) -> p b n", b=4)).then_inc(*step("dve", "ckTb"))
        dve.wait_ge(*after("pool", "k3"))
        for hf in range(2):
            h2 = slice(2 * hf, 2 * hf + 2)
            dve.wait_ge(*after("pe", f"sc{hf}"))
            for v in range(2):
                c = 2 * hf + v
                dve.tensor_tensor_reduce(sc[:, v, :], bank[5 + v][:, 0:160], msk[:, hf, :], 1.0, -3.0e38, ALU.add, ALU.max,
                                         mx[:, c:c + 1]).then_inc(*step("dve", f"s{hf}{v}"))
            dve.wait_ge(*after("dve", f"s{hf}1"))
            link(f"nb{hf}", dve.scalar_tensor_tensor(nb_[:, h2], mx[:, h2], -1.0, sinkr, ALU.mult, ALU.min))
            dve.tensor_tensor(sd[:, h2], nb_[:, h2], sinkr, ALU.subtract).then_inc(*step("dve", f"sd{hf}"))
            dve.wait_ge(*after("act", f"es{hf}"))
            link(f"den{hf}", dve.tensor_tensor(den[:, h2], es[:, h2], rsum[:, h2], ALU.add))
            link(f"ri{hf}", dve.reciprocal(ri[:, h2], den[:, h2]))
            dve.wait_ge(*after("pe", f"pv{hf}"))
            dve.tensor_tensor(att.rearrange("p (v d) -> p v d", v=2), bank[7][:, 0:P].rearrange("p (v d) -> p v d", v=2),
                              bc(ri[:, h2].rearrange("p (v u) -> p v u", u=1), [P, 2, HD]), ALU.mult).then_inc(*step("dve", f"att{hf}"))
        dve.wait_ge(*after("pe", "psT"))
        dve.tensor_copy(w["xdt"][:], bank[5][:]).then_inc(*step("dve", "psT"))
        dve.wait_ge(*after("pe", "pkT"))
        dve.tensor_copy(w["xs"][:, 0:P], bank[6][:, 0:P]).then_inc(*step("dve", "pkT"))

    @block.tensor
    def _(pe):
        credit(pe, stT_pe, yoff_done, ch_done)
        pe.wait_ge(loaded, 48)
        for k in range(8):
            ins = pe.transpose(bank[7][:, 24 * k:24 * k + 24], halo[0:24, P * k:P * k + P], ident[0:24, 0:24])
        ins.then_inc(*step("pe", "halo"))
        pe.transpose(bank[4][0:R, 0:8], w["dtr"][:, 256:256 + R], ident[0:8, 0:8]).then_inc(*step("pe", "dtT"))
        pe.wait_ge(*after("pool", "a8"))
        pe.transpose(bank[6][:, 0:4], selj, ident[0:4, 0:4])
        pe.matmul(bank[5][:, 0:160], selt, m4, start=True, stop=True).then_inc(*step("pe", "sels"))
        pe.wait_ge(*after("dve", "adt"))
        pe.wait_ge(*after("pool", "c2"))
        for m, lhs in enumerate((trius, slows, blk.rearrange("p a b -> p (a b)"))):
            ins = pe.matmul(bank[4][0:R, 32 + 8 * m:40 + 8 * m], lhs, adt, start=True, stop=True)
        ins.then_inc(*step("pe", "cum"))
        pe.wait_ge(*after("dve", "adtx"))
        for j in range(4):
            ins = pe.matmul(bank[4][:, 64 + 8 * j:72 + 8 * j], adtx[:, j, :], blk[:, :, 0], start=True, stop=True)
        ins.then_inc(*step("pe", "tot"))
        for j in range(4):
            pe.transpose(bank[2][0:R, P * j:P * j + P], xc[:, j, :], ident[:])
        for j in range(2):
            pe.transpose(bank[3][0:R, P * j:P * j + P], xc[:, 4 + j, :], ident[:])
        for m, k in enumerate((T_V, T_K)):
            ins = pe.transpose(bank[3][0:R, 256 + P * m:384 + P * m], proj[:, 0, k, off:off + R], ident[:])
        ins.then_inc(*step("pe", "tr"))
        for q in range(2):
            ins = pe.matmul(bank[6][0:R, 64 + R * q:96 + R * q], xc[:, 4 + q, :], xc[:, 6 + q, :], start=True, stop=True)
        ins.then_inc(*step("pe", "cb"))
        pe.wait_ge(*after("act", "mask"))
        pe.wait_ge(*after("pool", "rr"))
        pe.matmul(bank[5][0:R, 256:512], w["slow"][0:R, 0:R], rr.rearrange("p h n -> p (h n)"), start=True, stop=True)\
            .then_inc(*step("pe", "seg"))
        pe.wait_ge(*after("act", "kv"))
        for j in range(4):
            ins = pe.transpose(bank[3][0:R, P * j:P * j + P], zs[:, j, :], ident[:])
        ins.then_inc(*step("pe", "zT"))
        pe.wait_ge(*after("dve", "mm1"))
        for h in range(HEADS):
            ins = pe.matmul(bank[7][0:R, HD * h:HD * h + HD], mm[:, h, :], xdt[:, HD * h:HD * h + HD], start=True, stop=True)
        ins.then_inc(*step("pe", "ydiag"))
        pe.matmul(bank[6][0:R, :], zero, bc(w["triu"][:].rearrange("p (o n) -> p o n", o=1), [P, 4, P]), start=True, stop=False,
                  skip_group_check=True).then_inc(*step("pe", "zero"))
        pe.wait_ge(*after("pool", "xdd"))
        with pe.Fori(0, NB // 2) as i:
            for s in range(2):
                n = 2 * i + s
                pe.wait_ge(state_full[s], 16 * i + 16)
                pe.wait_ge(stT_done, ready(n - 1))
                for j in range(4):
                    ins = pe.transpose(bank[2][:, P * j:P * j + P], sn[:, s, j, :], ident[:])
                ins.then_inc(stT_pe, 1)
                pe.wait_ge(btm_done, ready(n))
                pe.wait_ge(snew_done, ready(n - 1))
                for j in range(4):
                    ins = pe.matmul(bank[5][:, P * j:P * j + P], xdd[:, P * j:P * j + P], btm[:, s, j // 2, :], start=True, stop=True)
                ins.then_inc(ch_done, 1)
                pe.wait_ge(stT_done, ready(n))
                pe.wait_ge(ctm_done, ready(n))
                for q in range(2):
                    ins = pe.matmul(bank[6][0:R, 256 * q:256 * q + 256], ctm[:, s, q, :], stT[:, s, 256 * q:256 * q + 256],
                                    start=False, stop=True, skip_group_check=True)
                ins.then_inc(yoff_done, 1)
        pe.wait_ge(*after("dve", "un1"))
        for j in range(4):
            ins = pe.transpose(bank[3][:, R * j:R * j + R], un[:, P * j:P * j + P], ident[0:R, 0:R])
        ins.then_inc(*step("pe", "unT"))
        for b in range(4):
            ins = pe.transpose(bank[2][:, P * b:P * b + P], ck[:, b, :], ident[:])
        ins.then_inc(*step("pe", "ckTa"))
        for b in range(4):
            ins = pe.transpose(bank[7][:, P * b:P * b + P], ck[:, 4 + b, :], ident[:])
        ins.then_inc(*step("pe", "ckTb"))
        pe.wait_ge(snew_done, ready(NB - 1))
        for hf in range(2):
            if hf == 0:
                pe.wait_ge(*after("act", "ckTa"))
                pe.wait_ge(*after("dve", "ckTb"))
            else:
                pe.wait_ge(*after("dve", "s01"))
            for v in range(2):
                rows = slice(HD * v, HD * v + HD)
                pe.matmul(bank[5 + v][:, P:160], qd[rows, 4 * hf:4 * hf + 4].rearrange("p b u j t -> p (b u j t)"),
                          proj[rows, 0, T_K, off:off + R], start=True, stop=True)
                for b in range(4):
                    ins = pe.matmul(bank[5 + v][R * b:R * b + R, 0:P], qd[rows, 4 * hf + b].rearrange("p u j t -> p (u j t)"),
                                    ckT[rows, 4 * hf + b, :], start=True, stop=True)
            ins.then_inc(*step("pe", f"sc{hf}"))
            pe.wait_ge(*after("act", f"e{hf}1"))
            if hf == 0:
                pe.wait_ge(*after("act", "mixs"))
            for v in range(2):
                ins = pe.transpose(bank[2][:, P * v:P * v + P], sc[:, v, 0:P], ident[:])
            ins.then_inc(*step("pe", f"pT{hf}"))
            for v in range(2):
                ins = pe.transpose(bank[3][0:R, P * v:P * v + P], sc[:, v, P:160], ident[:])
            ins.then_inc(*step("pe", f"pnT{hf}"))
            pe.wait_ge(*after("act", f"pn{hf}"))
            for v in range(2):
                cols = slice(HD * v, HD * v + HD)
                pe.matmul(bank[7][:, cols], pn[:, hf, v, :], kvt[:, 0, cols], start=True, stop=False, skip_group_check=True)
                for b in range(4):
                    ins = pe.matmul(bank[7][R * b:R * b + R, cols], pt[:, v, R * b:R * b + R], cv[:, 4 * hf + b, cols],
                                    start=False, stop=True, skip_group_check=True)
            ins.then_inc(*step("pe", f"pv{hf}"))
            pe.wait_ge(*after("dve", f"att{hf}"))
            pe.transpose(bank[4][:, 0:P], att, ident[:]).then_inc(*step("pe", f"aT{hf}"))
            pe.wait_ge(*after("act", f"mixa{hf}"))
        for m, name in enumerate(("rawa", "rawb")):
            for k in range(4):
                ins = pe.transpose(bank[2 + m][0:R, P * k:P * k + P], proj[:, 0, 4 * m + k, off:off + R], ident[:])
            ins.then_inc(*step("pe", name))
        for m, name in enumerate(("pca", "pcb")):
            for k in range(4):
                ins = pe.transpose(bank[(4, 7)[m]][0:3, P * k:P * k + P], proj[:, 0, 4 * m + k, off - 3:off], ident[:])
            ins.then_inc(*step("pe", name))
        for j in range(4):
            ins = pe.transpose(bank[5][:, P * j:P * j + P], w["st"][:, P * j:P * j + P], ident[:])
        ins.then_inc(*step("pe", "psT"))
        pe.transpose(bank[6][:, 0:P], w["kv"][:, 1, :], ident[:]).then_inc(*step("pe", "pkT"))

    in_block.close()


STAGES = ("mk", "mv", "w0", "w1", "w2", "x0", "x1", "o0", "o1", "x2", "o2")
FIRST = {s: KT * n for n, s in enumerate(STAGES)}
OPERANDS = ("m", "w0", "w1", "w2", "x0", "x1", "o0", "o1", "x2", "o2")
PARTS = {"m": 2, "w": 4, "x": 3, "o": 3}
OT_SLOT = dict(mv=1, w0=0, w1=1, w2=0, x0=1, x1=0, o0=1, o1=0, x2=1, o2=0)
NPANELS = KT * len(STAGES)


def part_of(operand, i):
    n = 0
    for o in OPERANDS:
        if o == operand:
            return n + i
        n += PARTS[o[0]]


def walk(do):
    panels, post, prea, preb, split = do["panels"], do["post"], do["prea"], do["preb"], do["split"]
    sc, soft, pt, pv, mem = do["sc"], do["soft"], do["pt"], do["pv"], do["mem"]
    prea("m", 0)
    preb("m", 0)
    prea("m", 1)
    preb("m", 1)
    do["start"]()
    panels("mk", 0, 8)
    split(0)
    panels("mv", 0, 2)
    mem("k", 0)
    mem("k", 1)
    panels("mv", 2, 6)
    panels("w0", 0, 2)
    split(1)
    mem("v", 0)
    mem("v", 1)
    panels("w0", 2, 6)
    panels("w1", 0, 1)
    split(2)
    post("w", 0)
    panels("w1", 1, 2)
    post("w", 1)
    panels("w1", 3, 2)
    post("w", 2)
    panels("w1", 5, 3)
    panels("w2", 0, 1)
    post("w", 3)
    prea("x", 0)
    panels("w2", 1, 1)
    preb("x", 0)
    post("w", 4)
    prea("x", 1)
    panels("w2", 2, 2)
    preb("x", 1)
    post("w", 5)
    prea("x", 2)
    panels("w2", 4, 2)
    preb("x", 2)
    panels("w2", 6, 2)
    panels("x0", 0, 1)
    post("w", 6)
    prea("x", 3)
    panels("x0", 1, 1)
    preb("x", 3)
    post("w", 7)
    prea("x", 4)
    panels("x0", 2, 2)
    preb("x", 4)
    post("w", 8)
    prea("x", 5)
    panels("x0", 4, 2)
    preb("x", 5)
    panels("x0", 6, 2)
    for g, stage in ((0, "x1"), (1, "o0")):
        t = 3 * g
        panels(stage, 0, 1)
        sc(t)
        soft(t)
        panels(stage, 1, 1)
        pt(t)
        sc(t + 1)
        soft(t + 1)
        panels(stage, 2, 1)
        pv(t)
        panels(stage, 3, 1)
        pt(t + 1)
        sc(t + 2)
        soft(t + 2)
        panels(stage, 4, 1)
        pv(t + 1)
        panels(stage, 5, 1)
        pt(t + 2)
        panels(stage, 6, 1)
        pv(t + 2)
        panels(stage, 7, 1)
    panels("o1", 0, 1)
    post("o", 0)
    prea("x", 6)
    panels("o1", 1, 1)
    preb("x", 6)
    post("o", 1)
    prea("x", 7)
    panels("o1", 2, 2)
    preb("x", 7)
    post("o", 2)
    prea("x", 8)
    panels("o1", 4, 2)
    preb("x", 8)
    panels("o1", 6, 2)
    panels("x2", 0, 1)
    for i in range(3):
        post("o", 3 + i)
        panels("x2", 1 + i, 1)
    panels("x2", 4, 4)
    sc(6)
    soft(6)
    sc(7)
    soft(7)
    pt(6)
    pv(6)
    pt(7)
    pv(7)
    do["samples"]()
    panels("o2", 0, 8)
    for i in range(3):
        post("o", 6 + i)


def build_cross(nc, keep, io, xm, ident, spent):
    ctx = ExitStack()
    with ctx:
        def sb(name, shape, dt=F32):
            return ctx.enter_context(nc.sbuf_tensor("b_" + name, shape, dt))

        def sem(name):
            return keep.enter_context(nc.semaphore("b_" + name))

        raw = sb("raw", [P, 4, KT, P])
        w_hi = sb("whi", [P, 2, KT, P], F32R)
        w_lo = sb("wlo", [P, 2, KT, P], F32R)
        op_hi = sb("ophi", [P, 2, KT, 384], F32R)
        op_lo = sb("oplo", [P, 2, KT, 384], F32R)
        ot = sb("ot", [P, 2, KT, 384])
        mkT = sb("mk", [P, KT, NMEM])
        mv = sb("mv", [P, 2, D])
        pm = sb("pm", [P, 2, 4, NMEM])
        pT = sb("pt", [P, 2, KT, P])
        hn = sb("hn", [P, D])
        junk = sb("junk", [P, D])
        gain = sb("gain", [P, 3, D])
        cache = sb("cache", [P, 2, D])
        tmp = sb("tmp", [P, D])
        mhalf = sb("mhalf", [P, 1])
        mstat = sb("stat", [P, 4, 2])
        mstat2 = sb("stat2", [P, 4, 1])
        mx = sb("mx", [P, 2, 4])
        nb = sb("nb", [P, 2, 4])
        rsum = sb("rsum", [P, 2, 4])
        ri = sb("ri", [P, 2, 4])
        bank = [ctx.enter_context(nc.psum_tensor(f"b_bank{n}", [P, 512], F32)) for n in range(2)]
        pair = {n: ctx.enter_context(nc.psum_tensor(f"b_pair{n}", [P, 1024], F32)) for n in (2, 4, 6)}

        memx = ot[:, 0].rearrange("p k n -> p (k n)")[:, 0:2 * D].rearrange("p (m n) -> p m n", m=2)
        qpad = pm[:].rearrange("p s h n -> p (s h n)").rearrange("p (k b r) -> p k b r", k=KT, b=NB)
        sp_ = pT[:, 1].rearrange("p k n -> p (k n)")[:, 0:NMEM]
        spT = pT[:, 1].rearrange("p k n -> p (k n)")[:, 256:512]
        vals = pair[4][:, 512:768]
        mixg = lambda g: xm[:, g, :].rearrange("p (k n) -> p k n", n=384)
        xt = lambda t: xm[:, t // 3, D * (t % 3):D * (t % 3 + 1)]
        GAIN = dict(m=2, w=0, x=1, o=2)

        raw_full = [sem(f"raw_full{n}") for n in range(4)]
        x_full = [sem(f"x_full{g}") for g in range(3)]
        mem_full, gains_full, gx_full, stored, setup = sem("mem_full"), sem("gains_full"), sem("gx_full"), sem("stored"), sem("setup")
        nat_full = [sem(f"nat_full{n}") for n in range(3)]
        owners = dict(
            act="hi_done evac_done sq_done ophi_done exp_done pta_done nata_done qpad_done",
            dve="lo_done turn_free normed oplo_done hn_done nb_done p_done ptd_done natd_done memout_done",
            pool="ms_done rstd_done",
            pe="panel_done turn_done sc_done pT_done pv_done natT_done nv_done")
        S = {n: sem(n) for names in owners.values() for n in names.split()}
        nc.clear_and_free_semaphores(spent)
        scope = ExitStack()
        block = scope.enter_context(nc.Block())

        def credit(eng, who):
            for n in owners[who].split():
                eng.sem_inc(S[n], CREDIT)

        turn = {}
        number = lambda kind, i: turn.setdefault(f"{kind}{i}", len(turn))
        norms = {}
        nothing = dict.fromkeys("panels split sc soft pt pv".split(), lambda *a: None)
        walk(dict(nothing, start=lambda: None, samples=lambda: None,
                  mem=number, preb=number,
                  post=lambda s, t: (number(s, t), norms.setdefault(("post", s, t), len(norms))),
                  prea=lambda s, t: norms.setdefault(("pre", s, t), len(norms))))

        def last_panel_before(operand):
            n = OPERANDS.index(operand) - 2
            if n < 0:
                return -1
            stage = OPERANDS[n]
            return FIRST["mv" if stage == "m" else stage] + KT - 1

        posts = [k[1:] for k in norms if k[0] == "post"]
        hn_write = {k[1:]: i for i, k in enumerate(k for k in norms if k[0] == "pre")}
        slot_of = lambda operand: OPERANDS.index(operand) % 2

        def width(stage):
            return NMEM if stage[0] == "m" else GW[int(stage[1])]

        def operand_of(stage):
            return "m" if stage[0] == "m" else stage

        def raw_count(n):
            return sum(48 if STAGES[m // KT][0] == "w" else 16 for m in range(n % 4, n + 1, 4))

        def nat_item(m):
            half, r = m // 8, m % 8
            return ("cache_mem_k" if r < 4 else "cache_mem_v"), 4 * half + r % 4

        def nat_count(m):
            return 4 * (m // 8) + m % 4

        def nat(m):
            return (ot[:, 0].rearrange("p k n -> p (k n)")[:, 0:2 * D].rearrange("p (m n) -> p m n", m=2), cache[:], mv[:])[m % 3]

        @block.sync
        def _(sp):
            sp.dma_start(memx, io["mem_prompt"][0].rearrange("(m p) n -> p m n", p=P)).then_inc(mem_full, 16)
            for i, name in ((2, "g_mem"), (0, "g_mix_post"), (1, "g_x_pre")):
                sp.dma_start(gain[:, i], io[name].rearrange("(o n) -> o n", o=1).broadcast_to([P, D])).then_inc(gains_full, 16)

            def load_panel(n):
                stage, j = STAGES[n // KT], n % KT
                sp.wait_ge(S["lo_done"], ready(n - 4))
                name = {"mk": "w_xk", "mv": "w_xv"}.get(stage) or {"w": "w_out", "x": "w_xq", "o": "w_xo"}[stage[0]]
                cols = io[name][:, P * j:P * j + P]
                if stage[0] != "w":
                    sp.dma_start(raw[:, n % 4], cols.rearrange("(k p) n -> p k n", p=P)).then_inc(raw_full[n % 4], 16)
                else:
                    sp.dma_start(raw[:, n % 4, 0:4], cols[0:SSD_W].rearrange("(k p) n -> p k n", p=P)).then_inc(raw_full[n % 4], 16)
                    for v in range(2):
                        sp.dma_start(raw[HD * v:HD * v + HD, n % 4, 4:8],
                                     cols[SSD_W + 256 * v:SSD_W + 256 * v + 256].rearrange("(k p) n -> p k n", p=HD))\
                            .then_inc(raw_full[n % 4], 16)

            for n in range(NPANELS):
                if n == 12:
                    sp.wait_ge(S["hn_done"], ready(1))
                    sp.dma_start(gain[:, 2], io["g_x_post"].rearrange("(o n) -> o n", o=1).broadcast_to([P, D])).then_inc(gx_full, 16)
                for stage, g in (("w0", 0), ("w1", 1), ("w2", 2)):
                    if n == FIRST[stage] + 6:
                        sp.wait_ge(S["oplo_done"], ready(part_of(stage, 3)))
                        if g == 2:
                            sp.wait_ge(setup, 2)
                        for i in range(3):
                            t = 3 * g + i
                            sp.dma_start(xt(t)[0:group_rows(t)], io["x"](t)).then_inc(x_full[g], 16)
                if n == FIRST["w0"] + 4:
                    for i in range(2):
                        sp.wait_ge(S["memout_done"], ready(i))
                        sp.dma_start(io["p_mem_k"][0, 0].rearrange("(m p) h d -> m p (h d)", p=P)[i], cache[:, i]).then_inc(stored, 16)
                if n == FIRST["w1"] + 4:
                    sp.wait_ge(S["memout_done"], ready(3))
                    sp.dma_start(io["p_mem_v"][0, 0].rearrange("(m p) h d -> p m (h d)", p=P), mv[:]).then_inc(stored, 16)
                if n == FIRST["o2"] + 2:
                    sp.wait_ge(stored, 48)
                    for m in range(2 * NB):
                        name, b = nat_item(m)
                        if m < 3:
                            sp.wait_ge(*((S["turn_done"], ready(turn["o5"])), (S["turn_done"], ready(turn["o5"])),
                                         (S["pv_done"], ready(7)))[m])
                        else:
                            k, _ = nat_item(m - 3)
                            if k == "cache_mem_k":
                                sp.wait_ge(S["natT_done"], ready(2 * nat_count(m - 3) + (m - 3) // 8 + 1))
                            else:
                                sp.wait_ge(S["nv_done"], ready(nat_count(m - 3)))
                        sp.dma_start(nat(m), io[name][0, b].rearrange("(m p) h d -> p m (h d)", p=P)).then_inc(nat_full[m % 3], 16)
                load_panel(n)
            sp.wait_ge(stored, 48)

        @block.gpsimd
        def _(pool):
            credit(pool, "pool")
            pool.memset(mhalf[:], -0.5).then_inc(setup, 1)
            pool.wait_ge(setup, 1)

            def stat(n):
                s = n % 4
                pool.wait_ge(S["sq_done"], ready(n))
                pool.wait_ge(S["normed"], ready(n - 4))
                pool.tensor_scalar(mstat2[:, s], mstat[:, s, 0:1], 1.0 / D, EPS, ALU.mult, ALU.add).then_inc(S["ms_done"], 1)
                pool.wait_ge(S["ms_done"], ready(n))
                pool.tensor_tensor(mstat[:, s, 1:2], mstat2[:, s], mhalf[:], ALU.pow).then_inc(S["rstd_done"], 1)

            def split(g):
                if g == 2:
                    pool.wait_ge(S["oplo_done"], ready(part_of("w2", 3)))
                    pool.memset(xt(8), 0.0).then_inc(setup, 1)

            skip = lambda *a: None
            walk(dict(panels=skip, preb=skip, sc=skip, soft=skip, pt=skip, pv=skip, mem=skip, start=skip, samples=skip, split=split,
                      post=lambda s, t: stat(norms["post", s, t]), prea=lambda s, t: stat(norms["pre", s, t])))

        def x_ready(eng, n, t):
            before = [norms["post", s, u] for s, u in posts if u == t and norms["post", s, u] < n]
            if before:
                eng.wait_ge(S["normed"], ready(max(before)))

        @block.scalar
        def _(act):
            credit(act, "act")

            def hi(n):
                act.wait_ge(raw_full[n % 4], raw_count(n))
                act.wait_ge(S["panel_done"], ready(n - 2))
                act.activation(w_hi[:, n % 2], raw[:, n % 4], ACT.Copy).then_inc(S["hi_done"], 1)

            def panels(stage, j0, cnt):
                for j in range(j0, j0 + cnt):
                    n = FIRST[stage] + j
                    w = width(stage)
                    dst = mkT[:, j, :] if stage == "mk" else ot[:, OT_SLOT[stage], j, 0:w]
                    act.wait_ge(S["panel_done"], ready(n))
                    if stage == "w0" and j == 0:
                        act.wait_ge(S["hn_done"], ready(1))
                    act.activation(dst, bank[n % 2][:, 0:w], ACT.Copy).then_inc(S["evac_done"], 1)
                    if n + 2 < NPANELS:
                        hi(n + 2)

            def split(g):
                name = f"w{g}"
                w = GW[g]
                for i in range(4):
                    act.wait_ge(S["panel_done"], ready(last_panel_before(name)))
                    act.activation(op_hi[:, slot_of(name), 2 * i:2 * i + 2, 0:w], mixg(g)[:, 2 * i:2 * i + 2, 0:w], ACT.Copy)\
                        .then_inc(S["ophi_done"], 1)

            def post(s, t):
                n, u = norms["post", s, t], turn[f"{s}{t}"]
                act.wait_ge(S["turn_done"], ready(u))
                act.wait_ge(S["normed"], ready(n - 4))
                act.wait_ge(S["sq_done"], ready(n - 1))
                act.activation(junk[:], pair[2][:], ACT.Square, accum_out=mstat[:, n % 4, 0:1]).then_inc(S["sq_done"], 1)

            def prea(s, t):
                n = norms["pre", s, t]
                if s == "m":
                    act.wait_ge(mem_full, 16)
                    src = memx[:, t]
                else:
                    x_ready(act, n, t)
                    src = xt(t)
                act.wait_ge(S["normed"], ready(n - 4))
                act.wait_ge(S["sq_done"], ready(n - 1))
                act.activation(junk[:], src, ACT.Square, accum_out=mstat[:, n % 4, 0:1]).then_inc(S["sq_done"], 1)

            def preb(s, t):
                name, c = ("m", t) if s == "m" else (f"x{t // 3}", t % 3)
                act.wait_ge(S["turn_done"], ready(turn[f"{s}{t}"]))
                act.wait_ge(S["panel_done"], ready(last_panel_before(name)))
                act.activation(op_hi[:, slot_of(name), :, P * c:P * c + P], pair[2][:].rearrange("p (k n) -> p k n", k=KT), ACT.Copy)\
                    .then_inc(S["ophi_done"], 1)

            def soft(t):
                s = t % 2
                act.wait_ge(S["nb_done"], ready(t))
                act.wait_ge(S["pT_done"], ready(t - 2))
                for h in range(4):
                    ins = act.activation(pm[:, s, h], pair[4][:, NMEM * h:NMEM * h + NMEM], ACT.Exp, bias=nb[:, s, h:h + 1],
                                         scale=1.0 / 16, accum_out=rsum[:, s, h:h + 1])
                ins.then_inc(S["exp_done"], 1)

            def pt(t):
                act.wait_ge(S["pT_done"], ready(t))
                act.wait_ge(S["pv_done"], ready(t - 2))
                act.activation(pT[:, t % 2, 0:4], pair[6][:, 0:512].rearrange("p (k n) -> p k n", k=4), ACT.Copy).then_inc(S["pta_done"], 1)

            def pv(t):
                name, c = f"o{t // 3}", t % 3
                act.wait_ge(S["pv_done"], ready(t))
                act.wait_ge(S["panel_done"], ready(last_panel_before(name)))
                act.activation(op_hi[:, slot_of(name), :, P * c:P * c + P], pair[6][:].rearrange("p (k n) -> p k n", k=KT), ACT.Copy)\
                    .then_inc(S["ophi_done"], 1)

            def samples():
                act.wait_ge(S["natd_done"], ready(0))
                act.wait_ge(S["evac_done"], ready(FIRST["x2"] + 7))
                act.activation(qpad.rearrange("p (h e) b (g t) -> p h e b g t", e=2, t=TS)[:, 0, :, :, 0],
                               ot[:, OT_SLOT["x2"], 0:2, 256:288].rearrange("p e (b t) -> p e b t", t=TS), ACT.Copy)
                for h in range(1, 4):
                    ins = act.activation(qpad.rearrange("p (h e) b (g t) -> p h e b g t", e=2, t=TS)[:, h, :, :, h],
                                         ot[:, OT_SLOT["x2"], 2 * h:2 * h + 2, 256:288].rearrange("p e (b t) -> p e b t", t=TS), ACT.Copy)
                ins.then_inc(S["qpad_done"], 1)
                for hf in range(2):
                    for i in range(4):
                        b = 4 * hf + i
                        act.wait_ge(S["natT_done"], ready(2 * b + hf))
                        act.wait_ge(S["sc_done"], ready(7 + b))
                        act.activation(mkT[:, 0:4, :], pair[2][:].rearrange("p (k n) -> p k n", k=4), ACT.Copy).then_inc(S["nata_done"], 1)
                    t = 8 + hf
                    act.wait_ge(S["nb_done"], ready(t))
                    act.wait_ge(*((S["natT_done"], ready(8)) if hf else (S["pv_done"], ready(7))))
                    act.activation(sp_, pair[4][:, 0:NMEM], ACT.Exp, bias=nb[:, t % 2, 0:1], scale=1.0 / 16,
                                   accum_out=rsum[:, t % 2, 0:1]).then_inc(S["exp_done"], 1)
                    act.wait_ge(S["natT_done"], ready(9 * hf + 8))
                    act.wait_ge(S["nv_done"], ready(4 * hf - 1))
                    act.activation(spT, pair[6][:, 512:768], ACT.Copy).then_inc(S["pta_done"], 1)
                act.wait_ge(S["nv_done"], ready(NB - 1))
                act.wait_ge(S["panel_done"], ready(last_panel_before("o2")))
                act.activation(op_hi[:, slot_of("o2"), :, 256:288], vals.rearrange("p (k n) -> p k n", k=KT), ACT.Copy)\
                    .then_inc(S["ophi_done"], 1)

            def start():
                hi(0)
                hi(1)

            walk(dict(panels=panels, post=post, prea=prea, preb=preb, split=split, sc=lambda t: None, soft=soft, pt=pt, pv=pv,
                      mem=lambda *a: None, start=start, samples=samples))

        @block.vector
        def _(dve):
            credit(dve, "dve")

            def lo(n):
                dve.wait_ge(S["hi_done"], ready(n))
                dve.tensor_tensor(w_lo[:, n % 2], raw[:, n % 4], w_hi[:, n % 2].bitcast(F32), ALU.subtract).then_inc(S["lo_done"], 1)

            def panels(stage, j0, cnt):
                for j in range(j0, j0 + cnt):
                    n = FIRST[stage] + j
                    if n + 2 < NPANELS:
                        lo(n + 2)

            def split(g):
                name, w = f"w{g}", GW[g]
                for i in range(4):
                    k = slice(2 * i, 2 * i + 2)
                    dve.wait_ge(S["ophi_done"], ready(part_of(name, i)))
                    dve.tensor_tensor(op_lo[:, slot_of(name), k, 0:w], mixg(g)[:, k, 0:w],
                                      op_hi[:, slot_of(name), k, 0:w].bitcast(F32), ALU.subtract).then_inc(S["oplo_done"], 1)

            def post(s, t):
                n, u = norms["post", s, t], turn[f"{s}{t}"]
                dve.wait_ge(S["rstd_done"], ready(n))
                dve.wait_ge(gains_full, 48)
                if s == "o":
                    dve.wait_ge(gx_full, 16)
                dve.wait_ge(x_full[t // 3], 48)
                dve.wait_ge(S["normed"], ready(n - 1))
                dve.scalar_tensor_tensor(tmp[:], pair[2][:], mstat[:, n % 4, 1:2], gain[:, GAIN[s]], ALU.mult, ALU.mult)\
                    .then_inc(S["turn_free"], 1)
                dve.wait_ge(S["turn_free"], ready(u))
                dve.tensor_tensor(xt(t), xt(t), tmp[:], ALU.add).then_inc(S["normed"], 1)

            def prea(s, t):
                n = norms["pre", s, t]
                src = memx[:, t] if s == "m" else xt(t)
                dve.wait_ge(S["rstd_done"], ready(n))
                dve.wait_ge(gains_full, 48)
                if s == "m":
                    dve.wait_ge(mem_full, 16)
                prev = [v for k, v in turn.items() if k[0] in "mx" and v < turn[f"{s}{t}"]]
                if prev:
                    dve.wait_ge(S["turn_done"], ready(max(prev)))
                if s == "x":
                    x_ready(dve, n, t)
                dve.scalar_tensor_tensor(hn[:], src, mstat[:, n % 4, 1:2], gain[:, GAIN[s]], ALU.mult, ALU.mult).then_inc(S["hn_done"], 1)
                dve.wait_ge(S["hn_done"], ready(hn_write[s, t]))
                dve.sem_inc(S["normed"], 1)

            def preb(s, t):
                name, c = ("m", t) if s == "m" else (f"x{t // 3}", t % 3)
                sl, cols = slot_of(name), slice(P * c, P * c + P)
                dve.wait_ge(S["ophi_done"], ready(part_of(name, c)))
                dve.tensor_tensor(op_lo[:, sl, :, cols], pair[2][:].rearrange("p (k n) -> p k n", k=KT),
                                  op_hi[:, sl, :, cols].bitcast(F32), ALU.subtract).then_inc(S["oplo_done"], 1)
                dve.wait_ge(S["oplo_done"], ready(part_of(name, c)))
                dve.sem_inc(S["turn_free"], 1)

            def mem(kind, i):
                u = turn[f"{kind}{i}"]
                dve.wait_ge(S["turn_done"], ready(u))
                dve.tensor_copy((cache if kind == "k" else mv)[:, i], pair[2][:]).then_inc(S["memout_done"], 1)
                dve.wait_ge(S["memout_done"], ready(i + (0 if kind == "k" else 2)))
                dve.sem_inc(S["turn_free"], 1)

            def soft(t, rows=4, shape=None):
                s = t % 2
                dve.wait_ge(S["sc_done"], ready(t if t < 8 else 7 + 4 * (t - 7)))
                dve.wait_ge(S["exp_done"], ready(t - 2))
                dve.tensor_reduce(mx[:, s, 0:rows], pair[4][:, 0:NMEM * rows].rearrange("p (h n) -> p h n", h=rows),
                                  mybir.AxisListType.X, ALU.max).then_inc(S["p_done"], 1)
                dve.wait_ge(S["p_done"], ready(3 * t))
                dve.tensor_scalar(nb[:, s, 0:rows], mx[:, s, 0:rows], -1.0 / 16, None, ALU.mult).then_inc(S["nb_done"], 1)
                dve.wait_ge(S["exp_done"], ready(t))
                dve.reciprocal(ri[:, s, 0:rows], rsum[:, s, 0:rows]).then_inc(S["p_done"], 1)
                dve.wait_ge(S["p_done"], ready(3 * t + 1))
                place = pm[:, s] if t < 8 else sp_.rearrange("p (h n) -> p h n", h=1)
                dve.tensor_tensor(place, place, bc(ri[:, s, 0:rows].rearrange("p (h u) -> p h u", u=1), [P, rows, NMEM]), ALU.mult)\
                    .then_inc(S["p_done"], 1)

            def pt(t):
                dve.wait_ge(S["pT_done"], ready(t))
                dve.wait_ge(S["pv_done"], ready(t - 2))
                dve.tensor_copy(pT[:, t % 2, 4:8], pair[6][:, 512:1024].rearrange("p (k n) -> p k n", k=4)).then_inc(S["ptd_done"], 1)

            def pv(t):
                name, c = f"o{t // 3}", t % 3
                sl, cols = slot_of(name), slice(P * c, P * c + P)
                dve.wait_ge(S["ophi_done"], ready(part_of(name, c)))
                dve.tensor_tensor(op_lo[:, sl, :, cols], pair[6][:].rearrange("p (k n) -> p k n", k=KT),
                                  op_hi[:, sl, :, cols].bitcast(F32), ALU.subtract).then_inc(S["oplo_done"], 1)

            def samples():
                dve.wait_ge(S["pT_done"], ready(7))
                dve.memset(pm[:], 0.0).then_inc(S["natd_done"], 1)
                for hf in range(2):
                    for i in range(4):
                        b = 4 * hf + i
                        dve.wait_ge(S["natT_done"], ready(2 * b + hf + 1))
                        dve.wait_ge(S["sc_done"], ready(7 + b))
                        dve.tensor_copy(mkT[:, 4:8, :], pair[6][:].rearrange("p (k n) -> p k n", k=4)).then_inc(S["natd_done"], 1)
                    soft(8 + hf, 1)
                sl = slot_of("o2")
                dve.wait_ge(S["ophi_done"], ready(part_of("o2", 2)))
                dve.tensor_tensor(op_lo[:, sl, :, 256:288], vals.rearrange("p (k n) -> p k n", k=KT),
                                  op_hi[:, sl, :, 256:288].bitcast(F32), ALU.subtract).then_inc(S["oplo_done"], 1)

            def start():
                lo(0)
                lo(1)

            walk(dict(panels=panels, post=post, prea=prea, preb=preb, split=split, sc=lambda t: None, soft=soft, pt=pt, pv=pv,
                      mem=mem, start=start, samples=samples))

        @block.tensor
        def _(pe):
            credit(pe, "pe")

            def panels(stage, j0, cnt):
                w, name = width(stage), operand_of(stage)
                sl = slot_of(name)
                pe.wait_ge(S["oplo_done"], ready(part_of(name, PARTS[name[0]] - 1)))
                for j in range(j0, j0 + cnt):
                    n = FIRST[stage] + j
                    pe.wait_ge(S["lo_done"], ready(n))
                    pe.wait_ge(S["evac_done"], ready(n - 2))
                    for k in range(KT):
                        for m, (a, b) in enumerate(((w_hi, op_hi), (w_hi, op_lo), (w_lo, op_hi))):
                            ins = pe.matmul(bank[n % 2][:, 0:w], a[:, n % 2, k, :], b[:, sl, k, 0:w],
                                            start=(k == 0 and m == 0), stop=(k == KT - 1 and m == 2))
                    ins.then_inc(S["panel_done"], 1)

            def turned(u, srcs, w=P):
                pe.wait_ge(S["turn_free"], ready(u - 1))
                for k, a in enumerate(srcs):
                    ins = pe.transpose(pair[2][:, P * k:P * k + P], a, ident[:])
                ins.then_inc(S["turn_done"], 1)

            def post(s, t):
                stage = f"{s}{t // 3}"
                pe.wait_ge(S["evac_done"], ready(FIRST[stage] + 7))
                c = P * (t % 3)
                turned(turn[f"{s}{t}"], [ot[:, OT_SLOT[stage], k, c:c + P] for k in range(KT)])

            def preb(s, t):
                pe.wait_ge(S["hn_done"], ready(hn_write[s, t]))
                turned(turn[f"{s}{t}"], [hn[:, P * k:P * k + P] for k in range(KT)])

            def mem(kind, i):
                pe.wait_ge(S["evac_done"], ready(FIRST["m" + kind] + 7))
                src = mkT if kind == "k" else ot[:, OT_SLOT["mv"]]
                turned(turn[f"{kind}{i}"], [src[:, k, P * i:P * i + P] for k in range(KT)])

            def sc(t):
                stage = f"x{t // 3}"
                pe.wait_ge(S["evac_done"], ready(FIRST[stage] + 7))
                pe.wait_ge(S["exp_done"], ready(t - 1))
                c = P * (t % 3)
                for h in range(4):
                    for e in range(2):
                        ins = pe.matmul(pair[4][:, NMEM * h:NMEM * h + NMEM], ot[:, OT_SLOT[stage], 2 * h + e, c:c + P],
                                        mkT[:, 2 * h + e, :], start=(e == 0), stop=(e == 1))
                ins.then_inc(S["sc_done"], 1)

            def pt(t):
                pe.wait_ge(S["p_done"], ready(3 * t + 2))
                if t:
                    c = t - 1
                    pe.wait_ge(S["oplo_done"], ready(part_of(f"o{c // 3}", c % 3)))
                for k in range(KT):
                    ins = pe.transpose(pair[6][:, P * k:P * k + P], pm[:, t % 2, k // 2, P * (k % 2):P * (k % 2) + P], ident[:])
                ins.then_inc(S["pT_done"], 1)

            def pv(t):
                pe.wait_ge(S["pta_done"], ready(t))
                pe.wait_ge(S["ptd_done"], ready(t))
                if t == 0:
                    pe.wait_ge(S["memout_done"], ready(3))
                for k in range(KT):
                    for m in range(2):
                        ins = pe.matmul(pair[6][:, P * k:P * k + P], mv[:, m, P * k:P * k + P], pT[:, t % 2, 2 * (k // 2) + m],
                                        start=(m == 0), stop=(m == 1))
                ins.then_inc(S["pv_done"], 1)

            def samples():
                pe.wait_ge(S["oplo_done"], ready(part_of("o2", 1)))
                pe.wait_ge(S["turn_free"], ready(turn["o5"]))
                loads_of = lambda kind, b: [m for m in range(2 * NB) if nat_item(m) == (kind, b)][0]
                for hf in range(2):
                    for i in range(4):
                        b = 4 * hf + i
                        m = loads_of("cache_mem_k", b)
                        pe.wait_ge(nat_full[m % 3], 16 * (m // 3 + 1))
                        for q, (pr, before) in enumerate(((2, S["nata_done"]), (6, S["natd_done"]))):
                            pe.wait_ge(before, ready(b - 1 + q))
                            for k in range(KT):
                                f = 4 * q + k // 2
                                ins = pe.transpose(pair[pr][:, P * k:P * k + P], nat(m)[:, k % 2, P * f:P * f + P], ident[:])
                            ins.then_inc(S["natT_done"], 1)
                        pe.wait_ge(S["nata_done"], ready(b))
                        pe.wait_ge(S["natd_done"], ready(b + 1))
                        pe.wait_ge(S["qpad_done"], ready(0))
                        if i == 0:
                            pe.wait_ge(S["exp_done"], ready(7 + hf))
                        for k in range(KT):
                            ins = pe.matmul(pair[4][32 * i:32 * i + 32, 0:NMEM], qpad[:, k, b, :], mkT[:, k, :],
                                            start=(k == 0), stop=(k == KT - 1))
                        ins.then_inc(S["sc_done"], 1)
                    t = 8 + hf
                    pe.wait_ge(S["p_done"], ready(3 * t + 2))
                    for m in range(2):
                        ins = pe.transpose(pair[6][:, 512 + P * m:640 + P * m], sp_[:, P * m:P * m + P], ident[:])
                    ins.then_inc(S["natT_done"], 1)
                    pe.wait_ge(S["pta_done"], ready(t))
                    for i in range(4):
                        b = 4 * hf + i
                        m = loads_of("cache_mem_v", b)
                        pe.wait_ge(nat_full[m % 3], 16 * (m // 3 + 1))
                        for k in range(KT):
                            for e in range(2):
                                ins = pe.matmul(vals[:, 32 * k + TS * b:32 * k + TS * b + TS], nat(m)[:, e, P * k:P * k + P],
                                                spT[:, P * e + 32 * i + TS * (k // 2):P * e + 32 * i + TS * (k // 2) + TS],
                                                start=(e == 0), stop=(e == 1))
                        ins.then_inc(S["nv_done"], 1)

            walk(dict(panels=panels, post=post, prea=lambda *a: None, preb=preb, split=lambda g: None, sc=sc,
                      soft=lambda t: None, pt=pt, pv=pv, mem=mem, start=lambda: None, samples=samples))

        scope.close()


def build_ffn(nc, keep, io, xm, ident):
    ctx = ExitStack()
    HK = FT // 2
    GUP = 2 * FT
    DOWN = 2 * KT
    UNITS = GUP + DOWN
    with ctx:
        def sb(name, shape, dt=F32):
            return ctx.enter_context(nc.sbuf_tensor("f_" + name, shape, dt))

        def sem(name):
            return keep.enter_context(nc.semaphore("f_" + name))

        raw = sb("raw", [P, 4, HK, P])
        w_hi = sb("whi", [P, 2, HK, P], F32R)
        w_lo = sb("wlo", [P, 2, HK, P], F32R)
        x_hi = sb("xhi", [P, KT, 384], F32R)
        x_lo = sb("xlo", [P, KT, 384], F32R)
        a_hi = sb("ahi", [P, FT, 384], F32R)
        a_lo = sb("alo", [P, FT, 384], F32R)
        sg = sb("sg", [P, 2, 384])
        act_f = sb("act", [P, 2, 384])
        ot = sb("ot", [P, KT, 384])
        hn = sb("hn", [P, D])
        gain = sb("gain", [P, 2, D])
        mhalf = sb("mhalf", [P, 1])
        st = {k: sb("st" + k, [P, 3]) for k in ("pre", "post")}
        bank = [ctx.enter_context(nc.psum_tensor(f"f_bank{n}", [P, 512], F32)) for n in range(4)]
        pair = [ctx.enter_context(nc.psum_tensor(f"f_pair{n}", [P, 1024], F32)) for n in range(2)]
        tmp = sb("tmp", [P, D])

        raw_full = [sem(f"raw_full{n}") for n in range(4)]
        gains_full, setup, stored = sem("gains_full"), sem("setup"), sem("stored")
        owners = dict(
            act="hi_done silu_done ahi_done ot_done presq_done postsq_done xhi_done",
            dve="lo_done gu_done alo_done hn_done xlo_done scaled_done x_done",
            pool="prems_done prers_done postms_done postrs_done",
            pe="unit_done preT_done postT_done")
        S = {n: sem(n) for names in owners.values() for n in names.split()}

        def credit(eng, who):
            for n in owners[who].split():
                eng.sem_inc(S[n], CREDIT)

        xt = lambda g, i: xm[:, g, ds(D * i, D)]
        post_pair = lambda i: pair[i % 2]

        def walk(eng, f, loops=True):
            for i in range(3):
                f["pre"](0, i, ())
            f["start"]()
            for g in range(3):
                f["gate4"](g, 0, False)
                if g:
                    f["post"](g - 1, 0)
                    f["post"](g - 1, 1)
                f["gate4"](g, 1, False)
                if g:
                    f["post"](g - 1, 2)
                with eng.Fori(0, GUP // 4 - 3) as i:
                    f["gate4"](g, i + 2, False)
                f["gate4"](g, GUP // 4 - 1, True)
                if g < 2:
                    with eng.Fori(0, 3) as i:
                        f["down4"](g, i, False, lambda u: f["pre"](g + 1, i, (u,)))
                    f["down4"](g, 3, True, lambda u: None)
                else:
                    with eng.Fori(0, 3) as i:
                        f["down4"](g, i, False, lambda u: None)
                    f["down4"](g, 3, True, lambda u: None)
            for i in range(3):
                f["post"](2, i)

        scope = ExitStack()
        block = scope.enter_context(nc.Block())

        @block.sync
        def _(sp):
            for i, name in enumerate(("g_ffn_pre", "g_ffn_post")):
                sp.dma_start(gain[:, i], io[name].rearrange("(o n) -> o n", o=1).broadcast_to([P, D])).then_inc(gains_full, 16)

            def store(g):
                for i in range(3):
                    t = 3 * g + i
                    sp.wait_ge(S["x_done"], ready(t))
                    sp.dma_start(io["y"](t), xt(g, i)[0:group_rows(t)]).then_inc(stored, 16)

            for g in range(3):
                for u in range(UNITS):
                    n = UNITS * g + u
                    sp.wait_ge(S["lo_done"], ready(n - 4))
                    if u < GUP:
                        j = u // 2
                        w = io["w_up" if u % 2 else "w_gate"][:, P * j:P * j + P]
                        sp.dma_start(raw[:, n % 4, 0:KT], w.rearrange("(k p) n -> p k n", p=P)).then_inc(raw_full[n % 4], 16)
                    else:
                        j, hf = (u - GUP) // 2, (u - GUP) % 2
                        w = io["w_down"][P * HK * hf:P * HK * (hf + 1), P * j:P * j + P]
                        sp.dma_start(raw[:, n % 4], w.rearrange("(k p) n -> p k n", p=P)).then_inc(raw_full[n % 4], 16)
                    if g and u == 16:
                        store(g - 1)
            store(2)
            sp.wait_ge(stored, 16 * 9)

        @block.gpsimd
        def _(pool):
            credit(pool, "pool")
            pool.memset(mhalf[:], -0.5).then_inc(setup, 1)
            pool.wait_ge(setup, 1)

            def stat(kind, t):
                a = st[kind]
                pool.wait_ge(S[kind + "sq_done"], ready(t))
                pool.tensor_scalar(a[:, 1:2], a[:, 0:1], 1.0 / D, EPS, ALU.mult, ALU.add).then_inc(S[kind + "ms_done"], 1)
                pool.wait_ge(S[kind + "ms_done"], ready(t))
                pool.wait_ge(S["hn_done" if kind == "pre" else "scaled_done"], ready(t - 1))
                pool.tensor_tensor(a[:, 2:3], a[:, 1:2], mhalf[:], ALU.pow).then_inc(S[kind + "rs_done"], 1)

            for i in range(3):
                stat("pre", i)
            for g in range(3):
                if g:
                    for i in range(3):
                        stat("post", 3 * (g - 1) + i)
                if g < 2:
                    for i in range(3):
                        stat("pre", 3 * (g + 1) + i)
            for i in range(3):
                stat("post", 6 + i)

        @block.scalar
        def _(act):
            credit(act, "act")

            def hi(n, s, it, kt):
                act.wait_ge(raw_full[s], 16 * it + 16)
                act.wait_ge(S["unit_done"], ready(n - 2))
                act.activation(w_hi[:, s % 2, 0:kt], raw[:, s, 0:kt], ACT.Copy).then_inc(S["hi_done"], 1)

            def ahead(g, it, last, s, kt, next_kt):
                n0 = UNITS * g + it * 4
                q = UNITS // 4 * g + it
                if last and s >= 2 and g == 2 and kt == HK:
                    return
                if s < 2:
                    hi(n0 + s + 2, s + 2, q, kt)
                else:
                    hi(n0 + s + 2, s - 2, q + 1, next_kt if last else kt)

            def gate4(g, it, last):
                w = GW[g]
                for s in range(4):
                    n = UNITS * g + it * 4 + s
                    j = it * 2 + s // 2
                    q = FT * g + j
                    if s % 2 == 0:
                        act.wait_ge(S["unit_done"], ready(n))
                        act.wait_ge(S["gu_done"], ready(q - 2))
                        act.activation(sg[:, s // 2, 0:w], bank[0][:, 0:w], ACT.Silu).then_inc(S["silu_done"], 1)
                    ahead(g, it, last, s, KT, HK)
                    if s % 2:
                        act.wait_ge(S["gu_done"], ready(q))
                        act.activation(a_hi[:, ds(j, 1), 0:w], act_f[:, s // 2:s // 2 + 1, 0:w], ACT.Copy).then_inc(S["ahi_done"], 1)

            def down4(g, it, last, pre):
                w = GW[g]
                for s in range(4):
                    n = UNITS * g + GUP + it * 4 + s
                    if s % 2:
                        act.wait_ge(S["unit_done"], ready(n))
                        act.activation(ot[:, ds(it * 2 + s // 2, 1), 0:w],
                                       bank[2 + s // 2][:, 0:w].rearrange("p (o n) -> p o n", o=1), ACT.Copy).then_inc(S["ot_done"], 1)
                    ahead(g, it + GUP // 4, last, s, HK, KT)
                    pre(s)

            def pre(g, i, where):
                t = 3 * g + i
                if not where or where[0] == 0:
                    act.wait_ge(S["prems_done"], ready(t - 1))
                    act.wait_ge(S["preT_done"], ready(t - 1))
                    act.activation(hn[:], xt(g, i), ACT.Square, accum_out=st["pre"][:, 0:1]).then_inc(S["presq_done"], 1)
                if not where or where[0] == 1:
                    act.wait_ge(S["preT_done"], ready(t))
                    act.wait_ge(S["unit_done"], ready(UNITS * (g - 1) + GUP - 1) if g else CREDIT)
                    act.activation(x_hi[:, :, ds(P * i, P)], pair[1][:].rearrange("p (k n) -> p k n", k=KT), ACT.Copy)\
                        .then_inc(S["xhi_done"], 1)

            def post(g, i):
                t = 3 * g + i
                act.wait_ge(S["postT_done"], ready(t))
                act.wait_ge(S["postms_done"], ready(t - 1))
                act.wait_ge(S["x_done"], ready(t - 1))
                act.activation(tmp[:], post_pair(i)[:], ACT.Square, accum_out=st["post"][:, 0:1]).then_inc(S["postsq_done"], 1)

            def start():
                hi(0, 0, 0, KT)
                hi(1, 1, 0, KT)

            walk(act, dict(gate4=gate4, down4=down4, pre=pre, post=post, start=start))

        @block.vector
        def _(dve):
            credit(dve, "dve")
            dve.wait_ge(gains_full, 32)

            def lo(n, s, kt):
                dve.wait_ge(S["hi_done"], ready(n))
                dve.tensor_tensor(w_lo[:, s % 2, 0:kt], raw[:, s, 0:kt], w_hi[:, s % 2, 0:kt].bitcast(F32), ALU.subtract)\
                    .then_inc(S["lo_done"], 1)

            def ahead(g, it, last, s, kt, next_kt):
                if last and s >= 2 and g == 2 and kt == HK:
                    return
                lo(UNITS * g + it * 4 + s + 2, (s + 2) % 4, next_kt if last and s >= 2 else kt)

            def gate4(g, it, last):
                w = GW[g]
                for s in range(4):
                    n = UNITS * g + it * 4 + s
                    j = it * 2 + s // 2
                    q = FT * g + j
                    h = slice(s // 2, s // 2 + 1)
                    if s % 2:
                        dve.wait_ge(S["silu_done"], ready(q))
                        dve.wait_ge(S["unit_done"], ready(n))
                        dve.wait_ge(S["alo_done"], ready(q - 2))
                        dve.tensor_tensor(act_f[:, s // 2, 0:w], sg[:, s // 2, 0:w], bank[1][:, 0:w], ALU.mult).then_inc(S["gu_done"], 1)
                    ahead(g, it, last, s, KT, HK)
                    if s % 2:
                        dve.wait_ge(S["ahi_done"], ready(q))
                        dve.tensor_tensor(a_lo[:, ds(j, 1), 0:w], act_f[:, h, 0:w], a_hi[:, ds(j, 1), 0:w].bitcast(F32),
                                          ALU.subtract).then_inc(S["alo_done"], 1)

            def down4(g, it, last, pre):
                for s in range(4):
                    ahead(g, it + GUP // 4, last, s, HK, KT)
                    pre(s)

            def pre(g, i, where):
                t = 3 * g + i
                if not where or where[0] == 0:
                    dve.wait_ge(S["prers_done"], ready(t))
                    dve.scalar_tensor_tensor(hn[:], xt(g, i), st["pre"][:, 2:3], gain[:, 0], ALU.mult, ALU.mult)\
                        .then_inc(S["hn_done"], 1)
                if not where or where[0] == 1:
                    dve.wait_ge(S["xhi_done"], ready(t))
                    cols = ds(P * i, P)
                    dve.tensor_tensor(x_lo[:, :, cols], pair[1][:].rearrange("p (k n) -> p k n", k=KT),
                                      x_hi[:, :, cols].bitcast(F32), ALU.subtract).then_inc(S["xlo_done"], 1)

            def post(g, i):
                t = 3 * g + i
                dve.wait_ge(S["postrs_done"], ready(t))
                dve.scalar_tensor_tensor(tmp[:], post_pair(i)[:], st["post"][:, 2:3], gain[:, 1], ALU.mult, ALU.mult)\
                    .then_inc(S["scaled_done"], 1)
                dve.wait_ge(S["scaled_done"], ready(t))
                dve.tensor_tensor(xt(g, i), xt(g, i), tmp[:], ALU.add).then_inc(S["x_done"], 1)

            def start():
                lo(0, 0, KT)
                lo(1, 1, KT)

            walk(dve, dict(gate4=gate4, down4=down4, pre=pre, post=post, start=start))

        @block.tensor
        def _(pe):
            credit(pe, "pe")

            def unit(n, s, out, a_h, a_l, k0, kt, first, last, w):
                pe.wait_ge(S["lo_done"], ready(n))
                for k in range(kt):
                    for m, (a, b) in enumerate(((w_hi, a_h), (w_hi, a_l), (w_lo, a_h))):
                        ins = pe.matmul(out, a[:, s % 2, k, :], b[:, k0 + k, 0:w], start=(first and k == 0 and m == 0),
                                        stop=(last and k == kt - 1 and m == 2))
                ins.then_inc(S["unit_done"], 1)

            def gate4(g, it, last):
                w = GW[g]
                pe.wait_ge(S["xlo_done"], ready(3 * g + 2))
                for s in range(4):
                    q = FT * g + it * 2 + s // 2
                    pe.wait_ge(S["gu_done" if s % 2 else "silu_done"], ready(q - 1))
                    unit(UNITS * g + it * 4 + s, s, bank[s % 2][:, 0:w], x_hi, x_lo, 0, KT, True, True, w)

            def down4(g, it, last, pre):
                w = GW[g]
                for s in range(4):
                    if s % 2 == 0:
                        pe.wait_ge(S["alo_done"], ready(FT * g + FT - 1))
                        pe.wait_ge(S["ot_done"], ready(KT * g + it * 2 + s // 2 - 2))
                    unit(UNITS * g + GUP + it * 4 + s, s, bank[2 + s // 2][:, 0:w], a_hi, a_lo, HK * (s % 2), HK,
                         s % 2 == 0, s % 2 == 1, w)
                    pre(s)

            def pre(g, i, where):
                t = 3 * g + i
                if not where or where[0] == 1:
                    pe.wait_ge(S["hn_done"], ready(t))
                    pe.wait_ge(S["xlo_done"], ready(t - 1))
                    pe.wait_ge(S["scaled_done"], ready(3 * (g - 2) + 1) if g > 1 else CREDIT)
                    for k in range(KT):
                        ins = pe.transpose(pair[1][:, P * k:P * k + P], hn[:, P * k:P * k + P], ident[:])
                    ins.then_inc(S["preT_done"], 1)

            def post(g, i):
                t = 3 * g + i
                pe.wait_ge(S["ot_done"], ready(KT * g + KT - 1))
                if i == 1:
                    pe.wait_ge(S["xlo_done"], ready(3 * min(g + 1, 2) + 2))
                pe.wait_ge(S["scaled_done"], ready(t - 2))
                for k in range(KT):
                    ins = pe.transpose(post_pair(i)[:, P * k:P * k + P], ot[:, k, P * i:P * i + P], ident[:])
                ins.then_inc(S["postT_done"], 1)

            walk(pe, dict(gate4=gate4, down4=down4, pre=pre, post=post, start=lambda: None))

        scope.close()


def hymba_step(nc, io):
    with ExitStack() as keep:
        xm = keep.enter_context(nc.sbuf_tensor("xm", [P, 3, 3 * D], F32))
        ident = keep.enter_context(nc.sbuf_tensor("ident", [P, P], F32))
        spent = []
        build_mixers(nc, spent, io, lambda g: xm[:, g, :].rearrange("p (k n) -> p k n", n=384), ident)
        build_cross(nc, keep, io, xm, ident, spent)
        build_ffn(nc, keep, io, xm, ident)


_INS = ["x_prompt", "x_sample", "state_ssm", "state_conv", "cache_win_k", "cache_win_v", "cache_mem_k", "cache_mem_v",
        "mem_prompt", "g_mix_pre", "w_in", "conv_w", "conv_b", "dt_bias", "a_log", "d_skip", "g_ssd_norm", "sinks", "w_out",
        "g_mix_post", "g_x_pre", "w_xq", "g_mem", "w_xk", "w_xv", "w_xo", "g_x_post", "g_ffn_pre", "w_gate", "w_up", "w_down",
        "g_ffn_post"]
_STATES = 9
_OUTS = dict(y_prompt=(1, SEQ, D), y_sample=(NB, TS, D), p_ssm=(1, 1, HEADS, HD, NST), p_conv=(1, 1, 3, XBC),
             p_win_k=(1, 1, P, 2, HD), p_win_v=(1, 1, P, 2, HD), p_mem_k=(1, 1, NMEM, 4, 256), p_mem_v=(1, 1, NMEM, 4, 256),
             s_ssm=(1, NB, HEADS, HD, NST), s_conv=(1, NB, 3, XBC), s_win_k=(1, NB, P, 2, HD), s_win_v=(1, NB, P, 2, HD))


def _io(nc, arrays):
    io = {}
    for i, name in enumerate(_INS):
        ap = nc.dram_tensor(name, arrays[name].shape, F32, kind="ExternalInput").ap()
        io[name] = ap if i < _STATES else ap[0]
    for name, shape in _OUTS.items():
        io[name] = nc.dram_tensor(name, shape, F32, kind="ExternalOutput").ap()
    rows = lambda full, tile: lambda t: full[0, P * t:P * t + P, :] if t < NCH else tile.rearrange("b t d -> (b t) d")
    io["x"] = rows(io["x_prompt"], io["x_sample"])
    io["y"] = rows(io["y_prompt"], io["y_sample"])
    return io


def kernel(**inputs):
    import numpy as np
    import concourse.bacc as bacc
    from concourse.bass_utils import run_bass_kernel_spmd

    arrays = {name: np.ascontiguousarray(inputs[name]) for name in _INS}
    nc = bacc.Bacc("TRN2", target_bir_lowering=False, num_devices=1)
    hymba_step(nc, _io(nc, arrays))
    nc.finalize()
    r = run_bass_kernel_spmd(nc, [arrays], core_ids=[0])
    return tuple(r.results[0][name] for name in _OUTS)
```

```python
from contextlib import ExitStack

import concourse.bass as bass
from concourse import mybir

F32 = mybir.dt.float32
F32R = mybir.dt.float32r
ALU = mybir.AluOpType
ACT = mybir.ActivationFunctionType
ds = bass.ds

P = 128
D = 1024
KT = D // P
SEQ = 1024
NCH = SEQ // P
NB, TS = 8, 4
NS = NB * TS
NTOK = SEQ + NS
SSD_W = 512
XBC = 1024
HEADS = 8
HD = 64
NST = 128
C_Z, C_XBC, C_DT, C_Q, C_K, C_V = 0, 512, 1536, 1544, 2056, 2184
DFF = 2816
FT = DFF // P
NMEM = 256
EPS = 1e-6
NEG = -1.0e30
GW = (384, 384, 288)
G0 = (0, 384, 768)
CREDIT = 32

T_XBC, T_Z, T_Q, T_K, T_V = 0, 8, 12, 16, 17
NPT = 18
NPA = NPT + 1
NMP = 2 * KT
MEM0 = 3 * NPA
NPANELS_1 = MEM0 + NMP


def ready(n):
    return n + 1 + CREDIT


def group_rows(t):
    return NS if t == NCH else P


def bc(ap, shape):
    return ap.broadcast_to(shape)


def build_mixers(nc, spent, io, mixT, residual, ident):
    ctx = ExitStack()
    with ctx:
        def sb(name, shape, dt=F32):
            return ctx.enter_context(nc.sbuf_tensor(name, shape, dt))

        def sem(name):
            spent.append(nc.alloc_semaphore(name=name))
            return spent[-1]

        raw = sb("a_raw", [P, 3, KT, P])
        w_hi = sb("a_whi", [P, 2, KT, P], F32R)
        w_lo = sb("a_wlo", [P, 2, KT, P], F32R)
        h_hi = sb("a_hhi", [P, KT, 384], F32R)
        h_lo = sb("a_hlo", [P, KT, 384], F32R)
        hn = [sb("a_hn0", [P, D]), sb("a_hn1", [P, D])]
        xt = lambda t: residual[:, 1, D * (t % 3):D * (t % 3 + 1)]
        gpre = sb("a_gpre", [P, D])
        ss = sb("a_ss", [P, 11])
        ms = sb("a_ms", [P, 11])
        rs = sb("a_rs", [P, 11])
        proj = sb("a_proj", [P, 2, NPT, 3 + 384])
        dtr = sb("a_dtr", [HEADS, 384])
        triu = sb("c_triu", [P, P])
        slow = sb("c_slow", [P, P])
        ones = sb("c_ones", [P, P])
        band = sb("c_band", [P, 2 * P])
        mask = sb("c_mask", [P, 2 * P])
        eps = sb("c_eps", [P, 2])
        mhalf = sb("c_mhalf", [P, 9])
        convw = sb("c_convw", [P, 4, 8])
        convb = sb("c_convb", [P, 8])
        graw = sb("c_graw", [44, P])
        dtb = sb("c_dtb", [P, HEADS])
        nega = sb("c_nega", [P, HEADS])
        dsk = sb("c_dsk", [P, HEADS])
        gssd = sb("c_gssd", [P, 4])
        nsink = sb("c_nsink", [P, 8])
        dx = sb("d_x", [P, 3 * HEADS])
        dna = sb("d_na", [P, 3 * HEADS])
        de = sb("d_e", [P, 3 * HEADS])
        du = sb("d_u", [P, 3 * HEADS])
        dl = sb("d_l", [P, 3 * HEADS])
        dv = sb("d_v", [P, 3 * HEADS])
        dw = sb("d_w", [P, 3 * HEADS])
        dts = [sb(f"d_dt{n}", [P, 3, HEADS]) for n in range(2)]
        adts = [sb(f"d_adt{n}", [P, 3, HEADS]) for n in range(2)]
        decays = [sb(f"d_decay{n}", [P, 3, 3 * HEADS]) for n in range(2)]
        xc = sb("k_xc", [P, 8, P])
        tz = sb("k_tz", [P, 4, P])
        zs = sb("k_zs", [P, 4, P])
        xs = sb("k_xs", [P, SSD_W])
        xdt = sb("k_xdt", [P, SSD_W])
        xdd = sb("k_xdd", [P, SSD_W])
        yd = xs
        bt = sb("k_bt", [P, 2, P])
        rr = sb("k_rr", [P, HEADS, P])
        mm = sb("k_mm", [P, HEADS, P])
        cbm = sb("k_cbm", [P, 2, P])
        yt = sb("k_yt", [P, SSD_W])
        un = sb("k_un", [P, SSD_W])
        ssu = sb("k_ssu", [P, 2])
        rsu = sb("k_rsu", [P, 2])
        st = sb("k_state", [P, SSD_W])
        qs = sb("k_qs", [P, 4, P])
        kv = sb("k_kv", [P, 3, P])
        kw = kv[:, 0:2, :].rearrange("p m n -> p (m n)")
        vs = kv[:, 2, :]
        vw = sb("k_vw", [P, 2, P])
        sc = sb("k_sc", [P, 4, 2 * P])
        pt = sb("k_pt", [P, 8, P])

        def conv_place(where):
            if where < 2:
                a = residual[:, 2, 0:2 * D].rearrange("p (m k n) -> p m k n", m=2, k=8)
                return a[:, 0], a[:, 1]
            a = proj[:, 1].rearrange("p k n -> p (k n)")[:, 4 * D:6 * D].rearrange("p (m k n) -> p m k n", m=2, k=8)
            return a[:, 0], a[:, 1]

        mem_kv = proj[:, 1].rearrange("p k n -> p (k n)")[:, 0:4 * D].rearrange("p (a m n) -> p a m n", a=2, m=2)
        x_in = lambda t: xt(t) if t < 9 else hn[t % 2][:]
        square_out = residual[:, 2, 2 * D:3 * D]
        mx = sb("k_mx", [P, 8])
        nb_ = sb("k_nb", [P, 8])
        sd = sb("k_sd", [P, 8])
        es = sb("k_es", [P, 8])
        rsum = sb("k_rsum", [P, 8])
        den = sb("k_den", [P, 8])
        ri = sb("k_ri", [P, 8])
        att = sb("k_att", [P, 4, 2, HD])

        bank = [ctx.enter_context(nc.psum_tensor(f"bank{n}", [P, 512], F32)) for n in range(8)]

        raw_full = [sem(f"raw_full{n}") for n in range(3)]
        x_full = [sem(f"x_full{n}") for n in range(3)]
        gpre_in, consts_in, consts_done, gmem_in, mem_stored = sem("gpre_in"), sem("consts_in"), sem("consts_done"), sem("gmem_in"), sem("mem_stored")
        names = """consts_T cols_done hi_done lo_done panel_done evac_done sumsq_done mean_done rstd_done hn_done hT_done hhi_done
        hlo_done halo_done dtT_done dt_steps dt_steps2 dt_exp dt_ln adt_done cum_done decay_done
        conv0_done conv_done tanhc_done xc_done tanhz_done zs_done qs_done k_shift kv_done scores_open
        t1_done xdt_done xs_done bt_done vshift_done vw_done yd_done xdd_done rr_done cb_done seg_done cbm_done exp_done mm_done
        ydiag_done yoff_done chst_done zT_done t_yoff t_ydiag t_y u_done usq_done um_done ur_done un_done
        sdec_done state_done sc_done msk_done nb_done sd_done es_done p_done den_done ri_done mask_done
        pT_done pTa_done pTv_done pv_done att_done unT_done mixs_done attT_done mixa_done""".split()
        S = {n: sem(n) for n in names}

        in_block = ExitStack()
        block = in_block.enter_context(nc.Block())

        owners = {
            "act": "cols_done hi_done evac_done sumsq_done hhi_done dt_exp dt_ln decay_done conv0_done tanhc_done tanhz_done "
                   "qs_done kv_done xs_done bt_done vw_done exp_done usq_done es_done p_done pTa_done mixs_done mixa_done",
            "dve": "k_shift vshift_done mask_done scores_open lo_done hn_done hlo_done dt_steps dt_steps2 adt_done conv_done xc_done zs_done xdt_done cbm_done mm_done t_yoff "
                   "t_ydiag t_y u_done un_done state_done msk_done nb_done sd_done den_done ri_done pTv_done att_done",
            "pool": "mean_done rstd_done halo_done yd_done xdd_done rr_done um_done ur_done sdec_done",
            "pe": "consts_T panel_done hT_done dtT_done cum_done t1_done cb_done seg_done ydiag_done yoff_done chst_done zT_done "
                  "sc_done pT_done pv_done unT_done attT_done",
        }

        def credit(eng, who):
            for n in owners[who].split():
                eng.sem_inc(S[n], CREDIT)

        x_rows = io["x"]
        row = lambda name: io[name].rearrange("(o n) -> o n", o=1)
        loads = [
            (graw[0:32, :], io["conv_w"].rearrange("t (k p) -> (t k) p", p=P)),
            (graw[32:40, :], io["conv_b"].rearrange("(k p) -> k p", p=P)),
            (graw[40:44, :], io["g_ssd_norm"].rearrange("(k p) -> k p", p=P)),
            (dtb[:], row("dt_bias").broadcast_to([P, HEADS])),
            (nega[:], row("a_log").broadcast_to([P, HEADS])),
            (dsk[:], row("d_skip").broadcast_to([P, HEADS])),
            (nsink[:], row("sinks").broadcast_to([P, HEADS])),
        ]

        @block.sync
        def _(sp):
            sp.dma_start(xt(0), x_rows(0)).then_inc(x_full[0], 16)
            sp.dma_start(gpre[:], row("g_mix_pre").broadcast_to([P, D])).then_inc(gpre_in, 16)

            def load_x(t):
                if t < 9:
                    sp.wait_ge(S["hn_done"], ready(t - 3))
                else:
                    sp.wait_ge(S["hT_done"], ready(2 * (t - 2) + 1))
                    src = io["mem_prompt"][0, P * (t - 9):P * (t - 8), :]
                    sp.dma_start(hn[t % 2][:], src).then_inc(x_full[t % 3], 16)
                    return
                r = group_rows(t)
                sp.dma_start(xt(t)[0:r, :], x_rows(t)).then_inc(x_full[t % 3], 16)

            def load_panel(n):
                if n >= MEM0:
                    sp.wait_ge(S["lo_done"], ready(n - 3))
                    j = (n - MEM0) % KT
                    w = io["w_xk" if n - MEM0 < KT else "w_xv"][:, P * j:P * j + P].rearrange("(k p) n -> p k n", p=P)
                    for m in range(2):
                        sp.dma_start(raw[:, n % 3, 4 * m:4 * m + 4], w[:, 4 * m:4 * m + 4]).then_inc(raw_full[n % 3], 16)
                    return
                k = n % NPA - 1
                sp.wait_ge(S["lo_done"], ready(n - 3))
                if T_Q <= k < T_K:
                    j = k - T_Q
                    cols = [(C_Q + HD * j, HD), (C_Q + HD * (j + 4), HD)]
                else:
                    c = C_DT if k < 0 else C_XBC + P * k if k < T_Z else C_Z + P * (k - T_Z) if k < T_Q else \
                        C_K if k == T_K else C_V
                    for m in range(2):
                        sp.dma_start(raw[:, n % 3, 4 * m:4 * m + 4, :],
                                     io["w_in"][512 * m:512 * m + 512, c:c + P].rearrange("(k p) n -> p k n", p=P))\
                            .then_inc(raw_full[n % 3], 16)
                    return
                for m, (c, w) in enumerate(cols):
                    sp.dma_start(raw[:, n % 3, :, m * HD:m * HD + w],
                                 io["w_in"][:, c:c + w].rearrange("(k p) n -> p k n", p=P)).then_inc(raw_full[n % 3], 16)

            load_x(1)
            load_x(2)
            for g in range(3):
                for n in range(NPA * g, NPA * g + NPA):
                    if n == 2:
                        for dst, src in loads:
                            sp.dma_start(dst, src).then_inc(consts_in, 16)
                    if g < 2 and n in (NPA * g + 6, NPA * g + 8, NPA * g + 10):
                        load_x(3 * g + 3 + (n - NPA * g - 6) // 2)
                    load_panel(n)
                    if n == NPA * 2 + 4:
                        sp.wait_ge(S["hn_done"], ready(8))
                        sp.dma_start(gpre[:], row("g_mem").broadcast_to([P, D])).then_inc(gmem_in, 16)
                        load_x(9)
                        load_x(10)
            for n in range(MEM0, NPANELS_1):
                load_panel(n)
            for a, name, j0, j1 in ((0, "p_mem_k", 0, 8), (1, "p_mem_v", 0, 6), (1, "p_mem_v", 6, 8)):
                sp.wait_ge(S["evac_done"], ready(MEM0 + KT * a + j1 - 1))
                cols = slice(P * j0, P * j1)
                sp.dma_start(io[name][0, 0].rearrange("(m p) h d -> p m (h d)", p=P)[:, :, cols], mem_kv[:, a, :, cols])\
                    .then_inc(mem_stored, 16)
            sp.wait_ge(mem_stored, 48)

        @block.gpsimd
        def _(pool):
            credit(pool, "pool")
            k = 0
            for m, v in ((triu, 1.0), (slow, 1.0), (ones, 1.0), (band, 0.0), (mask, NEG), (mhalf, -0.5), (eps, EPS), (ident, 0.0),
                         (st, 0.0), (kv, 0.0), (vw, 0.0)):
                pool.memset(m[:], v).then_inc(consts_done, 1)
                k += 1
            for gb in range(2):
                pool.memset(proj[:, gb, 0:8, 0:3], 0.0).then_inc(consts_done, 1)
                k += 1
            pool.wait_ge(consts_done, k)
            pool.affine_select(out=triu[:], in_=triu[:], compare_op=ALU.is_ge, fill=0.0, base=0,
                               pattern=[[1, P]], channel_multiplier=-1).then_inc(consts_done, 1)
            pool.affine_select(out=slow[:], in_=slow[:], compare_op=ALU.is_gt, fill=0.0, base=0,
                               pattern=[[-1, P]], channel_multiplier=1).then_inc(consts_done, 1)
            pool.affine_select(out=ident[:], in_=ident[:], compare_op=ALU.not_equal, fill=1.0, base=0,
                               pattern=[[-1, P]], channel_multiplier=1).then_inc(consts_done, 1)
            pool.affine_select(out=band[:, 0:P], in_=band[:, 0:P], compare_op=ALU.is_gt, fill=NEG, base=0,
                               pattern=[[1, P]], channel_multiplier=-1).then_inc(consts_done, 1)
            pool.affine_select(out=band[:, P:], in_=band[:, P:], compare_op=ALU.is_ge, fill=NEG, base=0,
                               pattern=[[-1, P]], channel_multiplier=1).then_inc(consts_done, 1)
            k += 5
            pool.wait_ge(consts_done, k)
            pool.tensor_copy(mask[:, P:], band[:, P:]).then_inc(consts_done, 1)
            k += 1

            def norm(t):
                r = group_rows(t)
                pool.wait_ge(S["sumsq_done"], ready(t))
                pool.tensor_scalar(ms[0:r, t:t + 1], ss[0:r, t:t + 1], 1.0 / D, EPS, ALU.mult, ALU.add)\
                    .then_inc(S["mean_done"], 1)
                pool.wait_ge(S["mean_done"], ready(t))
                pool.tensor_tensor(rs[0:r, t:t + 1], ms[0:r, t:t + 1], mhalf[0:r, 0:1], ALU.pow)\
                    .then_inc(S["rstd_done"], 1)

            def chunk(g, i):
                c = 3 * g + i
                adt, decay = adts[g % 2], decays[g % 2]
                pool.wait_ge(S["seg_done"], ready(c - 1))
                pool.wait_ge(S["adt_done"], ready(g))
                for q in range(2):
                    pool.tensor_tensor(rr[:, 4 * q:4 * q + 4, :], bc(triu[:].rearrange("p (o n) -> p o n", o=1), [P, 4, P]),
                                       bc(adt[:, ds(i, 1), 4 * q:4 * q + 4].rearrange("p o (h u) -> p (o h) u", u=1), [P, 4, P]),
                                       ALU.mult).then_inc(S["rr_done"], 1)
                pool.wait_ge(S["xdt_done"], ready(c))
                pool.wait_ge(S["decay_done"], ready(g))
                pool.wait_ge(S["chst_done"], ready(c - 1))
                pool.tensor_tensor(xdd[:].rearrange("p (h d) -> p h d", h=HEADS), xdt[:].rearrange("p (h d) -> p h d", h=HEADS),
                                   bc(decay[:, 1, ds(8 * i, 8)].rearrange("p (h u) -> p h u", u=1), [P, HEADS, HD]),
                                   ALU.mult).then_inc(S["xdd_done"], 1)
                pool.wait_ge(S["xs_done"], ready(c))
                pool.wait_ge(S["t_y"], ready(c - 1))
                pool.tensor_tensor(yd[:].rearrange("p (h d) -> p h d", h=HEADS), xs[:].rearrange("p (h d) -> p h d", h=HEADS),
                                   bc(dsk[:].rearrange("p (h u) -> p h u", u=1), [P, HEADS, HD]), ALU.mult)\
                    .then_inc(S["yd_done"], 1)
                pool.wait_ge(S["yoff_done"], ready(c))
                pool.wait_ge(S["state_done"], ready(c - 1))
                pool.tensor_tensor(st[:].rearrange("p (h d) -> p h d", h=HEADS), st[:].rearrange("p (h d) -> p h d", h=HEADS),
                                   bc(decay[:, 2, ds(8 * i, 8)].rearrange("p (h u) -> p h u", u=1), [P, HEADS, HD]),
                                   ALU.mult).then_inc(S["sdec_done"], 1)
                pool.wait_ge(S["usq_done"], ready(2 * c + 1))
                pool.tensor_tensor(rsu[:], ssu[:], eps[:, 0:2], ALU.add).then_inc(S["um_done"], 1)
                pool.wait_ge(S["um_done"], ready(c))
                pool.tensor_tensor(rsu[:], rsu[:], mhalf[:, 0:2], ALU.pow).then_inc(S["ur_done"], 1)

            for t in range(3):
                norm(t)
            for ph in range(4):
                g = ph - 1
                if g >= 0:
                    if g < 2:
                        pool.wait_ge(S["evac_done"], ready(NPA * g + 1 + T_XBC + 7))
                        pool.wait_ge(consts_done, k)
                        pool.tensor_copy(proj[:, (g + 1) % 2, 0:8, 0:3], proj[:, g % 2, 0:8, 384:387]).then_inc(S["halo_done"], 1)
                    with pool.Fori(0, 2 if g < 2 else 1) as i:
                        chunk(g, i)
                if g >= 0:
                    chunk(g, 2 if g < 2 else 1)
                if ph < 3:
                    for t in range(3 * ph + 3, 3 * ph + (6 if ph < 2 else 5)):
                        norm(t)

        @block.scalar
        def _(act):
            credit(act, "act")
            def split_hi(n, s3, s2, w3):
                act.wait_ge(raw_full[s3], w3)
                act.wait_ge(S["panel_done"], ready(n - 2))
                act.activation(w_hi[:, s2], raw[:, s3], ACT.Copy).then_inc(S["hi_done"], 1)

            def evac(n, g, k, s2):
                w = GW[g]
                act.wait_ge(S["panel_done"], ready(n))
                act.activation(proj[:, g % 2, ds(k, 1), 3:3 + w], bank[s2][:, 0:w].rearrange("p (o n) -> p o n", o=1),
                               ACT.Copy).then_inc(S["evac_done"], 1)

            def norm(t):
                r = group_rows(t)
                act.wait_ge(x_full[t % 3], 16 * (t // 3 + 1))
                act.wait_ge(S["sumsq_done"], ready(t - 1))
                act.activation(square_out[0:r, :], x_in(t)[0:r, :], ACT.Square, accum_out=ss[0:r, t:t + 1])\
                    .then_inc(S["sumsq_done"], 1)

            def norm_evac(t):
                r, g = group_rows(t), t // 3
                c0 = 128 * (t % 3)
                for h in range(2):
                    act.wait_ge(S["hT_done"], ready(2 * t + h))
                    act.wait_ge(S["panel_done"], ready(NPA * g - 1))
                    act.activation(h_hi[:, 4 * h:4 * h + 4, c0:c0 + r],
                                   bank[2 + h][:, 0:4 * r].rearrange("p (k n) -> p k n", k=4), ACT.Copy)\
                        .then_inc(S["hhi_done"], 1)

            def dt_part(g, step):
                cols = 24 if g < 2 else 16
                if step == 0:
                    act.wait_ge(S["dt_steps"], ready(6 * g + 1))
                    act.activation(de[:, 0:cols], dna[:, 0:cols], ACT.Exp).then_inc(S["dt_exp"], 1)
                elif step == 1:
                    act.wait_ge(S["dt_steps"], ready(6 * g + 2))
                    act.activation(dl[:, 0:cols], du[:, 0:cols], ACT.Ln).then_inc(S["dt_ln"], 1)
                else:
                    act.wait_ge(S["cum_done"], ready(g))
                    act.wait_ge(S["t_yoff"], ready(3 * g - 4))
                    act.wait_ge(S["sdec_done"], ready(3 * g - 4))
                    act.activation(decays[g % 2][:, :, 0:cols], bank[7][:, 32:32 + 3 * cols].rearrange("p (a n) -> p a n", a=3),
                                   ACT.Exp).then_inc(S["decay_done"], 1)

            def conv0(g, i, where, j0):
                c, b, off = 3 * g + i, g % 2, 128 * i
                for j in range(j0, j0 + 4):
                    act.wait_ge(S["xc_done"], ready(c - 1))
                    act.activation(conv_place(where)[0][:, j:j + 1, :], proj[:, b, j:j + 1, ds(off, P)], ACT.Identity,
                                   bias=convb[:, j:j + 1], scale=convw[:, 0, j:j + 1]).then_inc(S["conv0_done"], 1)

            def gates(g, i):
                c, b, off = 3 * g + i, g % 2, 128 * i
                act.wait_ge(S["zs_done"], ready(c - 1))
                act.activation(tz[:], proj[:, b, T_Z:T_Z + 4, ds(off + 3, P)], ACT.Tanh, scale=0.5).then_inc(S["tanhz_done"], 1)

            def conv_tanh(g, i, where):
                c = 3 * g + i
                act.wait_ge(S["conv_done"], ready(6 * c + 5))
                acc, tc_ = conv_place(where)
                act.activation(tc_, acc, ACT.Tanh).then_inc(S["tanhc_done"], 1)

            def queries(g, i):
                c, b, off = 3 * g + i, g % 2, 128 * i
                act.wait_ge(S["sc_done"], ready(2 * c - 1))
                act.activation(qs[:], proj[:, b, T_Q:T_Q + 4, ds(off + 3, P)], ACT.Copy, scale=0.125).then_inc(S["qs_done"], 1)
                act.wait_ge(S["k_shift"], ready(c))
                act.wait_ge(S["t1_done"], ready(c - 1))
                act.activation(kv[:, 1:3, :], proj[:, b, T_K:T_K + 2, ds(off + 3, P)], ACT.Copy).then_inc(S["kv_done"], 1)

            def elt1(g, i):
                c = 3 * g + i
                act.wait_ge(S["t1_done"], ready(c))
                act.wait_ge(S["t_y"], ready(c - 1))
                act.activation(xs[:], bank[2][:], ACT.Copy).then_inc(S["xs_done"], 1)
                act.wait_ge(S["chst_done"], ready(c - 1))
                act.activation(bt[:], bank[3][:, 0:256].rearrange("p (a n) -> p a n", a=2), ACT.Copy).then_inc(S["bt_done"], 1)
                act.wait_ge(S["vshift_done"], ready(c))
                act.activation(vw[:, 1, :], bank[3][:, 256:384], ACT.Copy).then_inc(S["vw_done"], 1)
                for q in range(2):
                    act.wait_ge(S["seg_done"], ready(c))
                    act.wait_ge(S["ydiag_done"], ready(c - 1))
                    act.activation(mm[:, 4 * q:4 * q + 4, :], bank[5 + q][:].rearrange("p (h n) -> p h n", h=4), ACT.Exp)\
                        .then_inc(S["exp_done"], 1)

            def softmax(g, i, r):
                c = 3 * g + i
                act.wait_ge(S["nb_done"], ready(2 * c + r))
                for h in range(4):
                    q = 4 * r + h
                    act.activation(sc[:, h, :], sc[:, h, :], ACT.Exp, bias=nb_[:, q:q + 1], accum_out=rsum[:, q:q + 1])\
                        .then_inc(S["p_done"], 1)
                act.wait_ge(S["sd_done"], ready(2 * c + r))
                act.activation(es[:, 4 * r:4 * r + 4], sd[:, 4 * r:4 * r + 4], ACT.Exp).then_inc(S["es_done"], 1)

            def elt2(g, i):
                c = 3 * g + i
                act.wait_ge(S["u_done"], ready(c))
                for q in range(2):
                    act.wait_ge(S["unT_done"], ready(c - 1))
                    act.activation(un[:, 256 * q:256 * q + 256], yt[:, 256 * q:256 * q + 256], ACT.Square,
                                   scale=1.0 / 16, accum_out=ssu[:, q:q + 1]).then_inc(S["usq_done"], 1)

            def evac_pt(g, i, r):
                c = 3 * g + i
                act.wait_ge(S["pT_done"], ready(4 * c + 2 * r))
                act.wait_ge(S["pv_done"], ready(2 * c + r - 1))
                act.activation(pt[:, 0:4, :], bank[2][:].rearrange("p (h n) -> p h n", h=4), ACT.Copy).then_inc(S["pTa_done"], 1)

            def mix_ssd(g, i):
                c = 3 * g + i
                act.wait_ge(S["unT_done"], ready(c))
                for j in range(4):
                    act.activation(mixT(g)[:, j:j + 1, ds(128 * i, P)], bank[3][:, 128 * j:128 * j + 128].rearrange("p (o n) -> p o n", o=1),
                                   ACT.Copy, scale=gssd[:, j:j + 1]).then_inc(S["mixs_done"], 1)

            def mix_att(g, i):
                c = 3 * g + i
                act.wait_ge(S["attT_done"], ready(c))
                act.activation(mixT(g)[:, 4:8, ds(128 * i, P)], bank[3][:].rearrange("p (o n) -> p o n", o=4), ACT.Copy)\
                    .then_inc(S["mixa_done"], 1)

            def mem_evac(n):
                if (n - MEM0) % 2 == 0:
                    return
                hi_ahead(n - 1)
                hi_ahead(n)
                act.wait_ge(S["panel_done"], ready(n))
                for q in (n - 1, n):
                    a, j = (q - MEM0) // KT, (q - MEM0) % KT
                    for t in range(2):
                        ins = act.activation(mem_kv[:, a, t, P * j:P * j + P], bank[t][:, P * (q % 2):P * (q % 2) + P], ACT.Copy)
                    ins.then_inc(S["evac_done"], 1)

            def hi_ahead(n, i=0):
                m = n + 2
                if m < NPANELS_1:
                    split_hi(m + 6 * i, m % 3, m % 2, 32 * (m // 3 + 1) + 64 * i)

            def slots(gp, gb, i, last):
                for k in range(6):
                    if gp < 3:
                        n = NPA * gp + 1 + k
                        if last:
                            hi_ahead(n + 6 * i)
                        else:
                            hi_ahead(n, i)
                        evac(n + 6 * i, gp, 6 * i + k, n % 2)
                    else:
                        mem_evac(MEM0 + 6 * i + k)
                    if last and gp < 3:
                        if k < 2 or k == 2 and gb < 0:
                            dt_part(gp, k)
                        if k >= 3 and (gp < 2 or k < 5):
                            norm(3 * gp + k)
                    nxt = (gb + 1, 0) if last else (gb, i + 1)
                    prep = nxt if not last or gp < 3 else None
                    where = min(max(gb, 0), 2)
                    if k == 0 and gb >= 0:
                        softmax(gb, i, 0)
                    elif k == 1 and gb >= 0:
                        elt1(gb, i)
                    elif k == 2 and gb >= 0:
                        evac_pt(gb, i, 0)
                        if last and gp < 3:
                            dt_part(gp, 2)
                        softmax(gb, i, 1)
                    if prep and (gb >= 0 or last) and k in (0, 2):
                        conv0(*prep, where, 2 * k)
                    if k < 4:
                        pass
                    elif k == 4:
                        if gb >= 0:
                            evac_pt(gb, i, 1)
                        if prep and (gb >= 0 or last):
                            gates(*prep)
                        if gb >= 0:
                            elt2(gb, i)
                    else:
                        if gb >= 0:
                            mix_ssd(gb, i)
                        if prep and (gb >= 0 or last):
                            conv_tanh(*prep, where)
                        if gb >= 0:
                            mix_att(gb, i)
                        if prep and (gb >= 0 or last):
                            queries(*prep)

            for t in range(3):
                norm(t)
            norm_evac(0)
            split_hi(0, 0, 0, 32)
            norm_evac(1)
            split_hi(1, 1, 1, 32)
            norm_evac(2)
            act.wait_ge(consts_in, 16 * len(loads))
            act.wait_ge(consts_done, 19)
            act.wait_ge(S["consts_T"], ready(0))
            act.activation(convw[:].rearrange("p t k -> p (t k)"), bank[7][:, 0:32], ACT.Copy, scale=0.5).then_inc(S["cols_done"], 1)
            act.activation(convb[:], bank[7][:, 32:40], ACT.Copy, scale=0.5).then_inc(S["cols_done"], 1)
            act.activation(gssd[:], bank[7][:, 40:44], ACT.Copy).then_inc(S["cols_done"], 1)
            act.activation(dna[:, 0:8], nega[:], ACT.Exp).then_inc(S["cols_done"], 1)
            act.activation(dna[:, 8:16], nsink[:], ACT.Copy, scale=-1.0).then_inc(S["cols_done"], 1)
            act.wait_ge(S["cols_done"], ready(4))
            act.activation(nega[:], dna[:, 0:8], ACT.Copy, scale=-1.0).then_inc(S["cols_done"], 1)
            act.activation(nsink[:].rearrange("p (j v) -> p j v", v=2), dna[:, 8:16].rearrange("p (v j) -> p j v", v=2), ACT.Copy).then_inc(S["cols_done"], 1)
            act.wait_ge(S["cols_done"], ready(6))
            for ph in range(4):
                gp, gb = ph, ph - 1
                if gp < 3:
                    n = NPA * gp
                    act.wait_ge(S["panel_done"], ready(n))
                    act.wait_ge(S["dtT_done"], ready(gp - 1))
                    act.activation(dtr[:, 0:GW[gp]], bank[n % 2][0:HEADS, 0:GW[gp]], ACT.Copy).then_inc(S["evac_done"], 1)
                    hi_ahead(n)
                if gp < 3:
                    with act.Fori(0, 2) as i:
                        slots(gp, gb, i, False)
                    slots(gp, gb, 2, True)
                    for t in range(3 * gp + 3, 3 * gp + (6 if gp < 2 else 5)):
                        norm_evac(t)
                else:
                    slots(gp, gb, 0, False)
                    slots(gp, gb, 1, True)
                    for n in range(MEM0 + 12, NPANELS_1):
                        mem_evac(n)

        @block.vector
        def _(dve):
            credit(dve, "dve")
            dve.wait_ge(gpre_in, 16)

            def split_lo(n, s3, s2):
                dve.wait_ge(S["hi_done"], ready(n))
                dve.tensor_tensor(w_lo[:, s2], raw[:, s3], w_hi[:, s2].bitcast(F32), ALU.subtract).then_inc(S["lo_done"], 1)

            def norm(t):
                r = group_rows(t)
                dve.wait_ge(S["rstd_done"], ready(t))
                dve.wait_ge(S["hT_done"], ready(2 * t - 3))
                if t >= 9:
                    dve.wait_ge(gmem_in, 16)
                    dve.wait_ge(x_full[t % 3], 16 * (t // 3 + 1))
                dve.scalar_tensor_tensor(hn[t % 2][0:r, :], x_in(t)[0:r, :], rs[0:r, t:t + 1], gpre[0:r, :], ALU.mult, ALU.mult)\
                    .then_inc(S["hn_done"], 1)

            def norm_evac(t):
                r = group_rows(t)
                c0 = 128 * (t % 3)
                for h in range(2):
                    dve.wait_ge(S["hhi_done"], ready(2 * t + h))
                    dve.tensor_tensor(h_lo[:, 4 * h:4 * h + 4, c0:c0 + r],
                                      bank[2 + h][:, 0:4 * r].rearrange("p (k n) -> p k n", k=4),
                                      h_hi[:, 4 * h:4 * h + 4, c0:c0 + r].bitcast(F32), ALU.subtract).then_inc(S["hlo_done"], 1)

            def dt_part(d, step):
                rows, chunks = P, 3 if d < 2 else 2
                cols = 8 * chunks
                dt, adt = dts[d % 2], adts[d % 2]
                v = lambda a: a[0:rows, 0:cols]
                v3 = lambda a: a[0:rows, 0:cols].rearrange("p (a n) -> p a n", n=8)
                if step == 0:
                    dve.wait_ge(S["dtT_done"], ready(d))
                    dve.wait_ge(S["adt_done"], ready(d - 1))
                    dve.tensor_tensor(v3(dx), v3(bank[7]), bc(dtb[0:rows, :].rearrange("p (o n) -> p o n", o=1), [rows, chunks, 8]),
                                      ALU.add).then_inc(S["dt_steps"], 1)
                    dve.wait_ge(S["dt_steps"], ready(6 * d))
                    dve.scalar_tensor_tensor(v(dna), v(dx), -1.0, v(dx), ALU.mult, ALU.min).then_inc(S["dt_steps"], 1)
                elif step == 1:
                    dve.wait_ge(S["dt_exp"], ready(d))
                    dve.tensor_scalar(v(du), v(de), 1.0, None, ALU.add).then_inc(S["dt_steps"], 1)
                    dve.wait_ge(S["dt_steps"], ready(6 * d + 2))
                    dve.tensor_scalar(v(dv), v(du), -1.0, 1e-30, ALU.add, ALU.max).then_inc(S["dt_steps"], 1)
                    dve.wait_ge(S["dt_steps"], ready(6 * d + 3))
                    dve.reciprocal(v(dw), v(dv)).then_inc(S["dt_steps"], 1)
                    dve.wait_ge(S["dt_steps"], ready(6 * d + 4))
                    dve.tensor_tensor(v(dw), v(dw), v(de), ALU.mult).then_inc(S["dt_steps"], 1)
                else:
                    dve.wait_ge(S["dt_steps"], ready(6 * d + 5))
                    dve.wait_ge(S["dt_ln"], ready(d))
                    dve.tensor_tensor(v(dl), v(dl), v(dw), ALU.mult).then_inc(S["dt_steps2"], 1)
                    dve.scalar_tensor_tensor(v(dv), v(dv), 1e-30, v(de), ALU.is_equal, ALU.mult).then_inc(S["dt_steps2"], 1)
                    dve.wait_ge(S["dt_steps2"], ready(4 * d + 1))
                    dve.tensor_tensor(v(dl), v(dl), v(dv), ALU.add).then_inc(S["dt_steps2"], 1)
                    dve.wait_ge(S["dt_steps2"], ready(4 * d + 2))
                    dve.wait_ge(S["xdt_done"], ready(3 * d - 4))
                    dve.wait_ge(S["rr_done"], ready(2 * (3 * d - 4) + 1))
                    dve.scalar_tensor_tensor(dt[0:rows, 0:chunks, :], v3(dx), 0.0, v3(dl), ALU.max, ALU.add)\
                        .then_inc(S["dt_steps2"], 1)
                    dve.wait_ge(S["dt_steps2"], ready(4 * d + 3))
                    dve.tensor_tensor(adt[0:rows, 0:chunks, :], dt[0:rows, 0:chunks, :],
                                      bc(nega[0:rows, :].rearrange("p (o n) -> p o n", o=1), [rows, chunks, 8]), ALU.mult)\
                        .then_inc(S["adt_done"], 1)

            def conv_tap(g, i, where, tap):
                c, b = 3 * g + i, g % 2
                acc, tc_ = conv_place(where)
                n = 6 * c + 2 * (tap - 1)
                dve.wait_ge(S["conv0_done"], ready(8 * c + 7))
                dve.wait_ge(S["conv_done"], ready(n - 1))
                dve.tensor_tensor(tc_, proj[:, b, 0:8, ds(128 * i + tap, P)],
                                  bc(convw[:, tap, :].rearrange("p (k u) -> p k u", u=1), [P, 8, P]), ALU.mult).then_inc(S["conv_done"], 1)
                dve.wait_ge(S["conv_done"], ready(n))
                dve.tensor_tensor(acc, acc, tc_, ALU.add).then_inc(S["conv_done"], 1)

            def gates(g, i):
                c, b = 3 * g + i, g % 2
                dve.wait_ge(S["tanhz_done"], ready(c))
                dve.wait_ge(S["zT_done"], ready(c - 1))
                dve.scalar_tensor_tensor(zs[:], tz[:], 1.0, proj[:, b, T_Z:T_Z + 4, ds(128 * i + 3, P)], ALU.add, ALU.mult)\
                    .then_inc(S["zs_done"], 1)

            def shift_keys(c):
                dve.wait_ge(S["sc_done"], ready(2 * c - 1))
                dve.tensor_copy(kv[:, 0, :], kv[:, 1, :]).then_inc(S["k_shift"], 1)

            def shift_values(c):
                dve.wait_ge(S["pv_done"], ready(2 * c - 1))
                dve.wait_ge(S["vw_done"], ready(c - 1))
                dve.tensor_copy(vw[:, 0, :], vw[:, 1, :]).then_inc(S["vshift_done"], 1)

            def silu_xc(g, i, where):
                c = 3 * g + i
                acc, tc_ = conv_place(where)
                dve.wait_ge(S["tanhc_done"], ready(c))
                dve.wait_ge(S["yoff_done"], ready(c - 1))
                dve.scalar_tensor_tensor(xc[:], tc_, 1.0, acc, ALU.add, ALU.mult).then_inc(S["xc_done"], 1)

            h3 = lambda a: a.rearrange("p (h d) -> p h d", d=HD)

            def per_head(a):
                return bc(a.rearrange("p (h u) -> p h u", u=1), [P, HEADS, HD])

            def elt1(g, i):
                c = 3 * g + i
                dve.wait_ge(S["xs_done"], ready(c))
                dve.wait_ge(S["ydiag_done"], ready(c - 1))
                dve.wait_ge(S["xdd_done"], ready(c - 1))
                dve.tensor_tensor(h3(xdt[:]), h3(xs[:]), bc(dts[g % 2][:, ds(i, 1), :].rearrange("p o (h u) -> p (o h) u", u=1),
                                                                 [P, HEADS, HD]), ALU.mult).then_inc(S["xdt_done"], 1)
                dve.wait_ge(S["cb_done"], ready(c))
                dve.wait_ge(S["mm_done"], ready(2 * c - 1))
                dve.tensor_tensor(cbm[:], bank[4][:, 0:256].rearrange("p (a n) -> p a n", a=2),
                                  bc(triu[:].rearrange("p (o n) -> p o n", o=1), [P, 2, P]), ALU.mult).then_inc(S["cbm_done"], 1)
                for q in range(2):
                    dve.wait_ge(S["exp_done"], ready(2 * c + q))
                    dve.wait_ge(S["cbm_done"], ready(c))
                    dve.tensor_tensor(mm[:, 4 * q:4 * q + 4, :], mm[:, 4 * q:4 * q + 4, :], bc(cbm[:, q:q + 1, :], [P, 4, P]),
                                      ALU.mult).then_inc(S["mm_done"], 1)

            def scores(g, i, r):
                c = 3 * g + i
                dve.wait_ge(S["sc_done"], ready(2 * c + r))
                dve.wait_ge(S["mask_done"], ready(c - 1))
                dve.wait_ge(S["pT_done"], ready(4 * c + 2 * r - 1))
                dve.sem_inc(S["scores_open"], 1)
                for h in range(4):
                    q = 4 * r + h
                    dve.tensor_tensor_reduce(sc[:, h, :], bank[5 + h % 2][:, 256 * (h // 2):256 * (h // 2) + 256], mask[:],
                                             1.0, -3.0e38, ALU.add, ALU.max, mx[:, q:q + 1]).then_inc(S["msk_done"], 1)
                dve.wait_ge(S["msk_done"], ready(8 * c + 4 * r + 3))
                dve.scalar_tensor_tensor(nb_[:, 4 * r:4 * r + 4], mx[:, 4 * r:4 * r + 4], -1.0, nsink[:, 4 * r:4 * r + 4],
                                         ALU.mult, ALU.min).then_inc(S["nb_done"], 1)
                dve.wait_ge(S["nb_done"], ready(2 * c + r))
                dve.tensor_tensor(sd[:, 4 * r:4 * r + 4], nb_[:, 4 * r:4 * r + 4], nsink[:, 4 * r:4 * r + 4], ALU.subtract)\
                    .then_inc(S["sd_done"], 1)
                if r == 1:
                    dve.tensor_copy(mask[:, 0:P], band[:, 0:P]).then_inc(S["mask_done"], 1)

            def denominators(g, i, r):
                c = 3 * g + i
                dve.wait_ge(S["es_done"], ready(2 * c + r))
                dve.wait_ge(S["p_done"], ready(8 * c + 4 * r + 3))
                dve.tensor_tensor(den[:, 4 * r:4 * r + 4], es[:, 4 * r:4 * r + 4], rsum[:, 4 * r:4 * r + 4], ALU.add)\
                    .then_inc(S["den_done"], 1)
                dve.wait_ge(S["den_done"], ready(2 * c + r))
                dve.wait_ge(S["att_done"], ready(2 * c + r - 2))
                dve.reciprocal(ri[:, 4 * r:4 * r + 4], den[:, 4 * r:4 * r + 4]).then_inc(S["ri_done"], 1)

            def y_off(g, i):
                c = 3 * g + i
                dve.wait_ge(S["yoff_done"], ready(c))
                dve.wait_ge(S["un_done"], ready(2 * c - 1))
                dve.tensor_tensor(h3(yt[:]), h3(bank[4][:]), per_head(decays[g % 2][:, 0, ds(8 * i, 8)]), ALU.mult)\
                    .then_inc(S["t_yoff"], 1)

            def y_sum(g, i):
                c = 3 * g + i
                dve.wait_ge(S["ydiag_done"], ready(c))
                dve.wait_ge(S["t_yoff"], ready(c))
                dve.tensor_tensor(yt[:], bank[7][:], yt[:], ALU.add).then_inc(S["t_ydiag"], 1)
                dve.wait_ge(S["yd_done"], ready(c))
                dve.wait_ge(S["t_ydiag"], ready(c))
                dve.tensor_tensor(yt[:], yt[:], yd[:], ALU.add).then_inc(S["t_y"], 1)
                dve.wait_ge(S["zT_done"], ready(c))
                dve.wait_ge(S["t_y"], ready(c))
                dve.scalar_tensor_tensor(yt[:], bank[3][:], 0.5, yt[:], ALU.mult, ALU.mult).then_inc(S["u_done"], 1)

            def next_state(g, i):
                c = 3 * g + i
                dve.wait_ge(S["chst_done"], ready(c))
                dve.wait_ge(S["sdec_done"], ready(c))
                dve.tensor_tensor(st[:], bank[2][:], st[:], ALU.add).then_inc(S["state_done"], 1)

            def normed_u(g, i):
                c = 3 * g + i
                dve.wait_ge(S["ur_done"], ready(c))
                for q in range(2):
                    dve.tensor_scalar(un[:, 256 * q:256 * q + 256], yt[:, 256 * q:256 * q + 256], rsu[:, q:q + 1], None, ALU.mult)\
                        .then_inc(S["un_done"], 1)

            def evac_pt(g, i, r):
                c = 3 * g + i
                dve.wait_ge(S["pT_done"], ready(4 * c + 2 * r + 1))
                dve.wait_ge(S["pv_done"], ready(2 * c + r - 1))
                dve.tensor_copy(pt[:, 4:8, :], bank[4][:].rearrange("p (h n) -> p h n", h=4)).then_inc(S["pTv_done"], 1)

            def attended(g, i, r):
                c = 3 * g + i
                dve.wait_ge(S["pv_done"], ready(2 * c + r))
                dve.wait_ge(S["ri_done"], ready(2 * c + r))
                dve.wait_ge(S["attT_done"], ready(c - 1))
                dve.tensor_tensor(att[:, 2 * r:2 * r + 2].rearrange("p j v d -> p (j v) d"),
                                  bank[7][:, 256 * r:256 * r + 256].rearrange("p (h d) -> p h d", d=HD),
                                  bc(ri[:, 4 * r:4 * r + 4].rearrange("p (h u) -> p h u", u=1), [P, 4, HD]), ALU.mult)\
                    .then_inc(S["att_done"], 1)

            def mem_lo(n):
                if (n - MEM0) % 2:
                    lo_ahead(n - 1)
                    lo_ahead(n)

            def lo_ahead(n, i=0):
                m = n + 2
                if m < NPANELS_1:
                    split_lo(m + 6 * i, m % 3, m % 2)

            def slots(gp, gb, i, last):
                nxt = (gb + 1, 0) if last else (gb, i + 1)
                prep = nxt if last and gp < 3 or not last and gb >= 0 else None
                where = min(max(gb, 0), 2)
                for k in range(6):
                    if gp < 3:
                        n = NPA * gp + 1 + k
                        if last:
                            lo_ahead(n + 6 * i)
                        else:
                            lo_ahead(n, i)
                    else:
                        mem_lo(MEM0 + 6 * i + k)
                    if last and gp < 3 and k < 3:
                        dt_part(gp, k)
                    if gb >= 0:
                        if k == 0:
                            scores(gb, i, 0)
                        elif k == 1:
                            shift_values(3 * gb + i)
                            elt1(gb, i)
                            denominators(gb, i, 0)
                        elif k == 2:
                            evac_pt(gb, i, 0)
                            scores(gb, i, 1)
                        elif k == 3:
                            y_off(gb, i)
                            attended(gb, i, 0)
                            denominators(gb, i, 1)
                        elif k == 4:
                            evac_pt(gb, i, 1)
                            y_sum(gb, i)
                        elif k == 5:
                            next_state(gb, i)
                            attended(gb, i, 1)
                    if last and gp < 3 and k == 5:
                        norm(3 * gp + 3)
                        norm(3 * gp + 4)
                    if prep:
                        if 2 <= k < 5:
                            conv_tap(*prep, where, k - 1)
                    if k == 4 and gb >= 0:
                        normed_u(gb, i)
                    if prep:
                        if k == 5:
                            silu_xc(*prep, where)
                            gates(*prep)
                            shift_keys(3 * prep[0] + prep[1])

            norm(0)
            norm(1)
            norm_evac(0)
            split_lo(0, 0, 0)
            norm(2)
            norm_evac(1)
            split_lo(1, 1, 1)
            norm_evac(2)
            dve.wait_ge(consts_in, 16 * len(loads))
            dve.wait_ge(consts_done, 19)
            dve.wait_ge(S["cols_done"], ready(6))
            for ph in range(4):
                gp, gb = ph, ph - 1
                if gp < 3:
                    lo_ahead(NPA * gp)
                if gp < 3:
                    with dve.Fori(0, 2) as i:
                        slots(gp, gb, i, False)
                    slots(gp, gb, 2, True)
                else:
                    slots(gp, gb, 0, False)
                    slots(gp, gb, 1, True)
                    for n in range(MEM0 + 12, NPANELS_1):
                        mem_lo(n)
                if gp < 2:
                    t = 3 * gp + 3
                    norm_evac(t)
                    norm(t + 2)
                    norm_evac(t + 1)
                    norm_evac(t + 2)
                elif gp == 2:
                    norm_evac(9)
                    norm_evac(10)

        @block.tensor
        def _(pe):
            credit(pe, "pe")
            pe.wait_ge(consts_done, 19)

            def panel(n, s2, w):
                pe.wait_ge(S["lo_done"], ready(n))
                pe.wait_ge(S["evac_done"], ready(n - 2))
                for k in range(KT):
                    for m, (a, b) in enumerate(((w_hi, h_hi), (w_hi, h_lo), (w_lo, h_hi))):
                        mm_ = pe.matmul(bank[s2][:, 0:w], a[:, s2, k, :], b[:, k, 0:w],
                                        start=(k == 0 and m == 0), stop=(k == KT - 1 and m == 2))
                mm_.then_inc(S["panel_done"], 1)

            def norm(t):
                r = group_rows(t)
                cl = 3 * (t // 3) - 4
                pe.wait_ge(S["hn_done"], ready(t))
                for h in range(2):
                    pe.wait_ge(S["hlo_done"], ready(2 * t + h - 2))
                    pe.wait_ge(S["mixa_done" if h else "state_done"], ready(cl))
                    for k in range(4):
                        mm_ = pe.transpose(bank[2 + h][:, r * k:r * k + r], hn[t % 2][0:r, P * (4 * h + k):P * (4 * h + k + 1)],
                                           ident[0:r, 0:r])
                    mm_.then_inc(S["hT_done"], 1)

            def dt_transposed(g, c):
                n = 3 if g < 2 else 2
                pe.wait_ge(S["evac_done"], ready(NPA * g))
                pe.wait_ge(S["cols_done"], ready(2))
                pe.wait_ge(S["att_done"], ready(2 * c - 1))
                for u in range(n):
                    mm_ = pe.transpose(bank[7][:, 8 * u:8 * u + 8], dtr[:, P * u:P * u + P], ident[0:8, 0:8])
                mm_.then_inc(S["dtT_done"], 1)

            def dt_sums(g):
                n = 3 if g < 2 else 2
                pe.wait_ge(S["adt_done"], ready(g))
                for m, lhs in enumerate((triu, slow, ones)):
                    mm_ = pe.matmul(bank[7][:, 32 + 8 * n * m:32 + 8 * n * (m + 1)], lhs[:],
                                    adts[g % 2][:, 0:n, :].rearrange("p a n -> p (a n)"), start=True, stop=True)
                mm_.then_inc(S["cum_done"], 1)

            def part1(g, i):
                c = 3 * g + i
                pe.wait_ge(S["xc_done"], ready(c))
                pe.wait_ge(S["state_done"], ready(c - 1))
                for j in range(4):
                    pe.transpose(bank[2][:, P * j:P * j + P], xc[:, j, :], ident[:])
                pe.wait_ge(S["mixa_done"], ready(c - 1))
                for j in range(2):
                    pe.transpose(bank[3][:, P * j:P * j + P], xc[:, 4 + j, :], ident[:])
                pe.wait_ge(S["kv_done"], ready(c))
                pe.transpose(bank[3][:, 256:384], vs, ident[:]).then_inc(S["t1_done"], 1)
                pe.wait_ge(S["pTv_done"], ready(2 * c - 1))
                for q in range(2):
                    mm_ = pe.matmul(bank[4][:, P * q:P * q + P], xc[:, 4 + q, :], xc[:, 6 + q, :], start=True, stop=True)
                mm_.then_inc(S["cb_done"], 1)
                pe.wait_ge(S["msk_done"], ready(8 * c + 3))
                pe.wait_ge(S["rr_done"], ready(2 * c + 1))
                for q in range(2):
                    mm_ = pe.matmul(bank[5 + q][:], slow[:], rr[:, 4 * q:4 * q + 4, :].rearrange("p h n -> p (h n)"),
                                    start=True, stop=True)
                mm_.then_inc(S["seg_done"], 1)

            def scores(c, r):
                for h in range(4):
                    j, v = 2 * r + h // 2, h % 2
                    mm_ = pe.matmul(bank[5 + h % 2][:, 256 * (h // 2):256 * (h // 2) + 256], qs[HD * v:HD * v + HD, j, :],
                                    kw[HD * v:HD * v + HD, :], start=True, stop=True)
                mm_.then_inc(S["sc_done"], 1)

            def gates(c):
                pe.wait_ge(S["zs_done"], ready(c))
                pe.wait_ge(S["bt_done"], ready(c))
                pe.wait_ge(S["vw_done"], ready(c))
                for j in range(4):
                    mm_ = pe.transpose(bank[3][:, P * j:P * j + P], zs[:, j, :], ident[:])
                mm_.then_inc(S["zT_done"], 1)

            def y_off(c):
                pe.wait_ge(S["pTv_done"], ready(2 * c))
                pe.wait_ge(S["state_done"], ready(c - 1))
                for q in range(2):
                    mm_ = pe.matmul(bank[4][:, 256 * q:256 * q + 256], xc[:, 6 + q, :], st[:, 256 * q:256 * q + 256],
                                    start=True, stop=True)
                mm_.then_inc(S["yoff_done"], 1)

            def y_diag(c):
                pe.wait_ge(S["mm_done"], ready(2 * c + 1))
                pe.wait_ge(S["att_done"], ready(2 * c))
                for h in range(HEADS):
                    mm_ = pe.matmul(bank[7][:, HD * h:HD * h + HD], mm[:, h, :], xdt[:, HD * h:HD * h + HD],
                                    start=True, stop=True)
                mm_.then_inc(S["ydiag_done"], 1)

            def chunk_state(c):
                pe.wait_ge(S["xdd_done"], ready(c))
                pe.wait_ge(S["pTa_done"], ready(2 * c + 1))
                for q in range(2):
                    mm_ = pe.matmul(bank[2][:, 256 * q:256 * q + 256], bt[:, q, :], xdd[:, 256 * q:256 * q + 256],
                                    start=True, stop=True)
                mm_.then_inc(S["chst_done"], 1)

            def p_transposed(c, r):
                pe.wait_ge(S["p_done"], ready(8 * c + 4 * r + 3))
                pe.wait_ge(*((S["pTa_done"], ready(2 * c)) if r else (S["xs_done"], ready(c))))
                for q in range(4):
                    mm_ = pe.transpose(bank[2][:, P * q:P * q + P], sc[:, q // 2, P * (q % 2):P * (q % 2) + P], ident[:])
                mm_.then_inc(S["pT_done"], 1)
                pe.wait_ge(*((S["t_yoff"], ready(c)) if r else (S["cbm_done"], ready(c))))
                for q in range(4):
                    mm_ = pe.transpose(bank[4][:, P * q:P * q + P], sc[:, 2 + q // 2, P * (q % 2):P * (q % 2) + P], ident[:])
                mm_.then_inc(S["pT_done"], 1)

            def values(c, r):
                pe.wait_ge(S["pTa_done"], ready(2 * c + r))
                pe.wait_ge(S["pTv_done"], ready(2 * c + r))
                pe.wait_ge(*((S["t_ydiag"], ready(c)) if r else (S["att_done"], ready(2 * c - 1))))
                for h in range(4):
                    for m in range(2):
                        mm_ = pe.matmul(bank[7][:, 256 * r + HD * h:256 * r + HD * h + HD], pt[:, 2 * h + m, :],
                                        vw[:, m, HD * (h % 2):HD * (h % 2) + HD], start=(m == 0), stop=(m == 1))
                mm_.then_inc(S["pv_done"], 1)

            def u_transposed(c):
                pe.wait_ge(S["un_done"], ready(2 * c + 1))
                pe.wait_ge(S["u_done"], ready(c))
                for j in range(4):
                    mm_ = pe.transpose(bank[3][:, P * j:P * j + P], un[:, P * j:P * j + P], ident[:])
                mm_.then_inc(S["unT_done"], 1)

            def att_transposed(c):
                pe.wait_ge(S["att_done"], ready(2 * c + 1))
                pe.wait_ge(S["mixs_done"], ready(4 * c + 3))
                for j in range(4):
                    mm_ = pe.transpose(bank[3][:, P * j:P * j + P], att[:, j].rearrange("p v d -> p (v d)"), ident[:])
                mm_.then_inc(S["attT_done"], 1)

            def mem_panel(n):
                t = (n - MEM0) % 2
                if t == 0:
                    pe.wait_ge(S["lo_done"], ready(n + 1))
                    pe.wait_ge(S["evac_done"], ready(n - 1))
                for k in range(KT):
                    for m, (a, b) in enumerate(((h_hi, w_hi), (h_hi, w_lo), (h_lo, w_hi))):
                        mm_ = pe.matmul(bank[t][:, 0:2 * P], a[:, k, P * t:P * t + P], b[:, 0:2, k, :],
                                        start=(k == 0 and m == 0), stop=(k == KT - 1 and m == 2))
                if t == 1:
                    mm_.then_inc(S["panel_done"], 1)
                    pe.wait_ge(S["panel_done"], ready(n - 1))
                    pe.sem_inc(S["panel_done"], 1)

            def slots(gp, gb, i, last):
                c = 3 * gb + i
                for k in range(6):
                    if gp < 3:
                        n = NPA * gp + 1 + k
                        panel(n + 6 * i, n % 2, GW[gp])
                    else:
                        mem_panel(MEM0 + 6 * i + k)
                    if last and gp < 3:
                        if k == 0:
                            dt_transposed(gp, c if gb >= 0 else 0)
                        elif k == 2 and gb < 0:
                            dt_sums(gp)
                    if gb >= 0:
                        if k == 0:
                            pe.wait_ge(S["qs_done"], ready(c))
                            pe.wait_ge(S["kv_done"], ready(c))
                            pe.wait_ge(S["msk_done"], ready(8 * c - 1))
                            scores(c, 0)
                        elif k == 1:
                            part1(gb, i)
                        elif k == 2:
                            p_transposed(c, 0)
                            gates(c)
                            pe.wait_ge(S["exp_done"], ready(2 * c + 1))
                            scores(c, 1)
                            if last and gp < 3:
                                dt_sums(gp)
                        elif k == 3:
                            y_off(c)
                            if last and gp < 3:
                                pe.wait_ge(S["decay_done"], ready(gp))
                            values(c, 0)
                        elif k == 4:
                            p_transposed(c, 1)
                            y_diag(c)
                        else:
                            chunk_state(c)
                            values(c, 1)
                            u_transposed(c)
                            att_transposed(c)

            for t in range(3):
                norm(t)
            pe.wait_ge(consts_in, 16 * len(loads))
            pe.transpose(bank[7][:, 0:44], graw[:], ident[0:44, 0:44]).then_inc(S["consts_T"], 1)
            for ph in range(4):
                gp, gb = ph, ph - 1
                if gp < 3:
                    pe.wait_ge(S["hlo_done"], ready(6 * gp + 5))
                    panel(NPA * gp, (NPA * gp) % 2, GW[gp])
                if gb >= 0:
                    pe.wait_ge(S["decay_done"], ready(gb))
                if gp < 3:
                    with pe.Fori(0, 2) as i:
                        slots(gp, gb, i, False)
                    slots(gp, gb, 2, True)
                    for t in range(3 * gp + 3, 3 * gp + (6 if gp < 2 else 5)):
                        norm(t)
                else:
                    pe.wait_ge(S["hlo_done"], ready(2 * 10 + 1))
                    slots(gp, gb, 0, False)
                    slots(gp, gb, 1, True)
                    for n in range(MEM0 + 12, NPANELS_1):
                        mem_panel(n)

        in_block.close()
        mix_samples(nc, spent, io, mixT, ident, dict(
            proj=proj, bank=bank, rr=rr, mm=mm, cbm=cbm, xs=xs, xdt=xdt, xdd=xdd, yt=yt, un=un, bt=bt, vw=vw, kv=kv, raw=raw,
            acc=pt, tc=sc[:].rearrange("p h (m n) -> p (h m) n", m=2), hn=hn[0], x=hn[1], zs=zs, tz=tz, st=st, qs=qs, gpre=gpre, gssd=gssd, dtb=dtb, nega=nega, dsk=dsk, nsink=nsink,
            eps=eps, mhalf=mhalf, convw=convw, convb=convb, triu=triu, slow=slow, dtr=dtr))

def mix_samples(nc, spent, io, mixT, ident, B):
    R = NS
    proj, bank, w = B["proj"], B["bank"], B
    off = 3 + 256
    spare = proj[:, 1].rearrange("p k n -> p (k n)")
    used = [0]

    def take(rows, *shape):
        n = 1
        for v in shape:
            n *= v
        a = spare[0:rows, used[0]:used[0] + n]
        used[0] += n
        assert used[0] <= NPT * 387
        names = "abcd"[:len(shape)]
        if len(shape) > 1:
            a = a.rearrange("p (" + " ".join(names) + ") -> p " + " ".join(names), **dict(zip(names, shape)))
        return a

    xr = take(P, 8, NB, 7)
    acc, tmp, th, xc = (take(P, 8, R) for _ in range(4))
    tz, zs = take(P, 4, R), take(P, 4, R)
    blk = take(R, NB, TS)
    trius, slows = take(R, R), take(R, R)
    mrow = take(P, NB, R)
    selt, selj = take(4, P), take(4, P)
    selc = take(P, 4)
    m4 = take(4, 160)
    msk = take(P, 2, 160)
    zero = take(P, R)
    dx, dna, de, du, dl, dv, dw, dt, adt = (take(R, HEADS) for _ in range(9))
    decay = take(R, 3, HEADS)
    adtx = take(R, 4, P)
    decs = take(P, 4, NB)
    ssu, rsu = take(R, 2), take(R, 2)
    qd = take(P, NB, 2, 4, TS)
    sinkr, tmp24, mx, nb_, sd, es, rsum, den, ri = take(P, 2), take(P, 2, 4), take(P, 4), take(P, 4), take(P, 4), take(P, 4), \
        take(P, 4), take(P, 4), take(P, 4)
    pn = take(R, 2, 2, P)
    ctm = take(P, 2, 2, R)
    btm = take(R, 2, 2, P)
    rr = w["rr"][0:R].rearrange("p h n -> p (h n)")[:, 0:256].rearrange("p (h n) -> p h n", n=R)
    mm = w["mm"][0:R].rearrange("p h n -> p (h n)")[:, 0:256].rearrange("p (h n) -> p h n", n=R)
    cbm = w["cbm"][0:R, :, 0:R]
    xs, xdt, xdd, yt, un = (w[n][0:R, :] for n in ("xs", "xdt", "xdd", "yt", "un"))
    bt = w["bt"][0:R]
    kvt = take(R, 2, P)
    ck, cv, ckT = (w["raw"][:, n] for n in range(3))
    as_state = lambda a: a.rearrange("p (j n) -> p j n", j=4)
    sn = [as_state(w["acc"][:, 4 * s:4 * s + 4].rearrange("p k n -> p (k n)")) for s in range(2)] + \
         [as_state(w[name][:].rearrange("p h n -> p (h n)")[:, 256:768]) for name in ("rr", "mm")]
    so = w["tc"][:].rearrange("p (s j) n -> p s j n", s=2)
    stT = w["hn"][:].rearrange("p (s n) -> p s n", s=2)
    halo = w["x"]
    sc = w["zs"][:].rearrange("p a n -> p (a n)")[:, 0:320].rearrange("p (v n) -> p v n", v=2)
    pt = w["tz"][:, 0:2, :]
    att = w["bt"][:].rearrange("p a n -> p (a n)")[:, 0:P]

    order = dict(
        pe="psT pkT halo dtT pca pcb sels cum tot tr cb seg zT ydiag zero rawa rawb unT ckTa ckTb sc0 pT0 pnT0 pv0 aT0 "
           "sc1 pT1 pnT1 pv1 aT1".split(),
        act="halo1 halo2 tanh tz qd0 qd1 mask exp ln decay decs xs bt kv expseg pca pcb rawa rawb sq0 sq1 mixs ckTa e00 e01 es0 pt0 pn0 mixa0 "
            "e10 e11 es1 pt1 pn1 mixa1".split(),
        dve="psT pkT m0 a0 m1 a1 m2 a2 m3 a3 xc zs selc snk0 snk1 dx dna du dv dw dw2 dl dve dl2 dt adt adtx xdt cbm mm0 mm1 "
            "yoff ydiag ysk u un0 un1 ckTb s00 s01 nb0 sd0 den0 ri0 att0 s10 s11 nb1 sd1 den1 ri1 att1".split(),
        pool="z1 z2 z3 z4 z5 z6 z8 a1 a2 a3 a4 a5 a6 a7 a8 c1 c2 k0 k1 k2 k3 rr xdd yd um ur".split(),
    )
    sems = {e: nc.alloc_semaphore(name=f"sample_{e}_steps") for e in order}
    spent += sems.values()
    at = {e: {n: k + 1 for k, n in enumerate(names)} for e, names in order.items()}
    count = dict.fromkeys(order, 0)

    def step(e, name):
        count[e] += 1
        assert order[e][count[e] - 1] == name, (e, name, order[e][count[e] - 1])
        return sems[e], 1

    def after(e, name):
        return sems[e], at[e][name]

    def sem(name):
        spent.append(nc.alloc_semaphore(name=name))
        return spent[-1]

    loaded, stored, state_full, state_stored = sem("s_loaded"), sem("s_stored"), [sem(f"s_sf{n}") for n in range(4)], [sem("s_ss0"), sem("s_ss1")]
    ctm_done, btm_done, stT_pe, stT_done, yoff_done, ch_done, sdec_done, snew_done = (
        sem(n) for n in "s_ctm s_btm s_stTpe s_stT s_yoff s_ch s_sdec s_snew".split())

    in_block = ExitStack()
    block = in_block.enter_context(nc.Block())

    @block.sync
    def _(sp):
        for s in range(2):
            sp.sem_inc(state_stored[s], 16)
        sp.dma_start(halo[0:24, :], io["state_conv"][0].rearrange("b j c -> (b j) c")).then_inc(loaded, 16)
        sp.dma_start(ck, io["cache_win_k"][0].rearrange("b k v d -> k b (v d)")).then_inc(loaded, 16)
        sp.dma_start(cv, io["cache_win_v"][0].rearrange("b k v d -> k b (v d)")).then_inc(loaded, 16)
        for name, cache in (("s_win_k", "cache_win_k"), ("s_win_v", "cache_win_v")):
            sp.dma_start(io[name][0, :, 0:P - TS], io[cache][0, :, TS:P]).then_inc(stored, 16)

        def load_state(b):
            sp.wait_ge(sdec_done, ready(b - 4))
            sp.wait_ge(stT_pe, ready(b - 4))
            sp.dma_start(sn[b % 4], io["state_ssm"][0, b].rearrange("(j u) p n -> (u p) j n", u=2)).then_inc(state_full[b % 4], 16)

        for b in range(3):
            load_state(b)
        for b in range(NB):
            if b + 3 < NB:
                load_state(b + 3)
            sp.wait_ge(snew_done, ready(b))
            sp.dma_start(io["s_ssm"][0, b].rearrange("(j u) p n -> (u p) j n", u=2), so[:, b % 2]).then_inc(state_stored[b % 2], 16)
        for name, m in (("s_win_k", 1), ("s_win_v", 0)):
            for b in range(NB):
                sp.dma_start(io[name][0, b, P - TS:P].rearrange("t v d -> t (v d)"), kvt[TS * b:TS * b + TS, m, :])\
                    .then_inc(stored, 16)
        sp.wait_ge(*after("act", "rawb"))
        for b in range(NB):
            sp.dma_start(io["s_conv"][0, b], halo[TS * b + 1:TS * b + TS, :]).then_inc(stored, 16)
        sp.dma_start(io["p_conv"][0, 0], w["gpre"][0:3, :]).then_inc(stored, 16)
        sp.wait_ge(*after("dve", "pkT"))
        sp.dma_start(io["p_ssm"][0, 0].rearrange("(j u) p n -> (u p) j n", u=2), w["qs"][:]).then_inc(stored, 16)
        sp.dma_start(io["p_win_k"][0, 0].rearrange("t v d -> t (v d)"), w["kv"][:, 0, :]).then_inc(stored, 16)
        sp.dma_start(io["p_win_v"][0, 0].rearrange("t v d -> t (v d)"), w["vw"][:, 1, :]).then_inc(stored, 16)
        sp.wait_ge(stored, 16 * (2 + 3 * NB + 4))
        for s in range(2):
            sp.wait_ge(state_stored[s], 16 * (NB // 2 + 1))

    def credit(eng, *which):
        for s in which:
            eng.sem_inc(s, CREDIT)

    @block.gpsimd
    def _(pool):
        for n, (a, v) in enumerate(((blk, 1.0), (mrow, 1.0), (selt, 1.0), (selj, 1.0), (m4, 0.0), (zero, 0.0))):
            pool.memset(a, v).then_inc(*step("pool", f"z{n + 1}"))
        pool.memset(rsu, 0.0).then_inc(*step("pool", "z8"))
        pool.wait_ge(*after("pool", "z8"))

        def select(n, a, op, fill, base, pattern, cm):
            pool.affine_select(out=a, in_=a, compare_op=op, fill=fill, base=base, pattern=pattern, channel_multiplier=cm)\
                .then_inc(*step("pool", f"a{n}"))

        sel4 = lambda a: a.rearrange("p (a b) -> p a b", b=4)
        select(1, blk, ALU.is_ge, 0.0, 0, [[-4, NB], [0, TS]], 1)
        pool.wait_ge(*after("pool", "a1"))
        select(2, blk, ALU.is_ge, 0.0, 3, [[4, NB], [0, TS]], -1)
        select(3, mrow, ALU.is_ge, 0.0, 0, [[-4, NB], [1, R]], 0)
        pool.wait_ge(*after("pool", "a3"))
        select(4, mrow, ALU.is_ge, 0.0, 3, [[4, NB], [-1, R]], 0)
        select(5, sel4(selt), ALU.is_equal, 0.0, 0, [[0, R], [1, 4]], -1)
        select(6, selj.rearrange("p (a b c) -> p a b c", b=4, c=4), ALU.is_equal, 0.0, 0, [[0, 8], [1, 4], [0, 4]], -1)
        select(7, m4[:, 0:P], ALU.is_ge, NEG, -1, [[1, P]], -1)
        select(8, sel4(m4[:, P:160]), ALU.is_ge, NEG, 0, [[0, NB], [-1, TS]], 1)
        pool.wait_ge(*after("pool", "a8"))
        b2 = blk.rearrange("p a b -> p (a b)")
        pool.tensor_tensor(trius, w["triu"][0:R, 0:R], b2, ALU.mult).then_inc(*step("pool", "c1"))
        pool.tensor_tensor(slows, w["slow"][0:R, 0:R], b2, ALU.mult).then_inc(*step("pool", "c2"))
        pool.wait_ge(*after("act", "mask"))
        for hf in range(2):
            a = sel4(msk[:, hf, P:160])
            pool.affine_select(out=a, in_=a, compare_op=ALU.is_ge, fill=NEG, base=P * hf, pattern=[[-R, NB], [0, TS]],
                               channel_multiplier=1).then_inc(*step("pool", f"k{2 * hf}"))
            pool.wait_ge(*after("pool", f"k{2 * hf}"))
            pool.affine_select(out=a, in_=a, compare_op=ALU.is_ge, fill=NEG, base=R - 1 - P * hf, pattern=[[R, NB], [0, TS]],
                               channel_multiplier=-1).then_inc(*step("pool", f"k{2 * hf + 1}"))
        pool.wait_ge(*after("dve", "adt"))
        pool.tensor_tensor(rr, bc(trius.rearrange("p (o n) -> p o n", o=1), [R, HEADS, R]),
                           bc(adt.rearrange("p (h u) -> p h u", u=1), [R, HEADS, R]), ALU.mult).then_inc(*step("pool", "rr"))
        pool.wait_ge(*after("dve", "xdt"))
        pool.wait_ge(*after("act", "decay"))
        h3 = lambda a: a.rearrange("p (h d) -> p h d", d=HD)
        ph = lambda a: bc(a.rearrange("p (h u) -> p h u", u=1), [R, HEADS, HD])
        pool.tensor_tensor(h3(xdd), h3(xdt), ph(decay[:, 1, :]), ALU.mult).then_inc(*step("pool", "xdd"))
        pool.tensor_tensor(h3(xs), h3(xs), ph(w["dsk"][0:R, :]), ALU.mult).then_inc(*step("pool", "yd"))
        pool.wait_ge(*after("act", "sq1"))
        pool.tensor_tensor(rsu, ssu, w["eps"][0:R, 0:2], ALU.add).then_inc(*step("pool", "um"))
        pool.wait_ge(*after("pool", "um"))
        pool.tensor_tensor(rsu, rsu, w["mhalf"][0:R, 0:2], ALU.pow).then_inc(*step("pool", "ur"))

    @block.scalar
    def _(act):
        credit(act, stT_done)
        act.wait_ge(*after("pe", "halo"))
        for k in range(8):
            ins = act.activation(xr[:, k, :, 0:3], bank[7][:, 24 * k:24 * k + 24].rearrange("p (b j) -> p b j", j=3), ACT.Copy)
        ins.then_inc(*step("act", "halo1"))
        for k in range(8):
            ins = act.activation(xr[:, k, :, 3:7], proj[:, 0, k, off:off + R].rearrange("p (b t) -> p b t", t=TS), ACT.Copy)
        ins.then_inc(*step("act", "halo2"))
        act.wait_ge(*after("dve", "a3"))
        act.activation(th, acc, ACT.Tanh).then_inc(*step("act", "tanh"))
        act.activation(tz, proj[:, 0, T_Z:T_Z + 4, off:off + R], ACT.Tanh, scale=0.5).then_inc(*step("act", "tz"))
        for m in range(2):
            act.activation(qd[:, :, m].rearrange("p b j t -> p j b t"),
                           proj[:, 0, T_Q:T_Q + 4, off:off + R].rearrange("p j (b t) -> p j b t", t=TS), ACT.Copy, scale=0.125)\
                .then_inc(*step("act", f"qd{m}"))
        act.wait_ge(*after("pe", "sels"))
        act.activation(msk, bc(bank[5][:, 0:160].rearrange("p (o n) -> p o n", o=1), [P, 2, 160]), ACT.Copy).then_inc(*step("act", "mask"))
        act.wait_ge(*after("dve", "dna"))
        act.activation(de, dna, ACT.Exp).then_inc(*step("act", "exp"))
        act.wait_ge(*after("dve", "du"))
        act.activation(dl, du, ACT.Ln).then_inc(*step("act", "ln"))
        act.wait_ge(*after("pe", "tot"))
        act.activation(decay, bank[4][0:R, 32:56].rearrange("p (a n) -> p a n", a=3), ACT.Exp).then_inc(*step("act", "decay"))
        act.activation(decs, bank[4][:, 64:96].rearrange("p (j b) -> p j b", j=4), ACT.Exp).then_inc(*step("act", "decs"))
        act.wait_ge(*after("pe", "tr"))
        act.activation(xs, bank[2][0:R, :], ACT.Copy).then_inc(*step("act", "xs"))
        act.activation(bt, bank[3][0:R, 0:256].rearrange("p (a n) -> p a n", a=2), ACT.Copy).then_inc(*step("act", "bt"))
        act.activation(kvt, bank[3][0:R, 256:512].rearrange("p (a n) -> p a n", a=2), ACT.Copy).then_inc(*step("act", "kv"))
        act.wait_ge(*after("pe", "seg"))
        act.activation(mm, bank[5][0:R, 256:512].rearrange("p (h n) -> p h n", n=R), ACT.Exp).then_inc(*step("act", "expseg"))
        for name, bk, rows, dst in (("pca", 0, 3, w["gpre"][0:3, 0:512]), ("pcb", 1, 3, w["gpre"][0:3, 512:1024]),
                                    ("rawa", 0, R, halo[0:R, 0:512]), ("rawb", 1, R, halo[0:R, 512:1024])):
            act.wait_ge(*after("pe", name))
            act.activation(dst, bank[bk][0:rows, :], ACT.Copy).then_inc(*step("act", name))
        with act.Fori(0, NB // 4) as i:
            for q in range(4):
                s = q % 2
                act.wait_ge(stT_pe, ready(4 * i + q))
                act.wait_ge(yoff_done, ready(4 * i + q - 2))
                act.activation(stT[:, s], bank[2][:], ACT.Copy).then_inc(stT_done, 1)
        act.wait_ge(*after("dve", "u"))
        for q in range(2):
            act.activation(un[:, 256 * q:256 * q + 256], yt[:, 256 * q:256 * q + 256], ACT.Square, scale=1.0 / 16,
                           accum_out=ssu[:, q:q + 1]).then_inc(*step("act", f"sq{q}"))
        act.wait_ge(*after("pe", "unT"))
        for j in range(4):
            ins = act.activation(mixT(2)[:, j, 256:256 + R], bank[3][:, R * j:R * j + R], ACT.Copy, scale=w["gssd"][:, j:j + 1])
        ins.then_inc(*step("act", "mixs"))
        act.wait_ge(*after("pe", "ckTa"))
        act.activation(ckT[:, 0:4, :], bank[2][:].rearrange("p (b n) -> p b n", b=4), ACT.Copy).then_inc(*step("act", "ckTa"))
        for hf in range(2):
            act.wait_ge(*after("dve", f"sd{hf}"))
            for v in range(2):
                c = 2 * hf + v
                act.activation(sc[:, v, :], sc[:, v, :], ACT.Exp, bias=nb_[:, c:c + 1], accum_out=rsum[:, c:c + 1])\
                    .then_inc(*step("act", f"e{hf}{v}"))
            act.activation(es[:, 2 * hf:2 * hf + 2], sd[:, 2 * hf:2 * hf + 2], ACT.Exp).then_inc(*step("act", f"es{hf}"))
            act.wait_ge(*after("pe", f"pnT{hf}"))
            act.activation(pt, bank[2][:, 0:256].rearrange("p (v n) -> p v n", v=2), ACT.Copy).then_inc(*step("act", f"pt{hf}"))
            act.activation(pn[:, hf], bank[3][0:R, 0:256].rearrange("p (v n) -> p v n", v=2), ACT.Copy).then_inc(*step("act", f"pn{hf}"))
            act.wait_ge(*after("pe", f"aT{hf}"))
            act.activation(mixT(2)[:, 4:8, 256 + 16 * hf:272 + 16 * hf].rearrange("p j (b t) -> p j b t", t=TS),
                           bank[4][:, 0:P].rearrange("p (b u j t) -> p u j b t", b=4, u=2, j=4)[:, 0], ACT.Copy)\
                .then_inc(*step("act", f"mixa{hf}"))

    @block.vector
    def _(dve):
        credit(dve, ctm_done, btm_done, sdec_done, snew_done)

        def link(name, ins):
            ins.then_inc(*step("dve", name))
            dve.wait_ge(*after("dve", name))

        v4 = lambda a: a.rearrange("p k (b t) -> p k b t", t=TS)
        dve.wait_ge(*after("pe", "psT"))
        dve.tensor_copy(w["qs"][:].rearrange("p j n -> p (j n)"), bank[0][:]).then_inc(*step("dve", "psT"))
        dve.wait_ge(*after("pe", "pkT"))
        dve.tensor_copy(w["kv"][:, 0, :], bank[1][:, 0:P]).then_inc(*step("dve", "pkT"))
        dve.wait_ge(*after("act", "halo2"))
        for t in range(4):
            wt = bc(w["convw"][:, t, :].rearrange("p (k u v) -> p k u v", u=1, v=1), [P, 8, NB, TS])
            link(f"m{t}", dve.tensor_tensor(v4(tmp if t else acc), xr[:, :, :, t:t + TS], wt, ALU.mult))
            other = tmp if t else bc(w["convb"][:].rearrange("p (k u) -> p k u", u=1), [P, 8, R])
            link(f"a{t}", dve.tensor_tensor(acc, acc, other, ALU.add))
        dve.wait_ge(*after("act", "tz"))
        dve.scalar_tensor_tensor(xc, th, 1.0, acc, ALU.add, ALU.mult).then_inc(*step("dve", "xc"))
        dve.scalar_tensor_tensor(zs, tz, 1.0, proj[:, 0, T_Z:T_Z + 4, off:off + R], ALU.add, ALU.mult).then_inc(*step("dve", "zs"))
        dve.wait_ge(*after("pe", "sels"))
        link("selc", dve.tensor_copy(selc, bank[6][:, 0:4]))
        link("snk0", dve.tensor_tensor(tmp24, w["nsink"][:].rearrange("p (j v) -> p v j", v=2),
                                       bc(selc.rearrange("p (o j) -> p o j", o=1), [P, 2, 4]), ALU.mult))
        link("snk1", dve.tensor_reduce(sinkr, tmp24, mybir.AxisListType.X, ALU.add))
        link("dx", dve.tensor_tensor(dx, bank[4][0:R, 0:8], w["dtb"][0:R, :], ALU.add))
        link("dna", dve.scalar_tensor_tensor(dna, dx, -1.0, dx, ALU.mult, ALU.min))
        dve.wait_ge(*after("act", "exp"))
        link("du", dve.tensor_scalar(du, de, 1.0, None, ALU.add))
        link("dv", dve.tensor_scalar(dv, du, -1.0, 1e-30, ALU.add, ALU.max))
        link("dw", dve.reciprocal(dw, dv))
        link("dw2", dve.tensor_tensor(dw, dw, de, ALU.mult))
        dve.wait_ge(*after("act", "ln"))
        link("dl", dve.tensor_tensor(dl, dl, dw, ALU.mult))
        link("dve", dve.scalar_tensor_tensor(dv, dv, 1e-30, de, ALU.is_equal, ALU.mult))
        link("dl2", dve.tensor_tensor(dl, dl, dv, ALU.add))
        link("dt", dve.scalar_tensor_tensor(dt, dx, 0.0, dl, ALU.max, ALU.add))
        link("adt", dve.tensor_tensor(adt, dt, w["nega"][0:R, :], ALU.mult))
        h3 = lambda a: a.rearrange("p (h d) -> p h d", d=HD)
        ph = lambda a: bc(a.rearrange("p (h u) -> p h u", u=1), [R, HEADS, HD])
        dve.tensor_copy(adtx.rearrange("p j (u d) -> p (j u) d", u=2), ph(adt)).then_inc(*step("dve", "adtx"))
        dve.wait_ge(*after("act", "xs"))
        dve.tensor_tensor(h3(xdt), h3(xs), ph(dt), ALU.mult).then_inc(*step("dve", "xdt"))
        dve.wait_ge(*after("pe", "cb"))
        link("cbm", dve.tensor_tensor(cbm, bank[6][0:R, 64:128].rearrange("p (q n) -> p q n", q=2),
                                      bc(trius.rearrange("p (o n) -> p o n", o=1), [R, 2, R]), ALU.mult))
        dve.wait_ge(*after("act", "expseg"))
        for q in range(2):
            dve.tensor_tensor(mm[:, 4 * q:4 * q + 4, :], mm[:, 4 * q:4 * q + 4, :], bc(cbm[:, q:q + 1, :], [R, 4, R]), ALU.mult)\
                .then_inc(*step("dve", f"mm{q}"))
        dve.wait_ge(*after("act", "decs"))
        with dve.Fori(0, NB // 4) as i:
            for r in range(4):
                s, n = r % 2, 4 * i + r
                dve.wait_ge(yoff_done, ready(n - 2))
                dve.tensor_tensor(ctm[:, s], xc[:, 6:8, :], bc(mrow[:, ds(n, 1), :], [P, 2, R]), ALU.mult).then_inc(ctm_done, 1)
                dve.wait_ge(ch_done, ready(n - 2))
                dve.tensor_tensor(btm[:, s], bt, bc(blk[:, ds(n, 1), 0:1], [R, 2, P]), ALU.mult).then_inc(btm_done, 1)
                dve.wait_ge(state_full[r], 16 * i + 16)
                dve.wait_ge(state_stored[s], 32 * i + 16 * (r // 2) + 16)
                dve.tensor_tensor(so[:, s], sn[r], bc(decs[:, :, ds(n, 1)], [P, 4, P]), ALU.mult).then_inc(sdec_done, 1)
                dve.wait_ge(ch_done, ready(n))
                dve.wait_ge(sdec_done, ready(n))
                dve.tensor_tensor(so[:, s], so[:, s], bank[5][:].rearrange("p (j n) -> p j n", j=4), ALU.add).then_inc(snew_done, 1)
        dve.wait_ge(yoff_done, ready(NB - 1))
        link("yoff", dve.tensor_tensor(h3(yt), h3(bank[6][0:R, :]), ph(decay[:, 0, :]), ALU.mult))
        dve.wait_ge(*after("pe", "ydiag"))
        link("ydiag", dve.tensor_tensor(yt, yt, bank[7][0:R, :], ALU.add))
        dve.wait_ge(*after("pool", "yd"))
        link("ysk", dve.tensor_tensor(yt, yt, xs, ALU.add))
        dve.wait_ge(*after("pe", "zT"))
        link("u", dve.scalar_tensor_tensor(yt, bank[3][0:R, :], 0.5, yt, ALU.mult, ALU.mult))
        dve.wait_ge(*after("pool", "ur"))
        for q in range(2):
            dve.tensor_scalar(un[:, 256 * q:256 * q + 256], yt[:, 256 * q:256 * q + 256], rsu[:, q:q + 1], None, ALU.mult)\
                .then_inc(*step("dve", f"un{q}"))
        dve.wait_ge(*after("pe", "ckTb"))
        dve.tensor_copy(ckT[:, 4:8, :], bank[7][:].rearrange("p (b n) -> p b n", b=4)).then_inc(*step("dve", "ckTb"))
        dve.wait_ge(*after("pool", "k3"))
        for hf in range(2):
            h2 = slice(2 * hf, 2 * hf + 2)
            dve.wait_ge(*after("pe", f"sc{hf}"))
            for v in range(2):
                c = 2 * hf + v
                dve.tensor_tensor_reduce(sc[:, v, :], bank[5 + v][:, 0:160], msk[:, hf, :], 1.0, -3.0e38, ALU.add, ALU.max,
                                         mx[:, c:c + 1]).then_inc(*step("dve", f"s{hf}{v}"))
            dve.wait_ge(*after("dve", f"s{hf}1"))
            link(f"nb{hf}", dve.scalar_tensor_tensor(nb_[:, h2], mx[:, h2], -1.0, sinkr, ALU.mult, ALU.min))
            dve.tensor_tensor(sd[:, h2], nb_[:, h2], sinkr, ALU.subtract).then_inc(*step("dve", f"sd{hf}"))
            dve.wait_ge(*after("act", f"es{hf}"))
            link(f"den{hf}", dve.tensor_tensor(den[:, h2], es[:, h2], rsum[:, h2], ALU.add))
            link(f"ri{hf}", dve.reciprocal(ri[:, h2], den[:, h2]))
            dve.wait_ge(*after("pe", f"pv{hf}"))
            dve.tensor_tensor(att.rearrange("p (v d) -> p v d", v=2), bank[7][:, 0:P].rearrange("p (v d) -> p v d", v=2),
                              bc(ri[:, h2].rearrange("p (v u) -> p v u", u=1), [P, 2, HD]), ALU.mult).then_inc(*step("dve", f"att{hf}"))

    @block.tensor
    def _(pe):
        credit(pe, stT_pe, yoff_done, ch_done)
        for j in range(4):
            ins = pe.transpose(bank[0][:, P * j:P * j + P], w["st"][:, P * j:P * j + P], ident[:])
        ins.then_inc(*step("pe", "psT"))
        pe.transpose(bank[1][:, 0:P], w["kv"][:, 1, :], ident[:]).then_inc(*step("pe", "pkT"))
        pe.wait_ge(loaded, 48)
        for k in range(8):
            ins = pe.transpose(bank[7][:, 24 * k:24 * k + 24], halo[0:24, P * k:P * k + P], ident[0:24, 0:24])
        ins.then_inc(*step("pe", "halo"))
        pe.transpose(bank[4][0:R, 0:8], w["dtr"][:, 256:256 + R], ident[0:8, 0:8]).then_inc(*step("pe", "dtT"))
        pe.wait_ge(*after("dve", "pkT"))
        for m, name in enumerate(("pca", "pcb")):
            for k in range(4):
                ins = pe.transpose(bank[m][0:3, P * k:P * k + P], proj[:, 0, 4 * m + k, off - 3:off], ident[:])
            ins.then_inc(*step("pe", name))
        pe.wait_ge(*after("pool", "a8"))
        pe.transpose(bank[6][:, 0:4], selj, ident[0:4, 0:4])
        pe.matmul(bank[5][:, 0:160], selt, m4, start=True, stop=True).then_inc(*step("pe", "sels"))
        pe.wait_ge(*after("dve", "adt"))
        pe.wait_ge(*after("pool", "c2"))
        for m, lhs in enumerate((trius, slows, blk.rearrange("p a b -> p (a b)"))):
            ins = pe.matmul(bank[4][0:R, 32 + 8 * m:40 + 8 * m], lhs, adt, start=True, stop=True)
        ins.then_inc(*step("pe", "cum"))
        pe.wait_ge(*after("dve", "adtx"))
        for j in range(4):
            ins = pe.matmul(bank[4][:, 64 + 8 * j:72 + 8 * j], adtx[:, j, :], blk[:, :, 0], start=True, stop=True)
        ins.then_inc(*step("pe", "tot"))
        for j in range(4):
            pe.transpose(bank[2][0:R, P * j:P * j + P], xc[:, j, :], ident[:])
        for j in range(2):
            pe.transpose(bank[3][0:R, P * j:P * j + P], xc[:, 4 + j, :], ident[:])
        for m, k in enumerate((T_V, T_K)):
            ins = pe.transpose(bank[3][0:R, 256 + P * m:384 + P * m], proj[:, 0, k, off:off + R], ident[:])
        ins.then_inc(*step("pe", "tr"))
        for q in range(2):
            ins = pe.matmul(bank[6][0:R, 64 + R * q:96 + R * q], xc[:, 4 + q, :], xc[:, 6 + q, :], start=True, stop=True)
        ins.then_inc(*step("pe", "cb"))
        pe.wait_ge(*after("act", "mask"))
        pe.wait_ge(*after("pool", "rr"))
        pe.matmul(bank[5][0:R, 256:512], w["slow"][0:R, 0:R], rr.rearrange("p h n -> p (h n)"), start=True, stop=True)\
            .then_inc(*step("pe", "seg"))
        pe.wait_ge(*after("act", "kv"))
        for j in range(4):
            ins = pe.transpose(bank[3][0:R, P * j:P * j + P], zs[:, j, :], ident[:])
        ins.then_inc(*step("pe", "zT"))
        pe.wait_ge(*after("dve", "mm1"))
        for h in range(HEADS):
            ins = pe.matmul(bank[7][0:R, HD * h:HD * h + HD], mm[:, h, :], xdt[:, HD * h:HD * h + HD], start=True, stop=True)
        ins.then_inc(*step("pe", "ydiag"))
        pe.matmul(bank[6][0:R, :], zero, bc(w["triu"][:].rearrange("p (o n) -> p o n", o=1), [P, 4, P]), start=True, stop=False,
                  skip_group_check=True).then_inc(*step("pe", "zero"))
        pe.wait_ge(*after("act", "pcb"))
        for m, name in enumerate(("rawa", "rawb")):
            for k in range(4):
                ins = pe.transpose(bank[m][0:R, P * k:P * k + P], proj[:, 0, 4 * m + k, off:off + R], ident[:])
            ins.then_inc(*step("pe", name))
        pe.wait_ge(*after("pool", "xdd"))
        with pe.Fori(0, NB // 4) as i:
            for r in range(4):
                s, n = r % 2, 4 * i + r
                pe.wait_ge(state_full[r], 16 * i + 16)
                pe.wait_ge(stT_done, ready(n - 1))
                for j in range(4):
                    ins = pe.transpose(bank[2][:, P * j:P * j + P], sn[r][:, j, :], ident[:])
                ins.then_inc(stT_pe, 1)
                pe.wait_ge(btm_done, ready(n))
                pe.wait_ge(snew_done, ready(n - 1))
                for j in range(4):
                    ins = pe.matmul(bank[5][:, P * j:P * j + P], xdd[:, P * j:P * j + P], btm[:, s, j // 2, :], start=True, stop=True)
                ins.then_inc(ch_done, 1)
                pe.wait_ge(stT_done, ready(n))
                pe.wait_ge(ctm_done, ready(n))
                for q in range(2):
                    ins = pe.matmul(bank[6][0:R, 256 * q:256 * q + 256], ctm[:, s, q, :], stT[:, s, 256 * q:256 * q + 256],
                                    start=False, stop=True, skip_group_check=True)
                ins.then_inc(yoff_done, 1)
        pe.wait_ge(*after("dve", "un1"))
        for j in range(4):
            ins = pe.transpose(bank[3][:, R * j:R * j + R], un[:, P * j:P * j + P], ident[0:R, 0:R])
        ins.then_inc(*step("pe", "unT"))
        for b in range(4):
            ins = pe.transpose(bank[2][:, P * b:P * b + P], ck[:, b, :], ident[:])
        ins.then_inc(*step("pe", "ckTa"))
        for b in range(4):
            ins = pe.transpose(bank[7][:, P * b:P * b + P], ck[:, 4 + b, :], ident[:])
        ins.then_inc(*step("pe", "ckTb"))
        pe.wait_ge(snew_done, ready(NB - 1))
        for hf in range(2):
            if hf == 0:
                pe.wait_ge(*after("act", "ckTa"))
                pe.wait_ge(*after("dve", "ckTb"))
            else:
                pe.wait_ge(*after("dve", "s01"))
            for v in range(2):
                rows = slice(HD * v, HD * v + HD)
                pe.matmul(bank[5 + v][:, P:160], qd[rows, 4 * hf:4 * hf + 4].rearrange("p b u j t -> p (b u j t)"),
                          proj[rows, 0, T_K, off:off + R], start=True, stop=True)
                for b in range(4):
                    ins = pe.matmul(bank[5 + v][R * b:R * b + R, 0:P], qd[rows, 4 * hf + b].rearrange("p u j t -> p (u j t)"),
                                    ckT[rows, 4 * hf + b, :], start=True, stop=True)
            ins.then_inc(*step("pe", f"sc{hf}"))
            pe.wait_ge(*after("act", f"e{hf}1"))
            if hf == 0:
                pe.wait_ge(*after("act", "mixs"))
            for v in range(2):
                ins = pe.transpose(bank[2][:, P * v:P * v + P], sc[:, v, 0:P], ident[:])
            ins.then_inc(*step("pe", f"pT{hf}"))
            for v in range(2):
                ins = pe.transpose(bank[3][0:R, P * v:P * v + P], sc[:, v, P:160], ident[:])
            ins.then_inc(*step("pe", f"pnT{hf}"))
            pe.wait_ge(*after("act", f"pn{hf}"))
            for v in range(2):
                cols = slice(HD * v, HD * v + HD)
                pe.matmul(bank[7][:, cols], pn[:, hf, v, :], kvt[:, 0, cols], start=True, stop=False, skip_group_check=True)
                for b in range(4):
                    ins = pe.matmul(bank[7][R * b:R * b + R, cols], pt[:, v, R * b:R * b + R], cv[:, 4 * hf + b, cols],
                                    start=False, stop=True, skip_group_check=True)
            ins.then_inc(*step("pe", f"pv{hf}"))
            pe.wait_ge(*after("dve", f"att{hf}"))
            pe.transpose(bank[4][:, 0:P], att, ident[:]).then_inc(*step("pe", f"aT{hf}"))
            pe.wait_ge(*after("act", f"mixa{hf}"))

    in_block.close()


STAGES = ("w0", "w1", "w2", "x0", "x1", "o0", "o1", "x2", "o2")
FIRST = {s: KT * n for n, s in enumerate(STAGES)}
OPERANDS = ("w0", "w1", "w2", "x0", "x1", "o0", "o1", "x2", "o2", "f0")
PARTS = {"w": 4, "x": 3, "o": 3, "f": 3}
OT_SLOT = dict(w0=0, w1=1, w2=0, x0=1, x1=0, o0=1, o1=0, x2=1, o2=0)
NPANELS = KT * len(STAGES)


def part_of(operand, i):
    n = 0
    for o in OPERANDS:
        if o == operand:
            return n + i
        n += PARTS[o[0]]


def walk(do):
    panels, post, prea, preb, split = do["panels"], do["post"], do["prea"], do["preb"], do["split"]
    sc, soft, pt, pv, mem = do["sc"], do["soft"], do["pt"], do["pv"], do["mem"]

    def weave(stage, s, t, u):
        panels(stage, 0, 1)
        post(s, t)
        panels(stage, 1, 1)
        prea("x", u)
        post(s, t + 1)
        panels(stage, 2, 1)
        preb("x", u)
        prea("x", u + 1)
        panels(stage, 3, 1)
        post(s, t + 2)
        panels(stage, 4, 1)
        preb("x", u + 1)
        prea("x", u + 2)
        panels(stage, 5, 2)
        preb("x", u + 2)
        panels(stage, 7, 1)

    split(0)
    do["start"]()
    split(1)
    panels("w0", 0, 2)
    mem("k", 0)
    panels("w0", 2, 1)
    mem("k", 1)
    panels("w0", 3, 5)
    panels("w1", 0, 1)
    split(2)
    post("w", 0)
    panels("w1", 1, 2)
    post("w", 1)
    panels("w1", 3, 2)
    post("w", 2)
    panels("w1", 5, 3)
    weave("w2", "w", 3, 0)
    weave("x0", "w", 6, 3)
    for g, stage in ((0, "x1"), (1, "o0")):
        t = 3 * g
        panels(stage, 0, 1)
        sc(t)
        soft(t)
        panels(stage, 1, 1)
        pt(t)
        sc(t + 1)
        soft(t + 1)
        panels(stage, 2, 1)
        pv(t)
        panels(stage, 3, 1)
        pt(t + 1)
        sc(t + 2)
        soft(t + 2)
        panels(stage, 4, 1)
        pv(t + 1)
        panels(stage, 5, 1)
        pt(t + 2)
        panels(stage, 6, 1)
        pv(t + 2)
        panels(stage, 7, 1)
    weave("o1", "o", 0, 6)
    panels("x2", 0, 1)
    for i in range(3):
        post("o", 3 + i)
        panels("x2", 1 + i, 1)
    panels("x2", 4, 4)
    do["fill"](0)
    sc(6)
    soft(6)
    sc(7)
    soft(7)
    do["kt"](0, 0)
    pt(6)
    do["kt"](0, 1)
    pv(6)
    pt(7)
    do["ksc"](0)
    pv(7)
    do["samples"]()
    prea("f", 0)
    panels("o2", 0, 2)
    preb("f", 0)
    prea("f", 1)
    panels("o2", 2, 2)
    preb("f", 1)
    prea("f", 2)
    panels("o2", 4, 2)
    preb("f", 2)
    panels("o2", 6, 2)


def build_cross(nc, keep, io, xm, ot_last, next_hi, next_lo, ident, spent):
    ctx = ExitStack()
    with ctx:
        def sb(name, shape, dt=F32):
            return ctx.enter_context(nc.sbuf_tensor("b_" + name, shape, dt))

        def sem(name):
            return keep.enter_context(nc.semaphore("b_" + name))

        raw = sb("raw", [P, 4, KT, P])
        w_hi = sb("whi", [P, 2, KT, P], F32R)
        w_lo = sb("wlo", [P, 2, KT, P], F32R)
        op_hi = [sb("ophi", [P, KT, 384], F32R), next_hi]
        op_lo = [sb("oplo", [P, KT, 384], F32R), next_lo]
        ot = [ot_last, sb("ot", [P, KT, 384])]
        mkT = sb("mk", [P, KT, NMEM])
        mv = sb("mv", [P, 2, D])
        pm = sb("pm", [P, 2, 4, NMEM])
        pT = sb("pt", [P, 2, KT, P])
        hn = sb("hn", [P, D])
        junk = sb("junk", [P, D])
        gain = sb("gain", [P, 3, D])
        cache = sb("cache", [P, 2, D])
        tmp = sb("tmp", [P, D])
        mhalf = sb("mhalf", [P, 1])
        mstat = sb("stat", [P, 4, 2])
        mstat2 = sb("stat2", [P, 4, 1])
        mx = sb("mx", [P, 2, 4])
        nb = sb("nb", [P, 2, 4])
        rsum = sb("rsum", [P, 2, 4])
        ri = sb("ri", [P, 2, 4])
        bank = [ctx.enter_context(nc.psum_tensor(f"b_bank{n}", [P, 512], F32)) for n in range(2)]
        pair = {n: ctx.enter_context(nc.psum_tensor(f"b_pair{n}", [P, 1024], F32)) for n in (2, 4, 6)}

        qpad = hn[:].rearrange("p (k i r) -> p k i r", k=KT, i=4)
        kT = (mkT[:], pm[:].rearrange("p s h n -> p (s h) n"))
        sp_ = pT[:, 1].rearrange("p k n -> p (k n)")[:, 0:NMEM]
        spT = pT[:, 1].rearrange("p k n -> p (k n)")[:, 256:512]
        mixg = lambda g: xm[:, g, :].rearrange("p (k n) -> p k n", n=384)
        xt = lambda t: xm[:, t // 3, D * (t % 3):D * (t % 3 + 1)]
        GAIN = dict(w=0, x=1, o=2, f=0)

        raw_full = [sem(f"raw_full{n}") for n in range(4)]
        x_full = [sem(f"x_full{g}") for g in range(3)]
        mem_full, gains_full, gffn_full, setup = sem("mem_full"), sem("gains_full"), sem("gffn_full"), sem("setup")
        nat_full = [sem(f"nat_full{n}") for n in range(3)]
        owners = dict(
            act="hi_done evac_done sq_done ophi_done exp_done pta_done nata_done qpad_done scopya_done shi_done",
            dve="lo_done turn_free normed oplo_done hn_done nb_done p_done ptd_done natd_done memout_done scopyd_done slo_done",
            pool="ms_done rstd_done",
            pe="panel_done turn_done sc_done pT_done pv_done natT_done nv_done svT_done")
        S = {n: sem(n) for names in owners.values() for n in names.split()}
        nc.clear_and_free_semaphores(spent)
        scope = ExitStack()
        block = scope.enter_context(nc.Block())

        def credit(eng, who):
            for n in owners[who].split():
                eng.sem_inc(S[n], CREDIT)

        turn = {}
        number = lambda kind, i: turn.setdefault(f"{kind}{i}", len(turn))
        norms = {}
        nothing = dict.fromkeys("panels split sc soft pt pv fill kt ksc".split(), lambda *a: None)
        walk(dict(nothing, start=lambda: None, samples=lambda: None,
                  mem=number, preb=number,
                  post=lambda s, t: (number(s, t), norms.setdefault(("post", s, t), len(norms))),
                  prea=lambda s, t: norms.setdefault(("pre", s, t), len(norms))))

        def last_panel_before(operand):
            n = OPERANDS.index(operand) - 2
            if n < 0:
                return -1
            stage = OPERANDS[n]
            return FIRST[stage] + KT - 1

        posts = [k[1:] for k in norms if k[0] == "post"]
        hn_write = {k[1:]: i for i, k in enumerate(k for k in norms if k[0] == "pre")}
        slot_of = lambda operand: OPERANDS.index(operand) % 2

        def width(stage):
            return GW[int(stage[1])]

        def raw_count(n):
            return sum(48 if STAGES[m // KT][0] == "w" else 16 for m in range(n % 4, n + 1, 4))

        def nat_item(m):
            half, r = m // 8, m % 8
            return ("cache_mem_k" if r < 4 else "cache_mem_v"), 4 * half + r % 4

        def nat_count(m):
            return 4 * (m // 8) + m % 4

        def nat(m):
            return (cache[:], ot[0][:].rearrange("p k n -> p (k n)")[:, 0:2 * D].rearrange("p (m n) -> p m n", m=2), mv[:])[m % 3]

        def k_place_free(b):
            return (S["sc_done"], ready(7)) if b == 0 else (S["pT_done"], ready(7)) if b == 1 else (S["sc_done"], ready(6 + b))

        def picked(op, hf, h):
            out = op[slot_of("o2")][:, 2 * h:2 * h + 2, 256 + 16 * hf:272 + 16 * hf].rearrange("p e (i t) -> p e i t", t=TS)
            return out, pair[2][:].rearrange("p (h e i g t) -> p h e i g t", h=4, e=2, i=4, t=TS)[:, h, :, :, h]

        @block.sync
        def _(sp):

            def load_panel(n):
                stage, j = STAGES[n // KT], n % KT
                sp.wait_ge(S["lo_done"], ready(n - 4))
                name = {"w": "w_out", "x": "w_xq", "o": "w_xo"}[stage[0]]
                cols = io[name][:, P * j:P * j + P]
                if stage[0] != "w":
                    sp.dma_start(raw[:, n % 4], cols.rearrange("(k p) n -> p k n", p=P)).then_inc(raw_full[n % 4], 16)
                else:
                    sp.dma_start(raw[:, n % 4, 0:4], cols[0:SSD_W].rearrange("(k p) n -> p k n", p=P)).then_inc(raw_full[n % 4], 16)
                    for v in range(2):
                        sp.dma_start(raw[HD * v:HD * v + HD, n % 4, 4:8],
                                     cols[SSD_W + 256 * v:SSD_W + 256 * v + 256].rearrange("(k p) n -> p k n", p=HD))\
                            .then_inc(raw_full[n % 4], 16)

            def load_nat(m):
                name, b = nat_item(m)
                if m < 3:
                    sp.wait_ge(*((S["memout_done"], ready(1)), (S["turn_done"], ready(turn["o5"])),
                                 (S["pv_done"], ready(7)))[m])
                else:
                    k, _ = nat_item(m - 3)
                    if k == "cache_mem_k":
                        sp.wait_ge(S["natT_done"], ready(2 * nat_count(m - 3) + (m - 3) // 8 + 1))
                    else:
                        sp.wait_ge(S["nv_done"], ready(nat_count(m - 3)))
                sp.dma_start(nat(m), io[name][0, b].rearrange("(m p) h d -> p m (h d)", p=P)).then_inc(nat_full[m % 3], 16)

            for n in range(NPANELS):
                if n == 4:
                    for i, name in ((0, "g_mix_post"), (1, "g_x_pre"), (2, "g_x_post")):
                        sp.dma_start(gain[:, i], io[name].rearrange("(o n) -> o n", o=1).broadcast_to([P, D])).then_inc(gains_full, 16)
                if n == 3:
                    for dst, name in ((cache, "p_mem_k"), (mv, "p_mem_v")):
                        sp.dma_start(dst[:], io[name][0, 0].rearrange("(m p) h d -> p m (h d)", p=P)).then_inc(mem_full, 16)
                for stage, g in (("w0", 0), ("w1", 1), ("w2", 2)):
                    if n == FIRST[stage] + (4 if g else 5):
                        sp.wait_ge(S["oplo_done"], ready(part_of(stage, 3)))
                        if g == 2:
                            sp.wait_ge(setup, 2)
                        for i in range(3):
                            t = 3 * g + i
                            sp.dma_start(xt(t)[0:group_rows(t)], io["x"](t)).then_inc(x_full[g], 16)
                if n == FIRST["x1"]:
                    sp.wait_ge(S["normed"], ready(norms["post", "w", 8]))
                    sp.dma_start(gain[:, 0], io["g_ffn_pre"].rearrange("(o n) -> o n", o=1).broadcast_to([P, D])).then_inc(gffn_full, 16)
                if n == FIRST["o0"]:
                    load_nat(0)
                if n == FIRST["x2"] + 6:
                    load_nat(1)
                if n == FIRST["o2"] + 6:
                    for m in range(2, 2 * NB):
                        load_nat(m)
                load_panel(n)

        @block.gpsimd
        def _(pool):
            credit(pool, "pool")
            pool.memset(mhalf[:], -0.5).then_inc(setup, 1)
            pool.wait_ge(setup, 1)

            def stat(n):
                s = n % 4
                pool.wait_ge(S["sq_done"], ready(n))
                pool.wait_ge(S["normed"], ready(n - 4))
                pool.tensor_scalar(mstat2[:, s], mstat[:, s, 0:1], 1.0 / D, EPS, ALU.mult, ALU.add).then_inc(S["ms_done"], 1)
                pool.wait_ge(S["ms_done"], ready(n))
                pool.tensor_tensor(mstat[:, s, 1:2], mstat2[:, s], mhalf[:], ALU.pow).then_inc(S["rstd_done"], 1)

            def split(g):
                if g == 2:
                    pool.wait_ge(S["oplo_done"], ready(part_of("w2", 3)))
                    pool.memset(xt(8), 0.0).then_inc(setup, 1)

            def sc(t):
                if t == 6:
                    pool.wait_ge(S["turn_done"], ready(turn["x8"]))
                    pool.memset(hn[:], 0.0).then_inc(setup, 1)

            skip = lambda *a: None
            walk(dict(panels=skip, preb=skip, fill=skip, kt=skip, ksc=skip, sc=sc, soft=skip, pt=skip, pv=skip, mem=skip, start=skip, samples=skip, split=split,
                      post=lambda s, t: stat(norms["post", s, t]), prea=lambda s, t: stat(norms["pre", s, t])))

        def x_ready(eng, n, t):
            before = [norms["post", s, u] for s, u in posts if u == t and norms["post", s, u] < n]
            if before:
                eng.wait_ge(S["normed"], ready(max(before)))

        @block.scalar
        def _(act):
            credit(act, "act")

            def hi(n):
                act.wait_ge(raw_full[n % 4], raw_count(n))
                act.wait_ge(S["panel_done"], ready(n - 2))
                act.activation(w_hi[:, n % 2], raw[:, n % 4], ACT.Copy).then_inc(S["hi_done"], 1)

            def panels(stage, j0, cnt):
                for j in range(j0, j0 + cnt):
                    n = FIRST[stage] + j
                    w = width(stage)
                    dst = ot[OT_SLOT[stage]][:, j, 0:w]
                    act.wait_ge(S["panel_done"], ready(n))
                    act.activation(dst, bank[n % 2][:, 0:w], ACT.Copy).then_inc(S["evac_done"], 1)
                    if n + 2 < NPANELS:
                        hi(n + 2)

            def split(g):
                name = f"w{g}"
                w = GW[g]
                for i in range(4):
                    act.wait_ge(S["panel_done"], ready(last_panel_before(name)))
                    act.activation(op_hi[slot_of(name)][:, 2 * i:2 * i + 2, 0:w], mixg(g)[:, 2 * i:2 * i + 2, 0:w], ACT.Copy)\
                        .then_inc(S["ophi_done"], 1)

            def post(s, t):
                n, u = norms["post", s, t], turn[f"{s}{t}"]
                act.wait_ge(S["turn_done"], ready(u))
                act.wait_ge(S["normed"], ready(n - 4))
                act.wait_ge(S["sq_done"], ready(n - 1))
                act.activation(junk[:], pair[2][:], ACT.Square, accum_out=mstat[:, n % 4, 0:1]).then_inc(S["sq_done"], 1)

            def prea(s, t):
                n = norms["pre", s, t]
                x_ready(act, n, t)
                src = xt(t)
                act.wait_ge(S["normed"], ready(n - 4))
                act.wait_ge(S["sq_done"], ready(n - 1))
                act.activation(junk[:], src, ACT.Square, accum_out=mstat[:, n % 4, 0:1]).then_inc(S["sq_done"], 1)

            def preb(s, t):
                name, c = f"{s}{t // 3}", t % 3
                act.wait_ge(S["turn_done"], ready(turn[f"{s}{t}"]))
                act.wait_ge(S["panel_done"], ready(last_panel_before(name)))
                act.activation(op_hi[slot_of(name)][:, :, P * c:P * c + P], pair[2][:].rearrange("p (k n) -> p k n", k=KT), ACT.Copy)\
                    .then_inc(S["ophi_done"], 1)

            def soft(t):
                s = t % 2
                act.wait_ge(S["nb_done"], ready(t))
                act.wait_ge(S["pT_done"], ready(t - 2))
                for h in range(4):
                    ins = act.activation(pm[:, s, h], pair[4][:, NMEM * h:NMEM * h + NMEM], ACT.Exp, bias=nb[:, s, h:h + 1],
                                         scale=1.0 / 16, accum_out=rsum[:, s, h:h + 1])
                ins.then_inc(S["exp_done"], 1)

            def pt(t):
                act.wait_ge(S["pT_done"], ready(t))
                act.wait_ge(S["pv_done"], ready(t - 2))
                act.activation(pT[:, t % 2, 0:4], pair[6][:, 0:512].rearrange("p (k n) -> p k n", k=4), ACT.Copy).then_inc(S["pta_done"], 1)

            def pv(t):
                name, c = f"o{t // 3}", t % 3
                act.wait_ge(S["pv_done"], ready(t))
                act.wait_ge(S["panel_done"], ready(last_panel_before(name)))
                act.activation(op_hi[slot_of(name)][:, :, P * c:P * c + P], pair[6][:].rearrange("p (k n) -> p k n", k=KT), ACT.Copy)\
                    .then_inc(S["ophi_done"], 1)

            def fill(hf):
                act.wait_ge(setup, 3)
                act.wait_ge(S["evac_done"], ready(FIRST["x2"] + 7))
                if hf:
                    act.wait_ge(S["sc_done"], ready(11))
                for h in range(4):
                    ins = act.activation(qpad.rearrange("p (h e) i (g t) -> p h e i g t", e=2, t=TS)[:, h, :, :, h],
                                         ot[OT_SLOT["x2"]][:, 2 * h:2 * h + 2, 256 + 16 * hf:272 + 16 * hf]
                                         .rearrange("p e (i t) -> p e i t", t=TS), ACT.Copy)
                ins.then_inc(S["qpad_done"], 1)

            def kt(b, q):
                if q == 0:
                    act.wait_ge(S["natT_done"], ready(2 * b + b // 4))
                    act.wait_ge(*k_place_free(b))
                    act.activation(kT[b % 2][:, 0:4, :], pair[2][:].rearrange("p (k n) -> p k n", k=4), ACT.Copy)\
                        .then_inc(S["nata_done"], 1)

            def samples():
                for hf in range(2):
                    if hf:
                        fill(1)
                    for b in range(4 * hf, 4 * hf + 4):
                        if b:
                            kt(b, 0)
                    t = 8 + hf
                    act.wait_ge(S["nb_done"], ready(t))
                    act.wait_ge(*((S["natT_done"], ready(8)) if hf else (S["pv_done"], ready(7))))
                    act.activation(sp_, pair[4][:, 0:NMEM], ACT.Exp, bias=nb[:, t % 2, 0:1], scale=1.0 / 16,
                                   accum_out=rsum[:, t % 2, 0:1]).then_inc(S["exp_done"], 1)
                    act.wait_ge(S["natT_done"], ready(9 * hf + 8))
                    act.wait_ge(S["nv_done"], ready(4 * hf - 1))
                    act.activation(spT, pair[6][:, 512:768], ACT.Copy).then_inc(S["pta_done"], 1)
                    act.wait_ge(S["nv_done"], ready(4 * hf + 3))
                    act.wait_ge(S["svT_done"], ready(hf - 1))
                    act.activation(junk[:, 0:512], pair[6][:, 0:512], ACT.Copy).then_inc(S["scopya_done"], 1)
                    act.wait_ge(S["svT_done"], ready(hf))
                    act.wait_ge(S["panel_done"], ready(last_panel_before("o2")))
                    for h in range(4):
                        ins = act.activation(*picked(op_hi, hf, h), ACT.Copy)
                    ins.then_inc(S["shi_done"], 1)
                act.wait_ge(S["shi_done"], ready(1))
                act.sem_inc(S["ophi_done"], 1)

            def start():
                hi(0)
                hi(1)

            walk(dict(panels=panels, post=post, prea=prea, preb=preb, split=split, sc=lambda t: None, soft=soft, pt=pt, pv=pv,
                      mem=lambda *a: None, start=start, samples=samples, fill=fill, kt=kt, ksc=lambda b: None))

        @block.vector
        def _(dve):
            credit(dve, "dve")

            def lo(n):
                dve.wait_ge(S["hi_done"], ready(n))
                dve.tensor_tensor(w_lo[:, n % 2], raw[:, n % 4], w_hi[:, n % 2].bitcast(F32), ALU.subtract).then_inc(S["lo_done"], 1)

            def panels(stage, j0, cnt):
                for j in range(j0, j0 + cnt):
                    n = FIRST[stage] + j
                    if n + 2 < NPANELS:
                        lo(n + 2)

            def split(g):
                name, w = f"w{g}", GW[g]
                for i in range(4):
                    k = slice(2 * i, 2 * i + 2)
                    dve.wait_ge(S["ophi_done"], ready(part_of(name, i)))
                    dve.tensor_tensor(op_lo[slot_of(name)][:, k, 0:w], mixg(g)[:, k, 0:w],
                                      op_hi[slot_of(name)][:, k, 0:w].bitcast(F32), ALU.subtract).then_inc(S["oplo_done"], 1)

            def post(s, t):
                n, u = norms["post", s, t], turn[f"{s}{t}"]
                dve.wait_ge(S["rstd_done"], ready(n))
                dve.wait_ge(gains_full, 48)
                dve.wait_ge(x_full[t // 3], 48)
                dve.wait_ge(S["normed"], ready(n - 1))
                dve.scalar_tensor_tensor(tmp[:], pair[2][:], mstat[:, n % 4, 1:2], gain[:, GAIN[s]], ALU.mult, ALU.mult)\
                    .then_inc(S["turn_free"], 1)
                dve.wait_ge(S["turn_free"], ready(u))
                dve.tensor_tensor(xt(t), xt(t), tmp[:], ALU.add).then_inc(S["normed"], 1)

            def prea(s, t):
                n = norms["pre", s, t]
                src = xt(t)
                dve.wait_ge(S["rstd_done"], ready(n))
                dve.wait_ge(gains_full, 48)
                if s == "f":
                    dve.wait_ge(gffn_full, 16)
                    dve.wait_ge(S["sc_done"], ready(15))
                prev = [v for k, v in turn.items() if k[0] in "xf" and v < turn[f"{s}{t}"]]
                if prev:
                    dve.wait_ge(S["turn_done"], ready(max(prev)))
                x_ready(dve, n, t)
                dve.scalar_tensor_tensor(hn[:], src, mstat[:, n % 4, 1:2], gain[:, GAIN[s]], ALU.mult, ALU.mult).then_inc(S["hn_done"], 1)
                dve.wait_ge(S["hn_done"], ready(hn_write[s, t]))
                dve.sem_inc(S["normed"], 1)

            def preb(s, t):
                name, c = f"{s}{t // 3}", t % 3
                sl, cols = slot_of(name), slice(P * c, P * c + P)
                dve.wait_ge(S["ophi_done"], ready(part_of(name, c)))
                dve.tensor_tensor(op_lo[sl][:, :, cols], pair[2][:].rearrange("p (k n) -> p k n", k=KT),
                                  op_hi[sl][:, :, cols].bitcast(F32), ALU.subtract).then_inc(S["oplo_done"], 1)
                dve.wait_ge(S["oplo_done"], ready(part_of(name, c)))
                dve.sem_inc(S["turn_free"], 1)

            def mem(kind, i):
                u = turn[f"{kind}{i}"]
                dve.wait_ge(S["turn_done"], ready(u))
                dve.tensor_copy(mkT[:, :, P * i:P * i + P], pair[2][:].rearrange("p (k n) -> p k n", k=KT)).then_inc(S["memout_done"], 1)
                dve.wait_ge(S["memout_done"], ready(i))
                dve.sem_inc(S["turn_free"], 1)

            def soft(t, rows=4, shape=None):
                s = t % 2
                dve.wait_ge(S["sc_done"], ready(t if t < 8 else 7 + 4 * (t - 7)))
                dve.wait_ge(S["exp_done"], ready(t - 2))
                dve.tensor_reduce(mx[:, s, 0:rows], pair[4][:, 0:NMEM * rows].rearrange("p (h n) -> p h n", h=rows),
                                  mybir.AxisListType.X, ALU.max).then_inc(S["p_done"], 1)
                dve.wait_ge(S["p_done"], ready(3 * t))
                dve.tensor_scalar(nb[:, s, 0:rows], mx[:, s, 0:rows], -1.0 / 16, None, ALU.mult).then_inc(S["nb_done"], 1)
                dve.wait_ge(S["exp_done"], ready(t))
                dve.reciprocal(ri[:, s, 0:rows], rsum[:, s, 0:rows]).then_inc(S["p_done"], 1)
                dve.wait_ge(S["p_done"], ready(3 * t + 1))
                place = pm[:, s] if t < 8 else sp_.rearrange("p (h n) -> p h n", h=1)
                dve.tensor_tensor(place, place, bc(ri[:, s, 0:rows].rearrange("p (h u) -> p h u", u=1), [P, rows, NMEM]), ALU.mult)\
                    .then_inc(S["p_done"], 1)

            def pt(t):
                dve.wait_ge(S["pT_done"], ready(t))
                dve.wait_ge(S["pv_done"], ready(t - 2))
                dve.tensor_copy(pT[:, t % 2, 4:8], pair[6][:, 512:1024].rearrange("p (k n) -> p k n", k=4)).then_inc(S["ptd_done"], 1)

            def pv(t):
                name, c = f"o{t // 3}", t % 3
                sl, cols = slot_of(name), slice(P * c, P * c + P)
                dve.wait_ge(S["ophi_done"], ready(part_of(name, c)))
                dve.tensor_tensor(op_lo[sl][:, :, cols], pair[6][:].rearrange("p (k n) -> p k n", k=KT),
                                  op_hi[sl][:, :, cols].bitcast(F32), ALU.subtract).then_inc(S["oplo_done"], 1)

            def kt(b, q):
                if q == 1:
                    dve.wait_ge(S["natT_done"], ready(2 * b + b // 4 + 1))
                    dve.wait_ge(*k_place_free(b))
                    dve.tensor_copy(kT[b % 2][:, 4:8, :], pair[6 if b else 2][:].rearrange("p (k n) -> p k n", k=4))\
                        .then_inc(S["natd_done"], 1)

            def samples():
                for hf in range(2):
                    for b in range(4 * hf, 4 * hf + 4):
                        if b:
                            kt(b, 1)
                    soft(8 + hf, 1)
                    dve.wait_ge(S["nv_done"], ready(4 * hf + 3))
                    dve.wait_ge(S["svT_done"], ready(hf - 1))
                    dve.tensor_copy(tmp[:, 0:512], pair[6][:, 512:1024]).then_inc(S["scopyd_done"], 1)
                    dve.wait_ge(S["shi_done"], ready(hf))
                    for h in range(4):
                        out, src = picked(op_lo, hf, h)
                        ins = dve.tensor_tensor(out, src, picked(op_hi, hf, h)[0].bitcast(F32), ALU.subtract)
                    ins.then_inc(S["slo_done"], 1)
                dve.wait_ge(S["slo_done"], ready(1))
                dve.sem_inc(S["oplo_done"], 1)

            def start():
                lo(0)
                lo(1)

            walk(dict(panels=panels, post=post, prea=prea, preb=preb, split=split, sc=lambda t: None, soft=soft, pt=pt, pv=pv,
                      mem=mem, start=start, samples=samples, fill=lambda hf: None, kt=kt, ksc=lambda b: None))

        @block.tensor
        def _(pe):
            credit(pe, "pe")

            def panels(stage, j0, cnt):
                w, name = width(stage), stage
                sl = slot_of(name)
                pe.wait_ge(S["oplo_done"], ready(part_of(name, PARTS[name[0]] - 1)))
                for j in range(j0, j0 + cnt):
                    n = FIRST[stage] + j
                    pe.wait_ge(S["lo_done"], ready(n))
                    pe.wait_ge(S["evac_done"], ready(n - 2))
                    for k in range(KT):
                        for m, (a, b) in enumerate(((w_hi, op_hi), (w_hi, op_lo), (w_lo, op_hi))):
                            ins = pe.matmul(bank[n % 2][:, 0:w], a[:, n % 2, k, :], b[sl][:, k, 0:w],
                                            start=(k == 0 and m == 0), stop=(k == KT - 1 and m == 2))
                    ins.then_inc(S["panel_done"], 1)

            def turned(u, srcs, w=P):
                pe.wait_ge(S["turn_free"], ready(u - 1))
                for k, a in enumerate(srcs):
                    ins = pe.transpose(pair[2][:, P * k:P * k + P], a, ident[:])
                ins.then_inc(S["turn_done"], 1)

            def post(s, t):
                stage = f"{s}{t // 3}"
                pe.wait_ge(S["evac_done"], ready(FIRST[stage] + 7))
                c = P * (t % 3)
                turned(turn[f"{s}{t}"], [ot[OT_SLOT[stage]][:, k, c:c + P] for k in range(KT)])

            def preb(s, t):
                pe.wait_ge(S["hn_done"], ready(hn_write[s, t]))
                if s == "f":
                    pe.wait_ge(S["slo_done"], ready(1))
                turned(turn[f"{s}{t}"], [hn[:, P * k:P * k + P] for k in range(KT)])

            def mem(kind, i):
                pe.wait_ge(mem_full, 32)
                turned(turn[f"{kind}{i}"], [cache[:, i, P * k:P * k + P] for k in range(KT)])

            def sc(t):
                stage = f"x{t // 3}"
                pe.wait_ge(S["evac_done"], ready(FIRST[stage] + 7))
                pe.wait_ge(S["exp_done"], ready(t - 1))
                pe.wait_ge(S["memout_done"], ready(1))
                c = P * (t % 3)
                for h in range(4):
                    for e in range(2):
                        ins = pe.matmul(pair[4][:, NMEM * h:NMEM * h + NMEM], ot[OT_SLOT[stage]][:, 2 * h + e, c:c + P],
                                        mkT[:, 2 * h + e, :], start=(e == 0), stop=(e == 1))
                ins.then_inc(S["sc_done"], 1)

            def pt(t):
                pe.wait_ge(S["p_done"], ready(3 * t + 2))
                if t:
                    c = t - 1
                    pe.wait_ge(S["oplo_done"], ready(part_of(f"o{c // 3}", c % 3)))
                for k in range(KT):
                    ins = pe.transpose(pair[6][:, P * k:P * k + P], pm[:, t % 2, k // 2, P * (k % 2):P * (k % 2) + P], ident[:])
                ins.then_inc(S["pT_done"], 1)

            def pv(t):
                pe.wait_ge(S["pta_done"], ready(t))
                pe.wait_ge(S["ptd_done"], ready(t))
                if t == 0:
                    pe.wait_ge(mem_full, 32)
                for k in range(KT):
                    for m in range(2):
                        ins = pe.matmul(pair[6][:, P * k:P * k + P], mv[:, m, P * k:P * k + P], pT[:, t % 2, 2 * (k // 2) + m],
                                        start=(m == 0), stop=(m == 1))
                ins.then_inc(S["pv_done"], 1)

            loads_of = lambda kind, b: [m for m in range(2 * NB) if nat_item(m) == (kind, b)][0]

            def kt(b, q):
                m = loads_of("cache_mem_k", b)
                pe.wait_ge(nat_full[m % 3], 16 * (m // 3 + 1))
                pr = 6 if q and b else 2
                if b == 0:
                    pe.wait_ge(*((S["nata_done"], ready(0)) if q else (S["turn_free"], ready(turn["o5"]))))
                elif q == 0:
                    pe.wait_ge(S["nata_done"], ready(b - 1))
                    pe.wait_ge(*((S["natd_done"], ready(0)) if b == 1 else (S["slo_done"], ready(b // 4 - 1))))
                else:
                    pe.wait_ge(*((S["natd_done"], ready(b - 1)) if b > 1 else (S["oplo_done"], ready(part_of("o2", 1)))))
                for k in range(KT):
                    f = 4 * q + k // 2
                    ins = pe.transpose(pair[pr][:, P * k:P * k + P], nat(m)[:, k % 2, P * f:P * f + P], ident[:])
                ins.then_inc(S["natT_done"], 1)

            def ksc(b):
                i = b % 4
                pe.wait_ge(S["nata_done"], ready(b))
                pe.wait_ge(S["natd_done"], ready(b))
                pe.wait_ge(S["qpad_done"], ready(b // 4))
                pe.wait_ge(S["exp_done"], ready(7 + b // 4))
                for k in range(KT):
                    ins = pe.matmul(pair[4][32 * i:32 * i + 32, 0:NMEM], qpad[:, k, i, :], kT[b % 2][:, k, :],
                                    start=(k == 0), stop=(k == KT - 1))
                ins.then_inc(S["sc_done"], 1)

            def samples():
                for hf in range(2):
                    if hf:
                        kt(4, 0)
                        kt(4, 1)
                    for i in range(4):
                        b = 4 * hf + i
                        if i < 3:
                            kt(b + 1, 0)
                            kt(b + 1, 1)
                        if b:
                            ksc(b)
                    t = 8 + hf
                    pe.wait_ge(S["p_done"], ready(3 * t + 2))
                    for m in range(2):
                        ins = pe.transpose(pair[6][:, 512 + P * m:640 + P * m], sp_[:, P * m:P * m + P], ident[:])
                    ins.then_inc(S["natT_done"], 1)
                    pe.wait_ge(S["pta_done"], ready(t))
                    for i in range(4):
                        b = 4 * hf + i
                        m = loads_of("cache_mem_v", b)
                        pe.wait_ge(nat_full[m % 3], 16 * (m // 3 + 1))
                        for c in range(2):
                            for e in range(2):
                                ins = pe.matmul(pair[6][32 * i:32 * i + 32, 512 * c:512 * c + 512],
                                                spT[:, P * e + 32 * i:P * e + 32 * i + 32], nat(m)[:, e, 512 * c:512 * c + 512],
                                                start=(e == 0), stop=(e == 1))
                        ins.then_inc(S["nv_done"], 1)
                    pe.wait_ge(S["scopya_done"], ready(hf))
                    pe.wait_ge(S["scopyd_done"], ready(hf))
                    for k in range(KT):
                        src = junk if k < 4 else tmp
                        ins = pe.transpose(pair[2][:, P * k:P * k + P], src[:, P * (k % 4):P * (k % 4) + P], ident[:])
                    ins.then_inc(S["svT_done"], 1)

            walk(dict(panels=panels, post=post, prea=lambda *a: None, preb=preb, split=lambda g: None, sc=sc,
                      soft=lambda t: None, pt=pt, pv=pv, mem=mem, start=lambda: None, samples=samples,
                      fill=lambda hf: None, kt=kt, ksc=ksc))

        scope.close()


def build_ffn(nc, keep, io, xm, ot, x_hi, x_lo, ident):
    ctx = ExitStack()
    HK = FT // 2
    GUP = 2 * FT
    DOWN = 2 * KT
    UNITS = GUP + DOWN
    with ctx:
        def sb(name, shape, dt=F32):
            return ctx.enter_context(nc.sbuf_tensor("f_" + name, shape, dt))

        def sem(name):
            return keep.enter_context(nc.semaphore("f_" + name))

        raw = sb("raw", [P, 4, HK, P])
        w_hi = sb("whi", [P, 2, HK, P], F32R)
        w_lo = sb("wlo", [P, 2, HK, P], F32R)
        a_hi = sb("ahi", [P, FT, 384], F32R)
        a_lo = sb("alo", [P, FT, 384], F32R)
        sg = sb("sg", [P, 2, 384])
        hn = sb("hn", [P, D])
        gain = sb("gain", [P, 3, D])
        mhalf = sb("mhalf", [P, 1])
        st = {k: sb("st" + k, [P, 3]) for k in ("pre", "post")}
        bank = [ctx.enter_context(nc.psum_tensor(f"f_bank{n}", [P, 512], F32)) for n in range(4)]
        pair = [ctx.enter_context(nc.psum_tensor(f"f_pair{n}", [P, 1024], F32)) for n in range(2)]
        tmp = sb("tmp", [P, D])

        raw_full = [sem(f"raw_full{n}") for n in range(4)]
        gpre_full, gains_full, setup, stored = sem("gpre_full"), sem("gains_full"), sem("setup"), sem("stored")
        owners = dict(
            act="hi_done silu_done ahi_done ot_done presq_done postsq_done xhi_done",
            dve="lo_done gu_done alo_done hn_done xlo_done scaled_done x_done",
            pool="prems_done prers_done postms_done postrs_done",
            pe="unit_done preT_done postT_done")
        S = {n: sem(n) for names in owners.values() for n in names.split()}

        def credit(eng, who):
            made = "presq_done prems_done prers_done hn_done preT_done xhi_done xlo_done".split()
            for n in owners[who].split():
                eng.sem_inc(S[n], CREDIT + (3 if n in made else 0))

        xt = lambda g, i: xm[:, g, ds(D * i, D)]
        post_pair = lambda i: pair[i % 2]

        def walk(eng, f, loops=True):
            f["start"]()
            for g in range(3):
                f["gate4"](g, 0, False)
                f["post"](g - 1, 0)
                f["post"](g - 1, 1)
                f["gate4"](g, 1, False)
                f["post"](g - 1, 2)
                with eng.Fori(0, GUP // 4 - 3) as i:
                    f["gate4"](g, i + 2, False)
                f["gate4"](g, GUP // 4 - 1, True)
                if g < 2:
                    with eng.Fori(0, 3) as i:
                        f["down4"](g, i, False, lambda u: f["pre"](g + 1, i, u))
                    f["down4"](g, 3, True, lambda u: None)
                else:
                    with eng.Fori(0, 3) as i:
                        f["down4"](g, i, False, lambda u: None)
                    f["down4"](g, 3, True, lambda u: None)
            for i in range(3):
                f["post"](2, i)

        scope = ExitStack()
        block = scope.enter_context(nc.Block())

        @block.sync
        def _(sp):
            def load_gain(i, name, sem_):
                sp.dma_start(gain[:, i], io[name].rearrange("(o n) -> o n", o=1).broadcast_to([P, D])).then_inc(sem_, 16)


            def store(g):
                for i in range(3):
                    t = 3 * g + i
                    sp.wait_ge(S["x_done"], ready(t + 3))
                    sp.dma_start(io["y"](t), xt(g, i)[0:group_rows(t)]).then_inc(stored, 16)

            for g in range(3):
                for u in range(UNITS):
                    n = UNITS * g + u
                    if n == 4:
                        load_gain(0, "g_ffn_pre", gpre_full)
                        load_gain(1, "g_x_post", gains_full)
                        load_gain(2, "g_ffn_post", gains_full)
                    sp.wait_ge(S["lo_done"], ready(n - 4))
                    if u < GUP:
                        j = u // 2
                        w = io["w_up" if u % 2 else "w_gate"][:, P * j:P * j + P]
                        sp.dma_start(raw[:, n % 4, 0:KT], w.rearrange("(k p) n -> p k n", p=P)).then_inc(raw_full[n % 4], 16)
                    else:
                        j, hf = (u - GUP) // 2, (u - GUP) % 2
                        w = io["w_down"][P * HK * hf:P * HK * (hf + 1), P * j:P * j + P]
                        sp.dma_start(raw[:, n % 4], w.rearrange("(k p) n -> p k n", p=P)).then_inc(raw_full[n % 4], 16)
                    if g and u == 16:
                        store(g - 1)
            store(2)
            sp.wait_ge(stored, 16 * 9)

        @block.gpsimd
        def _(pool):
            credit(pool, "pool")
            pool.memset(mhalf[:], -0.5).then_inc(setup, 1)
            pool.wait_ge(setup, 1)

            def stat(kind, t):
                a = st[kind]
                pool.wait_ge(S[kind + "sq_done"], ready(t))
                pool.wait_ge(S[kind + "rs_done"], ready(t - 1))
                pool.tensor_scalar(a[:, 1:2], a[:, 0:1], 1.0 / D, EPS, ALU.mult, ALU.add).then_inc(S[kind + "ms_done"], 1)
                pool.wait_ge(S[kind + "ms_done"], ready(t))
                pool.wait_ge(S["hn_done" if kind == "pre" else "scaled_done"], ready(t - 1))
                pool.tensor_tensor(a[:, 2:3], a[:, 1:2], mhalf[:], ALU.pow).then_inc(S[kind + "rs_done"], 1)

            for g in range(3):
                for i in range(3):
                    stat("post", 3 * g + i)
                if g < 2:
                    for i in range(3):
                        stat("pre", 3 * (g + 1) + i)
            for i in range(3):
                stat("post", 9 + i)

        @block.scalar
        def _(act):
            credit(act, "act")

            def hi(n, s, it, kt):
                act.wait_ge(raw_full[s], 16 * it + 16)
                act.wait_ge(S["unit_done"], ready(n - 2))
                act.activation(w_hi[:, s % 2, 0:kt], raw[:, s, 0:kt], ACT.Copy).then_inc(S["hi_done"], 1)

            def ahead(g, it, last, s, kt, next_kt):
                n0 = UNITS * g + it * 4
                q = UNITS // 4 * g + it
                if last and s >= 2 and g == 2 and kt == HK:
                    return
                if s < 2:
                    hi(n0 + s + 2, s + 2, q, kt)
                else:
                    hi(n0 + s + 2, s - 2, q + 1, next_kt if last else kt)

            def gate4(g, it, last):
                w = GW[g]
                for s in range(4):
                    n = UNITS * g + it * 4 + s
                    j = it * 2 + s // 2
                    q = FT * g + j
                    if s % 2 == 0:
                        act.wait_ge(S["unit_done"], ready(n))
                        act.wait_ge(S["alo_done"], ready(q - 2))
                        act.activation(sg[:, s // 2, 0:w], bank[0][:, 0:w], ACT.Silu).then_inc(S["silu_done"], 1)
                    ahead(g, it, last, s, KT, HK)
                    if s % 2:
                        act.wait_ge(S["gu_done"], ready(q))
                        act.activation(a_hi[:, ds(j, 1), 0:w], sg[:, s // 2:s // 2 + 1, 0:w], ACT.Copy).then_inc(S["ahi_done"], 1)

            def down4(g, it, last, pre):
                w = GW[g]
                for s in range(4):
                    n = UNITS * g + GUP + it * 4 + s
                    if s % 2:
                        act.wait_ge(S["unit_done"], ready(n))
                        act.activation(ot[:, ds(it * 2 + s // 2, 1), 0:w],
                                       bank[2 + s // 2][:, 0:w].rearrange("p (o n) -> p o n", o=1), ACT.Copy).then_inc(S["ot_done"], 1)
                    ahead(g, it + GUP // 4, last, s, HK, KT)
                    pre(s)

            def pre(g, i, where):
                t = 3 * g + i
                if where == 0:
                    if g == 2:
                        act.wait_ge(S["x_done"], ready(2))
                    act.wait_ge(S["prems_done"], ready(t - 1))
                    if g:
                        act.wait_ge(S["x_done"], ready(3 * g - 1))
                    act.wait_ge(S["presq_done"], ready(t - 1))
                    act.activation(tmp[:], xt(g, i), ACT.Square, accum_out=st["pre"][:, 0:1]).then_inc(S["presq_done"], 1)
                if where == 1:
                    act.wait_ge(S["preT_done"], ready(t))
                    act.wait_ge(S["unit_done"], ready(UNITS * (g - 1) + GUP - 1) if g else CREDIT)
                    act.activation(x_hi[:, :, ds(P * i, P)], pair[1][:].rearrange("p (k n) -> p k n", k=KT), ACT.Copy)\
                        .then_inc(S["xhi_done"], 1)

            def post(g, i):
                t = 3 * (g + 1) + i
                act.wait_ge(S["postT_done"], ready(t))
                act.wait_ge(S["postms_done"], ready(t - 1))
                act.wait_ge(S["presq_done"], ready(3 * min(g + 1, 2) + 2))
                act.wait_ge(S["x_done"], ready(t - 1))
                act.activation(tmp[:], post_pair(i)[:], ACT.Square, accum_out=st["post"][:, 0:1]).then_inc(S["postsq_done"], 1)

            def start():
                hi(0, 0, 0, KT)
                hi(1, 1, 0, KT)

            walk(act, dict(gate4=gate4, down4=down4, pre=pre, post=post, start=start))

        @block.vector
        def _(dve):
            credit(dve, "dve")

            def lo(n, s, kt):
                dve.wait_ge(S["hi_done"], ready(n))
                dve.tensor_tensor(w_lo[:, s % 2, 0:kt], raw[:, s, 0:kt], w_hi[:, s % 2, 0:kt].bitcast(F32), ALU.subtract)\
                    .then_inc(S["lo_done"], 1)

            def ahead(g, it, last, s, kt, next_kt):
                if last and s >= 2 and g == 2 and kt == HK:
                    return
                lo(UNITS * g + it * 4 + s + 2, (s + 2) % 4, next_kt if last and s >= 2 else kt)

            def gate4(g, it, last):
                w = GW[g]
                for s in range(4):
                    n = UNITS * g + it * 4 + s
                    j = it * 2 + s // 2
                    q = FT * g + j
                    h = slice(s // 2, s // 2 + 1)
                    if s % 2:
                        dve.wait_ge(S["silu_done"], ready(q))
                        dve.wait_ge(S["unit_done"], ready(n))
                        dve.tensor_tensor(sg[:, s // 2, 0:w], sg[:, s // 2, 0:w], bank[1][:, 0:w], ALU.mult).then_inc(S["gu_done"], 1)
                    ahead(g, it, last, s, KT, HK)
                    if s % 2:
                        dve.wait_ge(S["ahi_done"], ready(q))
                        dve.tensor_tensor(a_lo[:, ds(j, 1), 0:w], sg[:, h, 0:w], a_hi[:, ds(j, 1), 0:w].bitcast(F32),
                                          ALU.subtract).then_inc(S["alo_done"], 1)

            def down4(g, it, last, pre):
                for s in range(4):
                    ahead(g, it + GUP // 4, last, s, HK, KT)
                    pre(s)

            def pre(g, i, where):
                t = 3 * g + i
                if where == 0:
                    if g == 2:
                        dve.wait_ge(S["x_done"], ready(2))
                    dve.wait_ge(gpre_full, 16)
                    dve.wait_ge(S["prers_done"], ready(t))
                    dve.wait_ge(S["preT_done"], ready(t - 1))
                    dve.scalar_tensor_tensor(hn[:], xt(g, i), st["pre"][:, 2:3], gain[:, 0], ALU.mult, ALU.mult)\
                        .then_inc(S["hn_done"], 1)
                if where == 1:
                    dve.wait_ge(S["xhi_done"], ready(t))
                    cols = ds(P * i, P)
                    dve.tensor_tensor(x_lo[:, :, cols], pair[1][:].rearrange("p (k n) -> p k n", k=KT),
                                      x_hi[:, :, cols].bitcast(F32), ALU.subtract).then_inc(S["xlo_done"], 1)

            def post(g, i):
                t = 3 * (g + 1) + i
                dve.wait_ge(gains_full, 32)
                dve.wait_ge(S["postrs_done"], ready(t))
                dve.scalar_tensor_tensor(tmp[:], post_pair(i)[:], st["post"][:, 2:3], gain[:, 1 if g < 0 else 2], ALU.mult, ALU.mult)\
                    .then_inc(S["scaled_done"], 1)
                dve.wait_ge(S["scaled_done"], ready(t))
                dve.tensor_tensor(xt(g % 3, i), xt(g % 3, i), tmp[:], ALU.add).then_inc(S["x_done"], 1)

            def start():
                lo(0, 0, KT)
                lo(1, 1, KT)

            walk(dve, dict(gate4=gate4, down4=down4, pre=pre, post=post, start=start))

        @block.tensor
        def _(pe):
            credit(pe, "pe")

            def unit(n, s, out, a_h, a_l, k0, kt, first, last, w):
                pe.wait_ge(S["lo_done"], ready(n))
                for k in range(kt):
                    for m, (a, b) in enumerate(((w_hi, a_h), (w_hi, a_l), (w_lo, a_h))):
                        ins = pe.matmul(out, a[:, s % 2, k, :], b[:, k0 + k, 0:w], start=(first and k == 0 and m == 0),
                                        stop=(last and k == kt - 1 and m == 2))
                ins.then_inc(S["unit_done"], 1)

            def gate4(g, it, last):
                w = GW[g]
                pe.wait_ge(S["xlo_done"], ready(3 * g + 2))
                for s in range(4):
                    q = FT * g + it * 2 + s // 2
                    pe.wait_ge(S["gu_done" if s % 2 else "silu_done"], ready(q - 1))
                    unit(UNITS * g + it * 4 + s, s, bank[s % 2][:, 0:w], x_hi, x_lo, 0, KT, True, True, w)

            def down4(g, it, last, pre):
                w = GW[g]
                for s in range(4):
                    pe.wait_ge(S["alo_done"], ready(FT * g + HK * (s % 2 + 1) - 1))
                    if s % 2 == 0:
                        pe.wait_ge(S["ot_done"], ready(KT * g + it * 2 + s // 2 - 2))
                    unit(UNITS * g + GUP + it * 4 + s, s, bank[2 + s // 2][:, 0:w], a_hi, a_lo, HK * (s % 2), HK,
                         s % 2 == 0, s % 2 == 1, w)
                    pre(s)

            def pre(g, i, where):
                t = 3 * g + i
                if where == 1:
                    pe.wait_ge(S["hn_done"], ready(t))
                    pe.wait_ge(S["xlo_done"], ready(t - 1))
                    if g:
                        pe.wait_ge(S["scaled_done"], ready(3 * g - 1))
                    for k in range(KT):
                        ins = pe.transpose(pair[1][:, P * k:P * k + P], hn[:, P * k:P * k + P], ident[:])
                    ins.then_inc(S["preT_done"], 1)

            def post(g, i):
                t = 3 * (g + 1) + i
                if g >= 0:
                    pe.wait_ge(S["ot_done"], ready(KT * g + KT - 1))
                pe.wait_ge(S["xlo_done"], ready(3 * min(g + 1, 2) + 2))
                pe.wait_ge(S["scaled_done"], ready(t - 2))
                for k in range(KT):
                    ins = pe.transpose(post_pair(i)[:, P * k:P * k + P], ot[:, k, P * i:P * i + P], ident[:])
                ins.then_inc(S["postT_done"], 1)

            walk(pe, dict(gate4=gate4, down4=down4, pre=pre, post=post, start=lambda: None))

        scope.close()


def hymba_step(nc, io):
    with ExitStack() as keep:
        xm = keep.enter_context(nc.sbuf_tensor("xm", [P, 3, 3 * D], F32))
        ident = keep.enter_context(nc.sbuf_tensor("ident", [P, P], F32))
        spent = []
        build_mixers(nc, spent, io, lambda g: xm[:, g, :].rearrange("p (k n) -> p k n", n=384), xm, ident)
        ot_last = keep.enter_context(nc.sbuf_tensor("ot_last", [P, KT, 384], F32))
        next_hi = keep.enter_context(nc.sbuf_tensor("next_hi", [P, KT, 384], F32R))
        next_lo = keep.enter_context(nc.sbuf_tensor("next_lo", [P, KT, 384], F32R))
        build_cross(nc, keep, io, xm, ot_last, next_hi, next_lo, ident, spent)
        build_ffn(nc, keep, io, xm, ot_last, next_hi, next_lo, ident)


_INS = ["x_prompt", "x_sample", "state_ssm", "state_conv", "cache_win_k", "cache_win_v", "cache_mem_k", "cache_mem_v",
        "mem_prompt", "g_mix_pre", "w_in", "conv_w", "conv_b", "dt_bias", "a_log", "d_skip", "g_ssd_norm", "sinks", "w_out",
        "g_mix_post", "g_x_pre", "w_xq", "g_mem", "w_xk", "w_xv", "w_xo", "g_x_post", "g_ffn_pre", "w_gate", "w_up", "w_down",
        "g_ffn_post"]
_STATES = 9
_OUTS = dict(y_prompt=(1, SEQ, D), y_sample=(NB, TS, D), p_ssm=(1, 1, HEADS, HD, NST), p_conv=(1, 1, 3, XBC),
             p_win_k=(1, 1, P, 2, HD), p_win_v=(1, 1, P, 2, HD), p_mem_k=(1, 1, NMEM, 4, 256), p_mem_v=(1, 1, NMEM, 4, 256),
             s_ssm=(1, NB, HEADS, HD, NST), s_conv=(1, NB, 3, XBC), s_win_k=(1, NB, P, 2, HD), s_win_v=(1, NB, P, 2, HD))


def _io(nc, arrays):
    io = {}
    for i, name in enumerate(_INS):
        ap = nc.dram_tensor(name, arrays[name].shape, F32, kind="ExternalInput").ap()
        io[name] = ap if i < _STATES else ap[0]
    for name, shape in _OUTS.items():
        io[name] = nc.dram_tensor(name, shape, F32, kind="ExternalOutput").ap()
    rows = lambda full, tile: lambda t: full[0, P * t:P * t + P, :] if t < NCH else tile.rearrange("b t d -> (b t) d")
    io["x"] = rows(io["x_prompt"], io["x_sample"])
    io["y"] = rows(io["y_prompt"], io["y_sample"])
    return io


def kernel(**inputs):
    import numpy as np
    import concourse.bacc as bacc
    from concourse.bass_utils import run_bass_kernel_spmd

    arrays = {name: np.ascontiguousarray(inputs[name]) for name in _INS}
    nc = bacc.Bacc("TRN2", target_bir_lowering=False, num_devices=1)
    hymba_step(nc, _io(nc, arrays))
    nc.finalize()
    r = run_bass_kernel_spmd(nc, [arrays], core_ids=[0])
    return tuple(r.results[0][name] for name in _OUTS)
```
